# Optimizing a Trainium2 kernel written in Bass

```python
import jax, jax.numpy as jnp
from jax import lax
import numpy as np
import math

D_MODEL = 1024
BATCH = 1
SEQ = 1024
DEPTH = 1

GRID_W = 64
CTX_LEN = 256
D_FOURIER = 256
FOURIER_GROUPS = 4
D_CONV = 256
CONV_WIDTH = 31
N_NA_HEADS = 8
NA_HEAD_DIM = 64
D_NA = N_NA_HEADS * NA_HEAD_DIM
WIN_ROWS = 8
WIN_COLS = 16
QKV_START = D_FOURIER + 2 * D_CONV
KV_START = QKV_START + D_NA
D_IN = QKV_START + 3 * D_NA
D_MIX = D_FOURIER + D_CONV + D_NA
D_FF = 4 * D_MODEL
N_MOD = 6
RMS_EPS = 1e-6
LN_EPS = 1e-5


def rms_norm(x, g):
    xf = x.astype(jnp.float32)
    y = xf * lax.rsqrt(jnp.mean(xf * xf, axis=-1, keepdims=True) + RMS_EPS)
    return (y * g.astype(jnp.float32)).astype(x.dtype)

def layer_norm(x, g, b):
    xf = x.astype(jnp.float32)
    mu = jnp.mean(xf, axis=-1, keepdims=True)
    var = jnp.mean(jnp.square(xf - mu), axis=-1, keepdims=True)
    y = (xf - mu) * lax.rsqrt(var + LN_EPS)
    return (y * g.astype(jnp.float32) + b.astype(jnp.float32)).astype(x.dtype)

def modulate(x, shift, scale):
    return x * (1 + scale) + shift

def split_heads(u):
    b, l, _ = u.shape
    qkv = u[..., QKV_START:].reshape(b, l, 3, N_NA_HEADS, NA_HEAD_DIM)
    return u[..., :D_FOURIER], u[..., D_FOURIER:QKV_START], qkv[:, :, 0], qkv[:, :, 1], qkv[:, :, 2]

def fourier_mix(u, w):
    b, l, _ = u.shape
    ug = u.reshape(b, l, FOURIER_GROUPS, D_FOURIER // FOURIER_GROUPS).astype(jnp.float32)
    f = jnp.fft.fftn(ug, axes=(1, 3), norm="ortho").real
    return f.reshape(b, l, D_FOURIER).astype(u.dtype) @ w

def conv_module(u, dw_w, dw_b, ln_g, ln_b, pw_w, pw_b):
    a, gt = jnp.split(u, 2, axis=-1)
    v = a * jax.nn.sigmoid(gt)
    pad = CONV_WIDTH // 2
    v = lax.conv_general_dilated(v, dw_w[:, None, :].astype(v.dtype), window_strides=(1,), padding=[(pad, pad)],
                                 dimension_numbers=("NWC", "WIO", "NWC"), feature_group_count=D_CONV) + dw_b
    v = jax.nn.silu(layer_norm(v, ln_g, ln_b))
    return v @ pw_w + pw_b

def context_attention(q, k, v):
    s = jnp.einsum("bqhd,bkhd->bhqk", q, k).astype(jnp.float32) * (NA_HEAD_DIM ** -0.5)
    p = jax.nn.softmax(s, axis=-1).astype(v.dtype)
    o = jnp.einsum("bhqk,bkhd->bqhd", p, v)
    return o.reshape(q.shape[0], q.shape[1], D_NA)

def neighbourhood_attention(q, k, v, k_ctx, v_ctx, rpb):
    b, l, h, dh = q.shape
    rows = l // GRID_W
    kr = min(WIN_ROWS, rows)
    r = np.arange(rows)
    row_start = np.clip(r - kr // 2, 0, rows - kr)
    key_rows = row_start[:, None] + np.arange(kr)[None, :]
    col = np.arange(GRID_W)
    col_start = np.clip(col - WIN_COLS // 2, 0, GRID_W - WIN_COLS)
    col_valid = (col[None, :] >= col_start[:, None]) & (col[None, :] < col_start[:, None] + WIN_COLS)
    row_off = key_rows - r[:, None] + (WIN_ROWS - 1)
    col_off = np.clip(col[None, :] - col[:, None] + (WIN_COLS - 1), 0, 2 * WIN_COLS - 2)
    bias = rpb[:, row_off[:, :, None, None], col_off[None, None]].astype(jnp.float32)
    bias = jnp.where(jnp.asarray(col_valid)[None, None, None], bias, -jnp.inf)
    bias = bias.transpose(0, 1, 3, 2, 4).reshape(h, rows, GRID_W, kr * GRID_W)
    qg = q.reshape(b, rows, GRID_W, h, dh)
    kg = k.reshape(b, rows, GRID_W, h, dh)[:, key_rows].reshape(b, rows, kr * GRID_W, h, dh)
    vg = v.reshape(b, rows, GRID_W, h, dh)[:, key_rows].reshape(b, rows, kr * GRID_W, h, dh)
    scale = NA_HEAD_DIM ** -0.5
    s_loc = jnp.einsum("brqhd,brkhd->bhrqk", qg, kg).astype(jnp.float32) * scale + bias[None]
    s_ctx = jnp.einsum("brqhd,bchd->bhrqc", qg, k_ctx).astype(jnp.float32) * scale
    p = jax.nn.softmax(jnp.concatenate([s_loc, s_ctx], axis=-1), axis=-1).astype(v.dtype)
    n_loc = kr * GRID_W
    o = (jnp.einsum("bhrqk,brkhd->brqhd", p[..., :n_loc], vg)
         + jnp.einsum("bhrqc,bchd->brqhd", p[..., n_loc:], v_ctx))
    return o.reshape(b, l, D_NA)

def first_inputs(seed: int = 0) -> dict:
    key = jax.random.key(seed)
    ks = jax.random.split(key, 24)

    def nrm(k, shape, scale):
        return jax.random.normal(k, shape, jnp.float32) * scale

    return {
        "x": nrm(ks[0], (BATCH, SEQ, D_MODEL), 1.0),
        "c": nrm(ks[1], (BATCH, D_MODEL), 1.0),
        "ctx": nrm(ks[2], (BATCH, CTX_LEN, D_MODEL), 1.0),
        "c_ctx": nrm(ks[3], (D_MODEL,), 1.0),
        "ada_w": nrm(ks[4], (DEPTH, D_MODEL, N_MOD * D_MODEL), D_MODEL ** -0.5),
        "ada_b": nrm(ks[5], (DEPTH, N_MOD * D_MODEL), 0.02),
        "norm1_g": 1.0 + nrm(ks[6], (DEPTH, D_MODEL), 0.05),
        "norm2_g": 1.0 + nrm(ks[7], (DEPTH, D_MODEL), 0.05),
        "w_in": nrm(ks[8], (DEPTH, D_MODEL, D_IN), D_MODEL ** -0.5),
        "w_fourier": nrm(ks[9], (DEPTH, D_FOURIER, D_FOURIER), D_FOURIER ** -0.5),
        "conv_dw_w": nrm(ks[10], (DEPTH, CONV_WIDTH, D_CONV), CONV_WIDTH ** -0.5),
        "conv_dw_b": nrm(ks[11], (DEPTH, D_CONV), 0.02),
        "conv_norm_g": 1.0 + nrm(ks[12], (DEPTH, D_CONV), 0.05),
        "conv_norm_b": nrm(ks[13], (DEPTH, D_CONV), 0.02),
        "conv_pw_w": nrm(ks[14], (DEPTH, D_CONV, D_CONV), D_CONV ** -0.5),
        "conv_pw_b": nrm(ks[15], (DEPTH, D_CONV), 0.02),
        "na_rpb": nrm(ks[16], (DEPTH, N_NA_HEADS, 2 * WIN_ROWS - 1, 2 * WIN_COLS - 1), 0.1),
        "w_out": nrm(ks[17], (DEPTH, D_MIX, D_MODEL), D_MIX ** -0.5),
        "mlp_w1": nrm(ks[18], (DEPTH, D_MODEL, D_FF), D_MODEL ** -0.5),
        "mlp_w2": nrm(ks[19], (DEPTH, D_FF, D_MODEL), D_FF ** -0.5),
        "final_norm_g": 1.0 + nrm(ks[20], (D_MODEL,), 0.05),
    }

def first_block(x, c, ctx, c_ctx, ada_w, ada_b, norm1_g, norm2_g, w_in, w_fourier, conv_dw_w, conv_dw_b,
              conv_norm_g, conv_norm_b, conv_pw_w, conv_pw_b, na_rpb, w_out, mlp_w1, mlp_w2, final_norm_g):
    h_lat, h_ctx = x, ctx
    b = x.shape[0]
    n_ctx = ctx.shape[1]
    for i in range(DEPTH):
        last = i == DEPTH - 1
        conv_p = (conv_dw_w[i], conv_dw_b[i], conv_norm_g[i], conv_norm_b[i], conv_pw_w[i], conv_pw_b[i])
        mod = (jax.nn.silu(c) @ ada_w[i] + ada_b[i])[:, None, :]
        sh1, sc1, g1, sh2, sc2, g2 = jnp.split(mod, N_MOD, axis=-1)
        n_ctx_mod = (2 if last else N_MOD) * D_MODEL
        mod_c = (jax.nn.silu(c_ctx) @ ada_w[i][:, :n_ctx_mod] + ada_b[i][:n_ctx_mod])[None, None, :]
        mods_c = jnp.split(mod_c, n_ctx_mod // D_MODEL, axis=-1)

        hn_ctx = modulate(rms_norm(h_ctx, norm1_g[i]), mods_c[0], mods_c[1])
        if last:
            kv = (hn_ctx @ w_in[i][:, KV_START:]).reshape(b, n_ctx, 2, N_NA_HEADS, NA_HEAD_DIM)
            k_ctx, v_ctx = kv[:, :, 0], kv[:, :, 1]
        else:
            uf_c, uc_c, q_ctx, k_ctx, v_ctx = split_heads(hn_ctx @ w_in[i])
            mix_ctx = jnp.concatenate([fourier_mix(uf_c, w_fourier[i]), conv_module(uc_c, *conv_p),
                                       context_attention(q_ctx, k_ctx, v_ctx)], axis=-1)

        hn_lat = modulate(rms_norm(h_lat, norm1_g[i]), sh1, sc1)
        uf, uc, q, k, v = split_heads(hn_lat @ w_in[i])
        mix_lat = jnp.concatenate([fourier_mix(uf, w_fourier[i]), conv_module(uc, *conv_p),
                                   neighbourhood_attention(q, k, v, k_ctx, v_ctx, na_rpb[i])], axis=-1)
        h_lat = h_lat + g1 * (mix_lat @ w_out[i])

        hn = modulate(rms_norm(h_lat, norm2_g[i]), sh2, sc2)
        h_lat = h_lat + g2 * (jnp.square(jax.nn.relu(hn @ mlp_w1[i])) @ mlp_w2[i])

        if not last:
            h_ctx = h_ctx + mods_c[2] * (mix_ctx @ w_out[i])
            hn_c2 = modulate(rms_norm(h_ctx, norm2_g[i]), mods_c[3], mods_c[4])
            h_ctx = h_ctx + mods_c[5] * (jnp.square(jax.nn.relu(hn_c2 @ mlp_w1[i])) @ mlp_w2[i])
    return rms_norm(h_lat, final_norm_g)


HEAD_DIM = 64
POOL_WIDTH = D_MODEL // 4
POOL_WINDOWS = (2, 4, 8, 16)
POOL_GROUPS = len(POOL_WINDOWS)
POOL_GROUP_DIM = POOL_WIDTH // POOL_GROUPS
ATTN_WIDTH = D_MODEL - POOL_WIDTH
ATTN_HEADS = ATTN_WIDTH // HEAD_DIM
DILATION_CFG = ((128, 1), (512, 4), (2048, 16))
N_DIL = len(DILATION_CFG)
HEADS_PER_DIL = ATTN_HEADS // N_DIL
ATTN_OUT_WIDTH = HEADS_PER_DIL * HEAD_DIM
IN_PROJ_WIDTH = POOL_WIDTH + 3 * ATTN_WIDTH
OUT_PROJ_WIDTH = POOL_WIDTH + ATTN_OUT_WIDTH
ROT_DIM = HEAD_DIM // 4
ROPE_THETA = 500000.0
D_FF_2 = 11 * D_MODEL // 4
CONV_WIDTH_2 = 3
BLOCK = 128
NORM_EPS = 1e-6


def rms_norm_2(x, g):
    x32 = x.astype(jnp.float32)
    y = x32 * lax.rsqrt(jnp.mean(x32 * x32, axis=-1, keepdims=True) + NORM_EPS)
    return (y * g.astype(jnp.float32)).astype(x.dtype)

def partial_rope(t, cos, sin):
    half = ROT_DIM // 2
    t1 = t[..., :half]
    t2 = t[..., half:ROT_DIM]
    return jnp.concatenate(
        [t1 * cos - t2 * sin, t2 * cos + t1 * sin, t[..., ROT_DIM:]], axis=-1)

def causal_multiscale_pool(u, w_pool, b_pool, pool_scale):
    B, S, _ = u.shape
    u32 = u.astype(jnp.float32).reshape(B, S, POOL_GROUPS, POOL_GROUP_DIM)
    cs = jnp.cumsum(u32, axis=1)
    t = jnp.arange(S, dtype=jnp.float32)
    means = []
    for gi, w in enumerate(POOL_WINDOWS):
        csg = cs[:, :, gi]
        lagged = jnp.pad(csg[:, :S - w], ((0, 0), (w, 0), (0, 0)))
        count = jnp.minimum(t + 1.0, float(w))
        means.append((csg - lagged) / count[None, :, None])
    mixed = jnp.stack(means, axis=2) - u32
    y = jnp.einsum('bsgc,gcd->bsgd', mixed, w_pool.astype(jnp.float32)) + b_pool.astype(jnp.float32)
    return (y.reshape(B, S, POOL_WIDTH) * pool_scale.astype(jnp.float32)).astype(u.dtype)

def dilated_window_attention(q, k, v, window, dilation):
    B, S, H, hd = q.shape
    span = window // dilation
    assert span <= BLOCK
    chunk = dilation * BLOCK
    s_pad = -(-S // chunk) * chunk
    padw = ((0, 0), (0, s_pad - S), (0, 0), (0, 0))
    q, k, v = (jnp.pad(a.astype(jnp.float32), padw) for a in (q, k, v))
    nb = s_pad // chunk
    qb, kb, vb = (a.reshape(B, nb, BLOCK, dilation, H, hd) for a in (q, k, v))

    def with_prev(a):
        prev = jnp.pad(a[:, :-1], ((0, 0), (1, 0), (0, 0), (0, 0), (0, 0), (0, 0)))
        return jnp.concatenate([prev, a], axis=2)

    kk, vv = with_prev(kb), with_prev(vb)
    scores = jnp.einsum('bnirhd,bnjrhd->bnrhij', qb, kk)
    i = jnp.arange(BLOCK)[:, None]
    j = jnp.arange(2 * BLOCK)[None, :]
    n = jnp.arange(nb)[:, None, None]
    dist = BLOCK + i - j
    valid = (dist >= 0) & (dist <= span) & (n * BLOCK + j - BLOCK >= 0)
    scores = jnp.where(valid[None, :, None, None], scores, -jnp.inf)
    m = jnp.max(scores, axis=-1, keepdims=True)
    p = jnp.exp(scores - m)
    den = jnp.sum(p, axis=-1)
    o = jnp.einsum('bnrhij,bnjrhd->bnirhd', p, vv)
    den_t = jnp.moveaxis(den, -1, 2)
    lse_t = jnp.moveaxis(m[..., 0] + jnp.log(den), -1, 2)
    o = (o / den_t[..., None]).reshape(B, s_pad, H, hd)[:, :S]
    lse = lse_t.reshape(B, s_pad, H)[:, :S]
    return o, lse

def mixing_sublayer(h, cos, sin, w_in, w_pool, b_pool, pool_scale, w_out):
    B, S, _ = h.shape
    proj = h @ w_in
    u_pool = proj[..., :POOL_WIDTH]
    qkv = proj[..., POOL_WIDTH:].reshape(B, S, 3, ATTN_HEADS, HEAD_DIM)
    q = partial_rope(qkv[:, :, 0], cos, sin) * (HEAD_DIM ** -0.5)
    k = partial_rope(qkv[:, :, 1], cos, sin)
    v = qkv[:, :, 2]
    outs, lses = [], []
    for g, (window, dilation) in enumerate(DILATION_CFG):
        sl = slice(g * HEADS_PER_DIL, (g + 1) * HEADS_PER_DIL)
        o, l = dilated_window_attention(q[:, :, sl], k[:, :, sl], v[:, :, sl], window, dilation)
        outs.append(o)
        lses.append(l)
    alpha = jax.nn.softmax(jnp.stack(lses, axis=0), axis=0)
    attn = jnp.sum(alpha[..., None] * jnp.stack(outs, axis=0), axis=0)
    attn = attn.reshape(B, S, ATTN_OUT_WIDTH).astype(h.dtype)
    pool = causal_multiscale_pool(u_pool, w_pool, b_pool, pool_scale)
    return jnp.concatenate([pool, attn], axis=-1) @ w_out

def conv_ffn(h, w_up, conv_w, conv_b, w_down):
    S = h.shape[1]
    up = h @ w_up
    gate, val = up[..., :D_FF_2], up[..., D_FF_2:]
    gp = jnp.pad(gate, ((0, 0), (CONV_WIDTH_2 - 1, 0), (0, 0)))
    gate = gp[:, 0:S] * conv_w[0] + gp[:, 1:S + 1] * conv_w[1] + gp[:, 2:S + 2] * conv_w[2] + conv_b
    return (jax.nn.gelu(gate, approximate=True) * val) @ w_down

def second_inputs(seed: int = 0) -> dict:
    key = jax.random.key(seed)
    ks = jax.random.split(key, 20)
    f32 = jnp.float32
    nrm = lambda k, shape, s: jax.random.normal(k, shape, f32) * s
    L = DEPTH
    return {
        "x": nrm(ks[0], (BATCH, SEQ, D_MODEL), 1.0),
        "c": nrm(ks[1], (BATCH, D_MODEL), 1.0),
        "positions": jnp.broadcast_to(jnp.arange(SEQ, dtype=jnp.int32), (BATCH, SEQ)),
        "w_ada": nrm(ks[2], (L, D_MODEL, N_MOD * D_MODEL), D_MODEL ** -0.5),
        "b_ada": nrm(ks[3], (L, N_MOD * D_MODEL), 0.02),
        "g_pre_mix": 1.0 + nrm(ks[4], (L, D_MODEL), 0.05),
        "g_post_mix": 1.0 + nrm(ks[5], (L, D_MODEL), 0.05),
        "g_pre_ffn": 1.0 + nrm(ks[6], (L, D_MODEL), 0.05),
        "g_post_ffn": 1.0 + nrm(ks[7], (L, D_MODEL), 0.05),
        "w_in": nrm(ks[8], (L, D_MODEL, IN_PROJ_WIDTH), D_MODEL ** -0.5),
        "w_pool": nrm(ks[9], (L, POOL_GROUPS, POOL_GROUP_DIM, POOL_GROUP_DIM), POOL_GROUP_DIM ** -0.5),
        "b_pool": nrm(ks[10], (L, POOL_GROUPS, POOL_GROUP_DIM), 0.02),
        "pool_scale": 1.0 + nrm(ks[11], (L, POOL_WIDTH), 0.05),
        "w_out": nrm(ks[12], (L, OUT_PROJ_WIDTH, D_MODEL), OUT_PROJ_WIDTH ** -0.5),
        "w_up": nrm(ks[13], (L, D_MODEL, 2 * D_FF_2), D_MODEL ** -0.5),
        "conv_w": nrm(ks[14], (L, CONV_WIDTH_2, D_FF_2), CONV_WIDTH_2 ** -0.5),
        "conv_b": nrm(ks[15], (L, D_FF_2), 0.02),
        "w_down": nrm(ks[16], (L, D_FF_2, D_MODEL), D_FF_2 ** -0.5),
    }

def second_block(x, c, positions, w_ada, b_ada, g_pre_mix, g_post_mix, g_pre_ffn, g_post_ffn,
              w_in, w_pool, b_pool, pool_scale, w_out, w_up, conv_w, conv_b, w_down):
    inv_freq = ROPE_THETA ** (-jnp.arange(0, ROT_DIM, 2, dtype=jnp.float32) / ROT_DIM)
    ang = positions.astype(jnp.float32)[..., None] * inv_freq
    cos = jnp.cos(ang)[:, :, None, :].astype(x.dtype)
    sin = jnp.sin(ang)[:, :, None, :].astype(x.dtype)
    c_act = jax.nn.silu(c)
    for l in range(DEPTH):
        mod = c_act @ w_ada[l] + b_ada[l]
        sh_m, sc_m, gt_m, sh_f, sc_f, gt_f = (t[:, None, :] for t in jnp.split(mod, N_MOD, axis=-1))
        h = rms_norm_2(x, g_pre_mix[l]) * (1.0 + sc_m) + sh_m
        y = mixing_sublayer(h, cos, sin, w_in[l], w_pool[l], b_pool[l], pool_scale[l], w_out[l])
        x = x + gt_m * rms_norm_2(y, g_post_mix[l])
        h = rms_norm_2(x, g_pre_ffn[l]) * (1.0 + sc_f) + sh_f
        y = conv_ffn(h, w_up[l], conv_w[l], conv_b[l], w_down[l])
        x = x + gt_f * rms_norm_2(y, g_post_ffn[l])
    return x


def setup_inputs(seed=0):
    out = dict(first_inputs(seed))
    for name, value in second_inputs(seed + 1).items():
        if name != "x":
            out[name + "_2"] = value
    return out


def reference(
    x, c, ctx, c_ctx, ada_w, ada_b, norm1_g, norm2_g, w_in, w_fourier, conv_dw_w, conv_dw_b,
    conv_norm_g, conv_norm_b, conv_pw_w, conv_pw_b, na_rpb, w_out, mlp_w1, mlp_w2, final_norm_g,
    c_2, positions_2, w_ada_2, b_ada_2, g_pre_mix_2, g_post_mix_2, g_pre_ffn_2, g_post_ffn_2,
    w_in_2, w_pool_2, b_pool_2, pool_scale_2, w_out_2, w_up_2, conv_w_2, conv_b_2, w_down_2,
):
    x = first_block(
        x, c, ctx, c_ctx, ada_w, ada_b, norm1_g, norm2_g, w_in, w_fourier, conv_dw_w, conv_dw_b,
        conv_norm_g, conv_norm_b, conv_pw_w, conv_pw_b, na_rpb, w_out, mlp_w1, mlp_w2,
        final_norm_g,
    )
    return second_block(
        x, c_2, positions_2, w_ada_2, b_ada_2, g_pre_mix_2, g_post_mix_2, g_pre_ffn_2,
        g_post_ffn_2, w_in_2, w_pool_2, b_pool_2, pool_scale_2, w_out_2, w_up_2, conv_w_2,
        conv_b_2, w_down_2,
    )


_drawn_inputs = setup_inputs


def setup_inputs(seed=0):
    import zlib

    import numpy as np

    out = dict(_drawn_inputs(seed))
    spreads = {}
    factors = {'norm1_g': 2.893,
     'conv_dw_b': 8.0,
     'conv_norm_g': 4.961,
     'conv_norm_b': 23.723,
     'conv_pw_b': 8.0,
     'na_rpb': 8.0,
     'b_pool_2': 5.262,
     'conv_b_2': 8.0}
    for name, (base, spread) in spreads.items():
        noise = np.random.default_rng([zlib.crc32(name.encode()), seed]).standard_normal(out[name].shape)
        drawn = base * np.exp(spread * noise) if base else spread * noise
        out[name] = __import__('jax').numpy.asarray(drawn.astype(out[name].dtype))
    for name, factor in factors.items():
        out[name] = (out[name] * factor).astype(out[name].dtype)
    return out
```

```python
import math
from contextlib import ExitStack

import numpy as np

import concourse.bass as bass
from concourse import mybir

F32 = mybir.dt.float32
F32R = mybir.dt.float32r
I32 = mybir.dt.int32
ACT = mybir.ActivationFunctionType
ALU = mybir.AluOpType
AX = mybir.AxisListType

P = 128
SEQ = 1024
D = 1024
KT = D // P
TT = SEQ // P
CTX = 256
CT = CTX // P
HALF = 512
GRID_W = 64
HEADS = 8
PAIRS = HEADS // 2
DH = 64
SCALE = DH ** -0.5
D_FF = 4 * D
RMS_EPS = 1e-6
LN_EPS = 1e-5
TAPS = 31
PADT = TAPS // 2
D_IN = 2304
W_IN_TILES = D_IN // P
Q0, K0, V0 = 6, 10, 14
RPB_ROWS, RPB_COLS = 15, 31
RPB_PAD = 64
RPB_LEN = HEADS * RPB_ROWS * RPB_COLS + 2 * RPB_PAD
BIAS_ROWS = 14
BIG = -1e30

D_IN2 = 2560
W_IN2_TILES = D_IN2 // P
Q2, K2, V2 = 2, 8, 14
GROUPS = 3
GH = 4
HEAD_AT = [0, 2, 1, 3]
D_FF2 = 2816
FF2_TILES = D_FF2 // P
ROT = 16
THETA = 500000.0

ADA2 = 6 * D // (D_FF // 256)

VECS = [("ada_b", 48), ("b_ada_2", 48), ("norm1_g", 8), ("norm2_g", 8), ("final_norm_g", 8),
        ("g_pre_mix_2", 8), ("g_post_mix_2", 8), ("g_pre_ffn_2", 8), ("g_post_ffn_2", 8),
        ("c", 8), ("c_ctx", 8), ("c_2", 8), ("conv_dw_w", 62), ("conv_dw_b", 2), ("conv_norm_g", 2),
        ("conv_norm_b", 2), ("conv_pw_b", 2), ("b_pool_2", 2), ("pool_scale_2", 2),
        ("conv_w_2", 66), ("conv_b_2", 22)]
VROW = {}
_n = 0
for _name, _rows in VECS:
    VROW[_name] = _n
    _n += _rows
VEC_TILES = -(-_n // P)

CONSTS = [("ident", 128), ("col_mask", 64), ("causal", 256), ("causal16", 128), ("rotate", 128),
          ("dft_c", 128), ("dft_s", 128), ("inv_freq", 1), ("pool_inv", 2), ("pool_head", 32)]
CCOL = {}
_n = 0
for _name, _cols in CONSTS:
    CCOL[_name] = (_n, _cols)
    _n += _cols
N_CONST = _n


def constants():
    out = np.zeros((P, N_CONST), np.float32)

    def put(name, a):
        c, n = CCOL[name]
        out[:, c:c + n] = a

    put("ident", np.eye(P))
    col = np.arange(GRID_W)
    start = np.clip(col - 8, 0, GRID_W - 16)
    ok = (col[None] >= start[:, None]) & (col[None] < start[:, None] + 16)
    put("col_mask", np.tile(np.where(ok, 0.0, BIG), (2, 1)))
    i = np.arange(P)[:, None]
    j = np.arange(P)[None]
    put("causal", np.concatenate([np.where(j >= i, 0.0, BIG), np.where(j <= i, 0.0, BIG)], 1))
    put("causal16", np.where((j <= i) & ((i - j) % 2 == 0), 0.0, BIG))
    rot = np.zeros((P, P))
    inv = np.zeros((P, 1), np.float32)
    f = np.float32(THETA) ** (-np.arange(0, ROT, 2, dtype=np.float32) / np.float32(ROT))
    for h in range(2):
        for a in range(ROT // 2):
            lo, hi = h * DH + a, h * DH + a + ROT // 2
            rot[hi, lo] = -1.0
            rot[lo, hi] = 1.0
            inv[lo] = inv[hi] = f[a]
    put("rotate", rot)
    put("inv_freq", inv)
    k = np.arange(64)
    ang = 2 * np.pi * ((k[:, None] * k[None]) % 64) / 64
    norm = 1.0 / math.sqrt(SEQ * 64)
    for name, m in (("dft_c", np.cos(ang)), ("dft_s", np.sin(ang))):
        bd = np.zeros((P, P))
        bd[:64, :64] = bd[64:, 64:] = m * norm
        put(name, bd)
    win = np.array([[2, 8], [4, 16]])[np.arange(P) // 64]
    put("pool_inv", 1.0 / win)
    t = np.arange(16)
    put("pool_head", (1.0 / np.minimum(t[None, None] + 1, win[:, :, None])).reshape(P, 32))
    return out


NYQ = SEQ // 2


def dft_seq():
    t = np.arange(SEQ)
    s = np.arange(NYQ + 1)
    ang = 2 * np.pi * ((t[:, None] * s[None]) % SEQ) / SEQ
    return np.concatenate([np.cos(ang), np.sin(ang[:, :NYQ])], 1).astype(np.float32)


WIN_U = [0, 0, 0, 2, 4, 6, 8, 8]
WIN_N = [512, 512, 640, 640, 640, 640, 512, 512]


def perm(ap, g, b):
    if g == 0:
        return ap[:, b * P:(b + 1) * P]
    if g == 1:
        return ap.rearrange("p (n i r) -> p n r i", n=2, r=4)[:, b // 4, b % 4]
    return ap.rearrange("p (k r) -> p r k", r=8)[:, b]


def two_pi_parts():
    parts, rest = [], 2 * math.pi
    for _ in range(3):
        e = 2.0 ** (math.floor(math.log2(rest)) - 7)
        parts.append(math.floor(rest / e) * e)
        rest -= parts[-1]
    return parts + [rest]


def bass_two_blocks(nc, a, out):
    with ExitStack() as ctx:
        base = -(-nc.sbuf_base // 32) * 32

        def at(name, kb, shape, dt=F32):
            return nc.alloc_sbuf_tensor_at("b_" + name, shape, dt, offset=base + int(kb * 1024))

        sems = {}

        def sem(name):
            if name not in sems:
                sems[name] = ctx.enter_context(nc.semaphore("s_" + name))
            return sems[name]

        PS = ctx.enter_context(nc.psum_tensor("ps_all", [P, 8, HALF], F32))

        def bank2(b):
            return PS[:, b:b + 2, :].rearrange("p b n -> p (b n)")

        vcol = at("vcol", 0, [P, VEC_TILES * P])
        cst = at("cst", 1.5, [P, N_CONST])
        ones = at("ones", 5.5, [P, P])
        sm = [at("small0", 6, [P, 256]), at("small1", 207, [P, 200])]
        w_raw = at("w_raw", 183, [P, 2, 1024])
        up_h = at("up_h", 191, [P, 2, 1024], F32R)
        up_l = at("up_l", 199, [P, 2, 1024], F32R)
        dn_h = at("dn_h", 71, [P, 2, 1024], F32R)
        dn_l = at("dn_l", 79, [P, 2, 1024], F32R)

        def vec(name, t=0, n=1):
            return vcol[:, bass.ds(t + VROW[name], n)]

        def const(name):
            c, n = CCOL[name]
            return cst[:, c:c + n]

        ident = const("ident")
        small_at = [0, 0]

        def small(n):
            i = 0 if small_at[0] + n <= 256 else 1
            small_at[i] += n
            return sm[i][:, small_at[i] - n:small_at[i]]

        mod1, modc, mod2 = small(48), small(16), small(48)
        silu_c = small(24)
        gs1, gsc, gs2, gsm, gsf, ggm, ggf = (small(8) for _ in range(7))
        ss10, root10, rstd10 = small(10), small(10), small(10)
        root8, rstd8 = small(8), small(8)
        pbias = small(2)
        st_m, st_m2, st_neg, st_d, st_d2, st_r = (small(2) for _ in range(6))

        hn1_h = at("hn1_h", 87, [P, KT, SEQ + CTX], F32R)
        hn1_l = at("hn1_l", 127, [P, KT, SEQ + CTX], F32R)
        xtok = at("xtok", 127, [P, TT + CT, D])
        xs = at("xs", 7, [P, KT, SEQ + CTX])
        ada_acc0 = at("ada_acc0", 49, [P, 4, 1024])
        junk = at("junk", 71, [P, 2, 1024])
        vrow = at("vrow", 69, [P, VEC_TILES, P])
        ada_ring0 = at("ada_ring0", 167, [P, 2, 1024])
        ada_ring1 = at("ada_ring1", 167, [P, 2, 512])
        ada_acc1 = at("ada_acc1", 171, [P, 512])
        vpad = at("vpad", 173, [P, 2, SEQ + 2 * PADT])
        pt1 = at("pt1", 7, [P, W_IN_TILES, SEQ])
        ckv = at("ckv", 79, [P, 2 * PAIRS, CTX])
        conv_out = at("conv_out", 15, [P, 2, SEQ])
        conv_sq = conv_out
        conv_acc = at("conv_acc", 23, [P, 2, SEQ])
        pw = at("pw", 177, [P, 2, 256])
        ln_r = at("ln_r", 173, [P, SEQ])
        four_y = at("four_y", 7, [P, 2, SEQ])
        dseq = at("dseq", 87, [P, TT, 2 * NYQ + 1])
        zf = at("zf", 119.875, [P, TT, HALF])
        four_ab = at("four_ab", 163, [P, 2, HALF])
        wf = at("wf", 167, [P, 2, 256])
        four_e = [at("four_e0", 169, [P, HALF]), at("four_e1", 136.5, [P, HALF])]
        qs = [at(f"qs{s}", 87 + 4 * s, [P, SEQ]) for s in range(2)]
        ks = [at(f"ks{s}", 95 + 5 * s, [P, SEQ + CTX]) for s in range(2)]
        vs = at("vs", 105, [P, SEQ + CTX])
        prob = [at(f"prob{s}", 110 + 3.5 * s, [P, 896]) for s in range(2)]
        sbias = [at(f"sbias{s}", 117 + 2.5 * s, [P, 640]) for s in range(2)]
        probt = [at(f"probt{s}", 122 + 3.5 * s, [P, 896]) for s in range(2)]
        vt = [at(f"vt{s}", 129 + 5 * s, [P, TT + CT, P]) for s in range(2)]
        tb = [at(f"tb{s}", 139 + 7 * s, [P, 2, BIAS_ROWS * GRID_W]) for s in range(2)]
        tbm = [at(f"tbm{s}", 153 + 5 * s, [P, 2, 640]) for s in range(2)]
        ao = at("ao", 163, [P, PAIRS, SEQ])
        rdiag = [at(f"rdiag{s}", 179 + 0.5 * s, [P, P]) for s in range(2)]
        mix_h = at("mix_h", 39, [P, KT, SEQ], F32R)
        mix_l = at("mix_l", 87, [P, KT, SEQ], F32R)
        xslab = at("xslab", 119, [P, 2, TT, P])
        xt = at("xt", 7, [P, KT, SEQ])
        hn_h = at("hn_h", 119, [P, KT, SEQ], F32R)
        hn_l = at("hn_l", 151, [P, KT, SEQ], F32R)
        hid_h = at("hid_h", 39, [P, 2, 2, SEQ], F32R)
        hid_l = at("hid_l", 55, [P, 2, 2, SEQ], F32R)
        nsq = at("nsq", 39, [P, 2, SEQ])
        ndiag = at("ndiag", 47, [P, SEQ])
        nhn = at("nhn", 51, [P, 2, SEQ])
        sq = at("sq", 87, [P, 2, SEQ])
        ada_in2 = at("ada_in2", 95, [P, KT, ADA2])
        ada_acc2 = at("ada_acc2", 107, [P, ADA2])
        pt2 = at("pt2", 7, [P, W_IN2_TILES, SEQ])
        cos = at("cos", 87, [P, SEQ])
        sin = at("sin", 91, [P, SEQ])
        pos = at("pos", 95, [P, SEQ], I32)
        ang = at("ang", 99, [P, SEQ])
        turn = at("turn", 103, [P, SEQ])
        turn_i = at("turn_i", 107, [P, SEQ], I32)
        v2 = at("v2", 95, [P, GROUPS * TT, 256])
        qk2 = at("qk2", 119, [P, 12, SEQ])
        rt = [at(f"rt{s}", 167 + 4 * s, [P, SEQ]) for s in range(2)]
        rt2 = [at(f"rt2{s}", 175 + 4 * s, [P, SEQ]) for s in range(2)]
        ps2 = at("pools2", 43, [P, SEQ])
        ps4 = at("pools4", 47, [P, SEQ])
        pmix = at("pmix", 51, [P, 2, SEQ])
        pout = at("pout", 59, [P, SEQ])
        wp = at("wp", 85, [P, 2, P])
        s2 = [at(f"sc2{s}", 15 + 4 * s, [P, GH, 256]) for s in range(2)]
        pr2 = [at(f"pr2{s}", 23 + 4 * s, [P, GH, 256]) for s in range(2)]
        pt2t = [at(f"pt2t{s}", 31 + 4 * s, [P, 8, P]) for s in range(2)]
        ROWW = GH * DH + 2 * GH
        og = [at(f"og{s}", 87 + 1.5 * s, [P, ROWW]) for s in range(4)]
        oall = at("oall", 43, [P, TT, GROUPS, ROWW])
        cw = at("cw", 15, [P, TT, GROUPS, GH])
        cmax = at("cmax", 15.5, [P, TT, GH])
        cwn = at("cwn", 32, [P, TT, GROUPS, GH])
        cden = at("cden", 15.75, [P, TT, GH])
        csum = at("csum", 16, [P, TT, GH, DH])
        cterm = at("cterm", 24, [P, TT, GH, DH])
        mix2_h = at("mix2_h", 69, [P, 4, SEQ], F32R)
        mix2_l = at("mix2_l", 167, [P, 4, SEQ], F32R)
        y2 = at("y2", 87, [P, KT, SEQ])
        gbuf = at("gbuf", 7, [P, 2, SEQ])
        gelu = at("gelu", 15, [P, 2, SEQ])
        gv = at("gv", 23, [P, 2, SEQ])
        otok = at("otok", 119, [P, 2, D])

        st2_neg = [small(GH), small(GH)]
        st2_den = [x[:, GH * DH + GH:] for x in og]

        def keys2(n):
            g, b = divmod(n, TT)
            return 256 if (g == 0 and b) or (g == 1 and b >= 4) else P

        st_rr = small(4)

        def vpad_edges(side):
            lo = 0 if side == 0 else PADT + SEQ
            return vpad[:, :, lo:lo + PADT]

        o_rows = nc.dram_tensor("o_rows", [GROUPS, SEQ, ROWW], F32, kind="Internal").ap()
        rpb_rows = nc.dram_tensor("rpb_rows", [GRID_W, RPB_LEN], F32, kind="Internal").ap()
        xt_spill = nc.dram_tensor("xt_spill", [2, P, KT, SEQ], F32, kind="Internal").ap()

        U_G2, U_WO1 = 0, W_IN_TILES
        U_FF1 = U_WO1 + KT
        CH1 = D_FF // (2 * P)
        U_WIN2 = U_FF1 + 2 * CH1
        U_WO2 = U_WIN2 + W_IN2_TILES
        U_FF2 = U_WO2 + KT
        CH2 = FF2_TILES // 2
        C_FF1, C_FF2 = 0, CH1

        w_in = a["w_in"]
        raw_in = [sem("raw_in0"), sem("raw_in1")]
        up_full, dn_full = sem("up_full"), sem("dn_full")
        up_done = sem("up_done")
        up_evac = sem("up_evac")
        dn_done, dn_evac = sem("dn_done"), sem("dn_evac")
        raw_split = sem("raw_high")

        def up_src(w, col, kt=KT):
            return w.rearrange("(k p) f -> p k f", p=P)[:, :, col]

        block = ctx.enter_context(nc.Block())

        def carry(eng):
            eng.sem_inc(sem("carried"), 1)

        def load_up(sp, u, w, m, slot, raw_n, kt=KT, dn_before=None):
            sp.wait_ge(up_full, u + 1)
            if dn_before is not None:
                carry(sp)
                sp.wait_ge(dn_full, dn_before)
            carry(sp)
            sp.dma_start(w_raw[:, slot, 0:kt * P].rearrange("p (k f) -> p k f", k=kt),
                         up_src(w, bass.ts(m, P))).then_inc(raw_in[slot], 16)

        def load_dn(sp, d, w, row, slot, u_before):
            sp.wait_ge(up_full, u_before)
            carry(sp)
            sp.dma_start(w_raw[:, slot, :], w[bass.ts(row, P), :]).then_inc(raw_in[slot], 16)

        def split_up(pool, u, slot, raw_n, n_split, kt=KT):
            n = kt * P
            pool.wait_ge(raw_in[slot], 16 * raw_n)
            pool.wait_ge(up_done, u + 1)
            carry(pool)
            pool.tensor_scalar(up_h[:, slot, 0:n], w_raw[:, slot, 0:n], 0.0, 1.0, ALU.add,
                               ALU.mult).then_inc(raw_split, 1)
            pool.wait_ge(raw_split, n_split)
            pool.tensor_tensor(up_l[:, slot, 0:n], w_raw[:, slot, 0:n],
                               up_h[:, slot, 0:n].bitcast(F32), ALU.subtract).then_inc(up_full, 1)

        def split_dn(pool, d, slot, raw_n, n_split, units_before):
            pool.wait_ge(raw_in[slot], 16 * raw_n)
            pool.wait_ge(dn_done, units_before + 1)
            carry(pool)
            pool.tensor_scalar(dn_h[:, slot, :], w_raw[:, slot, :], 0.0, 1.0, ALU.add,
                               ALU.mult).then_inc(raw_split, 1)
            pool.wait_ge(raw_split, n_split)
            pool.tensor_tensor(dn_l[:, slot, :], w_raw[:, slot, :],
                               dn_h[:, slot, :].bitcast(F32), ALU.subtract).then_inc(dn_full, 1)

        def mul_up(pe, u, slot, xh, xl, kt=KT, extra=None):
            pe.wait_ge(up_full, u + 3)
            pe.wait_ge(up_evac, u + 1)
            spans = [(PS[:, 2 * slot + j, :], j * HALF, HALF) for j in range(2)]
            if extra:
                spans.append((PS[:, 4 + slot, 0:extra], SEQ, extra))
            for k in range(kt):
                for n, (w, x) in enumerate(((up_h, xh), (up_h, xl), (up_l, xh))):
                    for dst, c, width in spans:
                        mm = pe.matmul(dst, w[:, slot, k * P:(k + 1) * P], x[:, k, c:c + width],
                                       start=(k == 0 and n == 0), stop=(k == kt - 1 and n == 2))
            mm.then_inc(up_done, 1)

        def mul_dn(pe, d, hid, unit0):
            pe.wait_ge(dn_full, d + 4)
            for m in range(KT):
                for j in range(2):
                    i = 2 * m + j
                    pe.wait_ge(dn_evac, unit0 + i + 1)
                    for k in range(2):
                        for n, (w, x) in enumerate(((dn_h, hid_h), (dn_h, hid_l), (dn_l, hid_h))):
                            mm = pe.matmul(PS[:, 4 + i % 2, :], w[:, k, m * P:(m + 1) * P],
                                           x[:, hid, k, j * HALF:(j + 1) * HALF],
                                           start=(k == 0 and n == 0), stop=(k == 1 and n == 2))
                    mm.then_inc(dn_done, 1)

        NORMS = {"mlp": 0, "final": 1, "mix2": 2, "post2": 3, "ffn2": 4, "out": 5}
        MODULATED = {"mlp": 0, "mix2": 1, "ffn2": 2}
        nsem = {s: sem("norm_" + s) for s in ("sq", "sums", "root", "rstd", "diag", "bc", "hn", "mod", "high", "low")}

        def norm_scalar(act, n, src):
            n8, n1 = KT * NORMS[n], NORMS[n]
            for k in range(KT):
                if k >= 2:
                    act.wait_ge(nsem["sums"], n8 + k - 1)
                act.activation(nsq[:, k % 2, :], src[:, k, :], ACT.Square).then_inc(nsem["sq"], 1)
            act.wait_ge(nsem["sums"], n8 + KT)
            act.activation(root8, PS[:, 7, 0:TT], ACT.Sqrt, scale=1.0 / D,
                           bias=eps_rms).then_inc(nsem["root"], 1)

        def norm_tensor(pe, n):
            n8, n1 = KT * NORMS[n], NORMS[n]
            for k in range(KT):
                pe.wait_ge(nsem["sq"], n8 + k + 1)
                for t in range(TT):
                    mm = pe.matmul(PS[:, 7, t:t + 1], nsq[:, k % 2, t * P:(t + 1) * P], ones[:, 0:1],
                                   start=(k == 0 and t == 0), stop=(k == KT - 1), skip_group_check=True)
                mm.then_inc(nsem["sums"], 1)
            pe.wait_ge(nsem["diag"], n8 + TT)
            for j in range(2):
                mm = pe.matmul(PS[:, j, :], ones[:, :], ndiag[:, j * HALF:(j + 1) * HALF],
                               start=True, stop=True)
            mm.then_inc(nsem["bc"], 1)

        def norm_vector(dve, n):
            n8, n1 = KT * NORMS[n], NORMS[n]
            dve.wait_ge(nsem["root"], n1 + 1)
            dve.reciprocal(rstd8, root8).then_inc(nsem["rstd"], 1)
            dve.wait_ge(nsem["rstd"], n1 + 1)
            for t in range(TT):
                dve.tensor_scalar(ndiag[:, t * P:(t + 1) * P], ident, rstd8[:, t:t + 1], None,
                                  ALU.mult).then_inc(nsem["diag"], 1)
            dve.wait_ge(nsem["bc"], n1 + 1)

        def modulate_vector(dve, n, src):
            n8 = KT * MODULATED[n]
            for k in range(KT + 1):
                if k < KT:
                    if k >= 2:
                        dve.wait_ge(nsem["low"], n8 + k - 1)
                    dve.tensor_tensor(nhn[:, k % 2, :], src[:, k, :], bank2(0), ALU.mult
                                      ).then_inc(nsem["hn"], 1)
                if k >= 1:
                    j = k - 1
                    dve.wait_ge(nsem["high"], n8 + j + 1)
                    dve.tensor_tensor(hn_l[:, j, :], nhn[:, j % 2, :], hn_h[:, j, :].bitcast(F32),
                                      ALU.subtract).then_inc(nsem["low"], 1)

        def modulate_scalar(act, n, gs, sh):
            n8 = KT * MODULATED[n]
            for k in range(KT):
                act.wait_ge(nsem["hn"], n8 + k + 1)
                act.activation(nhn[:, k % 2, :], nhn[:, k % 2, :], ACT.Identity, scale=gs[:, k:k + 1],
                               bias=sh[:, k:k + 1]).then_inc(nsem["mod"], 1)
                act.wait_ge(nsem["mod"], n8 + k + 1)
                act.activation(hn_h[:, k, :], nhn[:, k % 2, :], ACT.Copy).then_inc(nsem["high"], 1)

        eps_rms = small(1)
        eps_ln = small(1)

        @block.sync
        def _(sp):
            sp.dma_start(vrow[:, :, :], a["vecs"].rearrange("(t p) f -> p t f", p=P)).then_inc(sem("tables_in"), 16)
            sp.dma_start(cst[:, :], a["consts"]).then_inc(sem("tables_in"), 16)
            for b in range(2):
                for k in range(KT):
                    n = b * KT + k
                    sp.wait_ge(sem("ada_used"), n + 1)
                    sp.dma_start(ada_ring0[:, n % 2, :], a["ada_w"][bass.ts(k, P), bass.ts(b, 1024)]
                                 ).then_inc(sem(f"ada_in{n % 2}"), 16)
            with sp.Fori(0, 5) as i:
                for s in range(2):
                    load_up(sp, i * 2 + s, w_in, i * 2 + s, s, None)
            sp.wait_ge(sem("ada_sum0"), 2)
            with sp.Fori(0, 4) as i:
                for s in range(2):
                    load_up(sp, i * 2 + K0 + s, w_in, i * 2 + K0 + s, s, None)
                for b in range(2):
                    for k in range(KT):
                        s = k % 2
                        sp.wait_ge(sem("ada1_used"), i * 16 + b * KT + k + 1)
                        sp.dma_start(ada_ring1[:, s, :], a["ada_w"][bass.ts(k, P),
                                     bass.ds(i * 1024 + 2048 + b * 512, 512)]).then_inc(sem(f"ada1_in{s}"), 16)
            sp.dma_start(rpb_rows, bass.AP(a["rpb"].tensor, 0, [[0, GRID_W], [1, RPB_LEN]])).then_inc(sem("rpb_in"), 16)
            for m in range(2):
                load_up(sp, U_WO1 + m, a["w_out"], m, m, None)
            sp.wait_ge(up_done, U_WO1 + 2)
            sp.wait_ge(sem("ada1_mod"), 8)
            sp.dma_start(dseq[:, :, :], a["dft_seq"].rearrange("(t p) f -> p t f", p=P)).then_inc(sem("four_in"), 16)
            sp.dma_start(wf[:, :, :], a["w_fourier"].rearrange("(t p) f -> p t f", p=P)).then_inc(sem("four_in"), 16)
            sp.wait_ge(sem("taps"), 2 * TAPS)
            sp.dma_start(pw[:, :, :], a["conv_pw_w"].rearrange("(t p) f -> p t f", p=P)).then_inc(sem("point_in"), 16)
            sp.wait_ge(sem("rpb_in"), 16)
            for p in range(PAIRS):
                s = p % 2
                if p >= 2:
                    sp.wait_ge(sem("na_biased"), 16 * p + 1)
                for h in range(2):
                    for par in range(2):
                        off = RPB_PAD + (2 * p + h) * RPB_ROWS * RPB_COLS + (1 - par) * RPB_COLS + RPB_COLS // 2
                        src = bass.AP(rpb_rows.tensor, off, [[RPB_LEN - 1, GRID_W], [RPB_COLS, BIAS_ROWS], [1, GRID_W]])
                        dst = tb[s][par * GRID_W:(par + 1) * GRID_W, h, :].rearrange("p (r c) -> p r c", c=GRID_W)
                        sp.dma_start(dst, src).then_inc(sem(f"bias_in{s}"), 16)
            sp.wait_ge(sem("na_o"), 16 * PAIRS + 1)
            for m in range(2):
                sp.dma_start(xslab[:, m, :, :], a["x"].rearrange("(t p) f -> p t f", p=P)[:, :, bass.ts(m, P)]
                             ).then_inc(sem(f"slab_in{m}"), 16)
            with sp.Fori(1, 4) as i:
                for s in range(2):
                    load_up(sp, i * 2 + U_WO1 + s, a["w_out"], i * 2 + s, s, None)
                    sp.wait_ge(sem("slab_used"), i * 2 + s - 1)
                    sp.dma_start(xslab[:, s, :, :], a["x"].rearrange("(t p) f -> p t f", p=P)[:, :, bass.ds((i * 2 + s) * P, P)]
                                 ).then_inc(sem(f"slab_in{s}"), 16)
            def ff1_up(c):
                for s in range(2):
                    load_up(sp, c * 2 + U_FF1 + s, a["mlp_w1"], c * 2 + s, s, None, dn_before=c * 2 + s - 1 + 2 * C_FF1)

            def ff1_dn(c):
                for s in range(2):
                    load_dn(sp, None, a["mlp_w2"], c * 2 + s, s, c * 2 + U_FF1 + 2 + 3 + s)

            def ada2_in(b):
                sp.wait_ge(sem("ada2_used"), b * KT + 2)
                carry(sp)
                sp.dma_start(ada_in2[:, :, :], a["w_ada_2"].rearrange("(k p) f -> p k f", p=P)[:, :, bass.ds(b * ADA2, ADA2)]
                             ).then_inc(sem("ada2_in"), 16)

            for s in range(2):
                load_up(sp, U_FF1 + s, a["mlp_w1"], s, s, None)
            sp.wait_ge(up_done, U_FF1 + 2)
            ada2_in(0)
            with sp.Fori(0, (CH1 - 2) // 2) as j:
                for e in range(2):
                    ff1_up(j * 2 + 1 + e)
                    ada2_in(j * 2 + 1 + e)
                    ff1_dn(j * 2 + e)
            ff1_up(CH1 - 1)
            ada2_in(CH1 - 1)
            ff1_dn(CH1 - 2)
            for s in range(2):
                sp.wait_ge(dn_full, 2 * (CH1 - 2) + s + 3)
                load_dn(sp, None, a["mlp_w2"], 2 * (CH1 - 1) + s, s, U_FF1 + 2 * CH1 + 2)
            sp.wait_ge(dn_done, 16 * CH1 + 1)
            sp.dma_start(pos[:, :], bass.AP(a["positions_2"].tensor, 0, [[0, P], [1, SEQ]])).then_inc(sem("pos_in"), 16)
            for s in range(2):
                load_up(sp, U_WIN2 + s, a["w_in_2"], s, s, None, dn_before=2 * CH1 + 2)
            sp.wait_ge(sem("x1_ready"), KT)
            sp.dma_start(xt_spill[0], xt[:, :, :]).then_inc(sem("x_moved"), 16)
            with sp.Fori(1, W_IN2_TILES // 2) as i:
                for s in range(2):
                    load_up(sp, i * 2 + U_WIN2 + s, a["w_in_2"], i * 2 + s, s, None)
            for m in range(2):
                load_up(sp, U_WO2 + m, a["w_out_2"], m, m, None, kt=4)
            sp.wait_ge(sem("v2_turned"), GROUPS * TT // 4)
            sp.dma_start(wp[:, :, :], a["w_pool"].rearrange("c p f -> p c f")).then_inc(sem("point_in"), 16)
            for g in range(GROUPS):
                rows = o_rows[g]
                for b in range(TT):
                    n = g * TT + b
                    sp.wait_ge(sem("o2_ready"), n + 1)
                    if g == 0:
                        dst = rows[b * P:(b + 1) * P]
                    elif g == 1:
                        dst = rows.rearrange("(n i r) w -> n r i w", n=2, r=4)[b // 4, b % 4]
                    else:
                        dst = rows.rearrange("(k r) w -> r k w", r=8)[b]
                    sp.dma_start(dst, og[n % 4][:, :]).then_inc(sem(f"o2_out{n % 4}"), 16)
            for e in range(4):
                sp.wait_ge(sem(f"o2_out{e}"), 16 * GROUPS * TT // 4)
            for g in range(GROUPS):
                sp.dma_start(oall[:, :, g, :], o_rows[g].rearrange("(t p) w -> p t w", p=P)).then_inc(sem("oall_in"), 16)
            with sp.Fori(1, KT // 2) as i:
                for s in range(2):
                    load_up(sp, i * 2 + U_WO2 + s, a["w_out_2"], i * 2 + s, s, None, kt=4)
            sp.wait_ge(sem("mix2_split"), 4)
            sp.wait_ge(sem("x_moved"), 16)
            sp.dma_start(xt[:, :, :], xt_spill[0]).then_inc(sem("x_moved"), 16)
            def ff2_up(c):
                for i in range(4):
                    f = c * 2 + i // 2 + (FF2_TILES if i % 2 else 0)
                    load_up(sp, c * 4 + U_FF2 + i, a["w_up_2"], f, i % 2, None,
                            dn_before=(c * 2 + i - 1 + 2 * C_FF2) if i < 2 else None)

            def ff2_dn(c):
                for s in range(2):
                    load_dn(sp, None, a["w_down_2"], c * 2 + s, s, c * 4 + U_FF2 + 4 + 5 + s)

            ff2_up(0)
            sp.wait_ge(sem("x2_ready"), KT)
            sp.dma_start(xt_spill[1], xt[:, :, :]).then_inc(sem("x_moved"), 16)
            with sp.Fori(0, (CH2 - 1) // 2) as j:
                ff2_up(j * 2 + 1)
                ff2_dn(j * 2)
                ff2_up(j * 2 + 2)
                ff2_dn(j * 2 + 1)
            for s in range(2):
                sp.wait_ge(dn_full, 2 * (C_FF2 + CH2 - 2) + s + 3)
                load_dn(sp, None, a["w_down_2"], 2 * (CH2 - 1) + s, s, U_FF2 + 4 * CH2 + 2)
            sp.wait_ge(sem("ff2_low"), 2 * CH2)
            sp.wait_ge(sem("x_moved"), 48)
            sp.dma_start(xt[:, :, :], xt_spill[1]).then_inc(sem("x_moved"), 16)
            for t in range(TT):
                sp.wait_ge(sem("o_ready"), t + 1)
                sp.dma_start(out[t * P:(t + 1) * P, :], otok[:, t % 2, :]).then_inc(sem(f"stored{t % 2}"), 16)
            for s in range(2):
                sp.wait_ge(sem(f"stored{s}"), 16 * TT // 2)

        @block.gpsimd
        def _(pool):
            pool.sem_inc(up_full, 2)
            pool.sem_inc(dn_full, 2)
            pool.sem_inc(up_done, 2)
            pool.sem_inc(up_evac, 2)
            pool.sem_inc(dn_evac, 2)
            pool.sem_inc(sem("ada_used"), 2)
            pool.sem_inc(sem("ada1_used"), 2)
            pool.sem_inc(sem("ada2_used"), 2)
            pool.sem_inc(sem("mod2"), 1)
            pool.sem_inc(sem("na_biased"), 17)
            pool.sem_inc(dn_done, 1)
            pool.sem_inc(sem("v_turned"), 1)
            pool.sem_inc(sem("probt_set"), 1)
            pool.sem_inc(sem("na_o"), 1)
            pool.memset(ones[:, :], 1.0).then_inc(sem("ones_set"), 1)
            pool.memset(eps_rms, RMS_EPS).then_inc(sem("ones_set"), 1)
            pool.memset(eps_ln, LN_EPS).then_inc(sem("ones_set"), 1)
            with pool.Fori(0, W_IN_TILES // 2) as i:
                for s in range(2):
                    split_up(pool, i * 2 + s, s, i + 1, i * 2 + s + 1)
            for s in range(2):
                split_up(pool, U_WO1 + s, s, U_WO1 // 2 + 1, U_WO1 + s + 1)
            with pool.Fori(0, PAIRS // 2) as i:
                for s in range(2):
                    pool.wait_ge(up_evac, W_IN_TILES + 2)
                    pool.wait_ge(sem("four_done"), 4)
                    pool.wait_ge(sem("na_biased"), i * 32 + (16 * s + 1))
                    pool.tensor_copy(qs[s][:, :], pt1[:, i * 2 + (Q0 + s), :]).then_inc(sem("staged"), 1)
                    pool.tensor_copy(ks[s][:, 0:SEQ], pt1[:, i * 2 + (K0 + s), :]).then_inc(sem("staged"), 1)
                    pool.tensor_copy(ks[s][:, SEQ:], ckv[:, i * 2 + s, :]).then_inc(sem("staged"), 1)
                    pool.wait_ge(sem("v_turned"), i * 4 + (2 * s + 1))
                    pool.tensor_copy(vs[:, 0:SEQ], pt1[:, i * 2 + (V0 + s), :]).then_inc(sem("staged"), 1)
                    pool.tensor_copy(vs[:, SEQ:], ckv[:, i * 2 + (PAIRS + s), :]).then_inc(sem("staged"), 1)
                    pool.wait_ge(sem(f"bias_in{s}"), i * 64 + 64)
                    tbv = tb[s][:, :, :].rearrange("p h (r c) -> p (h r) c", c=GRID_W)
                    pool.tensor_tensor(tbv, tbv, const("col_mask").unsqueeze(1).to_broadcast([P, 2 * BIAS_ROWS, GRID_W]),
                                       ALU.add).then_inc(sem("bias_set"), 1)
                    pool.wait_ge(sem("bias_set"), i * 10 + 5 * s + 1)
                    carry(pool)
                    pool.tensor_copy(tbm[s][:, :, :], tb[s][:, :, 2 * GRID_W:12 * GRID_W]).then_inc(sem("bias_set"), 1)
                    pool.wait_ge(sem("bias_set"), i * 10 + 5 * s + 2)
                    carry(pool)
                    pool.memset(tbm[s][0:64, :, 8 * GRID_W:], BIG).then_inc(sem("bias_set"), 1)
                    pool.memset(tbm[s][64:P, :, 0:GRID_W], BIG).then_inc(sem("bias_set"), 1)
                    pool.memset(tbm[s][64:P, :, 9 * GRID_W:], BIG).then_inc(sem("bias_set"), 1)
                    pool.wait_ge(sem("bias_set"), i * 10 + 5 * s + 5)
            with pool.Fori(1, KT // 2) as i:
                for s in range(2):
                    split_up(pool, i * 2 + U_WO1 + s, s, i + U_WO1 // 2 + 1, i * 2 + U_WO1 + s + 1)

            r0 = U_FF1

            def ff1_up(c, r):
                for s in range(2):
                    split_up(pool, c * 2 + U_FF1 + s, s, r + 1, r * 2 + s + 1)

            def ff1_dn(c, r):
                for s in range(2):
                    split_dn(pool, None, s, r + 1, r * 2 + s + 1, c * 16)

            ff1_up(0, r0 // 2)
            with pool.Fori(0, (CH1 - 2) // 2) as j:
                ff1_up(j * 2 + 1, j * 4 + r0 // 2 + 1)
                ff1_dn(j * 2, j * 4 + r0 // 2 + 2)
                ff1_up(j * 2 + 2, j * 4 + r0 // 2 + 3)
                ff1_dn(j * 2 + 1, j * 4 + r0 // 2 + 4)
            n = 2 * (CH1 - 2) + r0 // 2 + 1
            ff1_up(CH1 - 1, n)
            ff1_dn(CH1 - 2, n + 1)
            ff1_dn(CH1 - 1, n + 2)
            r1 = r0 + 4 * CH1
            with pool.Fori(0, W_IN2_TILES // 2) as i:
                for s in range(2):
                    split_up(pool, i * 2 + U_WIN2 + s, s, i + r1 // 2 + 1, i * 2 + r1 + s + 1)
            r2 = r1 + W_IN2_TILES
            for s in range(2):
                split_up(pool, U_WO2 + s, s, r2 // 2 + 1, r2 + s + 1, kt=4)
            with pool.Fori(1, KT // 2) as i:
                for s in range(2):
                    split_up(pool, i * 2 + U_WO2 + s, s, i + r2 // 2 + 1, i * 2 + r2 + s + 1, kt=4)
            r3 = r2 + KT

            def ff2_up(c, r):
                for i in range(4):
                    split_up(pool, c * 4 + U_FF2 + i, i % 2, r + 1 + i // 2, r * 2 + i + 1)

            def ff2_dn(c, r):
                for s in range(2):
                    split_dn(pool, None, s, r + 1, r * 2 + s + 1, c * 16 + 16 * C_FF2)

            ff2_up(0, r3 // 2)
            with pool.Fori(0, (CH2 - 1) // 2) as j:
                ff2_up(j * 2 + 1, j * 6 + r3 // 2 + 2)
                ff2_dn(j * 2, j * 6 + r3 // 2 + 4)
                ff2_up(j * 2 + 2, j * 6 + r3 // 2 + 5)
                ff2_dn(j * 2 + 1, j * 6 + r3 // 2 + 7)
            ff2_dn(CH2 - 1, 3 * (CH2 - 1) + r3 // 2 + 2)

        @block.scalar
        def _(act):
            for t in range(0, TT + CT, 2):
                src = a["x"][t * P:(t + 2) * P, :] if t < TT else a["ctx"]
                act.dma_start(xtok[:, t:t + 2, :], src.rearrange("(t p) f -> p t f", p=P)).then_inc(sem(f"x_in{t // 2}"), 16)
            act.wait_ge(sem("ones_set"), 3)
            for t in range(TT + CT):
                act.wait_ge(sem(f"x_in{t // 2}"), 16)
                if t >= 2:
                    act.wait_ge(sem("ss"), t - 1)
                act.activation(junk[:, t % 2, :], xtok[:, t, :], ACT.Square, accum_out=ss10[:, t:t + 1]).then_inc(sem("ss"), 1)
            act.wait_ge(sem("ss"), TT + CT)
            act.activation(root10, ss10, ACT.Sqrt, scale=1.0 / D, bias=eps_rms).then_inc(sem("root10"), 1)
            act.wait_ge(sem("vec_set"), 1)
            act.activation(silu_c, vec("c", 0, 24), ACT.Silu).then_inc(sem("silu"), 1)
            act.wait_ge(sem("rstd10"), 1)
            for t in range(TT + CT + 1):
                if t < TT + CT:
                    act.activation(xtok[:, t, :], xtok[:, t, :], ACT.Copy, scale=rstd10[:, t:t + 1]
                                   ).then_inc(sem("x_scaled"), 1)
                if t >= 1:
                    act.wait_ge(sem("x_turned"), t)
                    act.activation(xs[:, :, (t - 1) * P:t * P],
                                   bank2(2 * ((t - 1) % 2)).rearrange("p (k n) -> p k n", n=P), ACT.Copy
                                   ).then_inc(sem("xs_set"), 1)
            for k in range(KT):
                act.wait_ge(sem("hn1"), 2 * (k + 1))
                act.activation(hn1_h[:, k, :], xs[:, k, :], ACT.Copy).then_inc(sem("hn1_high"), 1)

            def out1(u, scale=1.0, ctx_tile=None, slot=0):
                act.wait_ge(up_done, u + 3)
                if ctx_tile is not None:
                    act.activation(ckv[:, ctx_tile, :], PS[:, 4 + slot, 0:CTX], ACT.Copy).then_inc(sem("ckv_set"), 1)
                act.activation(pt1[:, u, :], bank2(2 * slot), ACT.Copy, scale=scale).then_inc(up_evac, 1)

            act.wait_ge(sem("hn1_low"), KT)
            with act.Fori(0, Q0 // 2) as i:
                for s in range(2):
                    out1(i * 2 + s, slot=s)
            act.wait_ge(up_evac, Q0 + 2)
            act.activation(pt1[:, 4:6, :], pt1[:, 4:6, :], ACT.Sigmoid).then_inc(sem("gate"), 1)
            with act.Fori(Q0 // 2, K0 // 2) as i:
                for s in range(2):
                    out1(i * 2 + s, scale=SCALE, slot=s)
            with act.Fori(0, 4) as i:
                for s in range(2):
                    out1(i * 2 + (K0 + s), ctx_tile=i * 2 + s, slot=s)
            for c in range(2):
                act.wait_ge(sem("four_w"), c + 1)
                act.activation(four_ab[:, c, :], PS[:, 6 + c, :], ACT.Copy).then_inc(sem("four_ab"), 1)
            for t in range(TT):
                act.wait_ge(sem("four_z"), t + 1)
                act.activation(zf[:, t, :], PS[:, 4 + t % 2, :], ACT.Copy).then_inc(sem("zf_set"), 1)
            for c in range(2):
                act.wait_ge(sem("ln_d"), c + 1)
                act.activation(conv_sq[:, c, :], conv_acc[:, c, :], ACT.Square).then_inc(sem("ln_sq"), 1)
            act.wait_ge(sem("ln_sums"), 2)
            act.activation(ln_r[:, :], bank2(2), ACT.Sqrt, scale=1.0 / 256, bias=eps_ln).then_inc(sem("ln_root"), 1)
            for n in range(2):
                act.wait_ge(sem("four_done"), 2 * n + 1)
                act.activation(four_e[n][:, :], PS[:, 6 - 2 * n, :], ACT.Copy).then_inc(sem("four_e"), 1)
                act.activation(four_y[:, n, NYQ:NYQ + 1], PS[:, n, 0:1], ACT.Copy).then_inc(sem("four_e"), 1)
            for c in range(2):
                act.wait_ge(sem("ln_y"), c + 1)
                act.activation(conv_acc[:, c, :], conv_acc[:, c, :], ACT.Silu, scale=vec("conv_norm_g", c),
                               bias=vec("conv_norm_b", c)).then_inc(sem("conv_s"), 1)
            for m in range(2):
                act.wait_ge(sem("conv_pw"), m + 1)
                act.activation(conv_out[:, m, :], bank2(2 * m), ACT.Identity, bias=vec("conv_pw_b", m)
                               ).then_inc(sem("conv_done"), 1)
            act.wait_ge(sem("four_mir"), 4)
            with act.Fori(0, PAIRS // 2) as i:
                for s in range(2):
                    n0 = i * 32 + 16 * s
                    for r in range(2):
                        lo, cnt = 8 * r, 8 if r == 0 else 2
                        act.wait_ge(sem("v_turned"), i * 4 + (2 * s + r + 2))
                        act.activation(vt[s][:, lo:lo + cnt, :], bank2(4)[:, 0:cnt * P].rearrange("p (t c) -> p t c", c=P),
                                       ACT.Copy).then_inc(sem("vt_set"), 1)
                    for n in range(17):
                        if n < 16:
                            w = WIN_N[n % 8]
                            act.wait_ge(sem("na_max"), n0 + n + 1)
                            act.activation(prob[n % 2][:, 0:w], sbias[n % 2][:, 0:w], ACT.Exp,
                                           bias=st_neg[:, n % 2:n % 2 + 1], accum_out=st_d[:, n % 2:n % 2 + 1]
                                           ).then_inc(sem("na_exp"), 1)
                            act.activation(prob[n % 2][:, w:w + CTX], bank2(2 * (n % 2))[:, w:w + CTX], ACT.Exp,
                                           bias=st_neg[:, n % 2:n % 2 + 1], accum_out=st_d2[:, n % 2:n % 2 + 1]
                                           ).then_inc(sem("na_exp"), 1)
                        if n >= 1:
                            w = WIN_N[(n - 1) % 8] + CTX
                            act.wait_ge(sem("na_turned"), n0 + n)
                            act.activation(probt[(n - 1) % 2][:, 0:w], bank2(4)[:, 0:w], ACT.Copy).then_inc(sem("probt_set"), 1)
            for k in range(4):
                act.wait_ge(sem("four_mir"), 4)
                src = four_y[:, k, :] if k < 2 else conv_out[:, k - 2, :]
                if k == 0:
                    act.wait_ge(sem("na_o"), 16 * PAIRS + 1)
                    act.wait_ge(sem("four_e"), 4)
                act.activation(mix_h[:, k, :], src, ACT.Copy).then_inc(sem("mix_high"), 1)
            for f in range(4):
                act.activation(mix_h[:, 4 + f, :], ao[:, f, :], ACT.Copy).then_inc(sem("mix_high"), 1)
            act.wait_ge(sem("mix_low"), KT)
            with act.Fori(0, KT // 2) as i:
                for s in range(2):
                    act.wait_ge(sem("slab_used"), i * 2 + s + 1)
                    act.activation(xt[:, i * 2 + s, :], bank2(4 + 2 * s), ACT.Copy).then_inc(sem("xt_set"), 1)
            act.wait_ge(up_evac, U_FF1 + 2)
            norm_scalar(act, "mlp", xt)
            modulate_scalar(act, "mlp", gs2, mod1[:, 24:32])

            def ff1_square(c, s, hid, wait_free):
                act.wait_ge(up_done, c * 2 + U_FF1 + s + 3)
                if wait_free:
                    act.wait_ge(sem("ff1_low"), c * 2 + s - 1)
                act.activation(sq[:, s, :], bank2(2 * s), ACT.Relu).then_inc(up_evac, 1)
                act.wait_ge(up_evac, c * 2 + U_FF1 + s + 3)
                act.activation(sq[:, s, :], sq[:, s, :], ACT.Square).then_inc(sem("ff1_sq"), 1)
                act.wait_ge(sem("ff1_sq"), c * 2 + s + 1)
                if wait_free:
                    act.wait_ge(dn_done, c * 16 - 15 + 16 * C_FF1)
                act.activation(hid_h[:, hid, s, :], sq[:, s, :], ACT.Copy).then_inc(sem("ff1_high"), 1)

            for s in range(2):
                ff1_square(0, s, 0, False)
            with act.Fori(0, (CH1 - 2) // 2) as j:
                for e in range(2):
                    for s in range(2):
                        ff1_square(j * 2 + 1 + e, s, 1 - e, True)
            for s in range(2):
                ff1_square(CH1 - 1, s, 1, True)
            act.wait_ge(dn_evac, 16 * CH1 + 2)
            norm_scalar(act, "final", xt)
            act.wait_ge(sem("x1_ready"), KT)
            norm_scalar(act, "mix2", xt)
            modulate_scalar(act, "mix2", gsm, mod2[:, 0:8])

            act.wait_ge(sem("sin_arg"), 1)
            act.activation(sin[:, :], ang[:, :], ACT.Sin).then_inc(sem("rot_tab"), 1)
            act.wait_ge(sem("cos_arg"), 1)
            act.activation(cos[:, :], turn[:, :], ACT.Sin).then_inc(sem("rot_tab"), 1)
            act.wait_ge(sem("x_moved"), 16)

            def out2(u, m, scale, slot):
                act.wait_ge(up_done, u + 3)
                act.activation(pt2[:, m, :], bank2(2 * slot), ACT.Copy, scale=scale).then_inc(up_evac, 1)

            for m in range(2):
                out2(U_WIN2 + m, m, 1.0, m)
            with act.Fori(1, 4) as i:
                for s in range(2):
                    out2(i * 2 + (U_WIN2 + s), i * 2 + s, SCALE, s)
            with act.Fori(4, W_IN2_TILES // 2) as i:
                for s in range(2):
                    out2(i * 2 + (U_WIN2 + s), i * 2 + s, 1.0, s)
            for n in range(GROUPS * TT // 4):
                act.wait_ge(sem("v2_turned"), n + 1)
                act.activation(v2[:, 4 * n:4 * n + 4, :], bank2(4 + 2 * (n % 2)).rearrange("p (t c) -> p t c", c=256), ACT.Copy
                               ).then_inc(sem("v2_set"), 1)
            for c in range(2):
                act.wait_ge(sem("pool_y"), c + 1)
                act.wait_ge(sem("pool_b"), 1)
                if c:
                    act.wait_ge(sem("mix2_split"), 1)
                act.activation(pout[:, :], bank2(2 * c), ACT.Identity, scale=vec("pool_scale_2", c),
                               bias=pbias[:, c:c + 1]).then_inc(sem("pout"), 1)
                act.wait_ge(sem("pout"), c + 1)
                act.activation(mix2_h[:, c, :], pout[:, :], ACT.Copy).then_inc(sem("mix2_high"), 1)
            for n in range(GROUPS * TT + 1):
                if n < GROUPS * TT:
                    w = keys2(n)
                    act.wait_ge(sem("d_max"), n + 1)
                    for h in range(GH):
                        act.activation(pr2[n % 2][:, h, 0:w], s2[n % 2][:, h, 0:w], ACT.Exp, bias=st2_neg[n % 2][:, h:h + 1],
                                       accum_out=st2_den[n % 4][:, h:h + 1]).then_inc(sem("d_exp"), 1)
                if n >= 1:
                    w = keys2(n - 1) // P * GH
                    act.wait_ge(sem("d_turned"), n)
                    act.activation(pt2t[(n - 1) % 2][:, 0:w, :], bank2(4)[:, 0:w * P].rearrange("p (k q) -> p k q", q=P),
                                   ACT.Copy).then_inc(sem("pt2_set"), 1)
            act.wait_ge(sem("c_diff"), 1)
            act.activation(cw[:, :, :, :], cw[:, :, :, :], ACT.Exp).then_inc(sem("c_exp"), 1)
            for c in range(2):
                act.wait_ge(sem("c_turned"), c + 1)
                act.activation(mix2_h[:, 2 + c, :], bank2(2 * c), ACT.Copy).then_inc(sem("mix2_high"), 1)
            with act.Fori(0, KT // 2) as i:
                for s in range(2):
                    act.wait_ge(up_done, i * 2 + (U_WO2 + 3 + s))
                    act.activation(y2[:, i * 2 + s, :], bank2(2 * s), ACT.Copy).then_inc(up_evac, 1)
            act.wait_ge(up_evac, U_FF2 + 2)
            norm_scalar(act, "post2", y2)
            act.wait_ge(sem("x2_ready"), KT)
            norm_scalar(act, "ffn2", xt)
            modulate_scalar(act, "ffn2", gsf, mod2[:, 24:32])

            def ff2_tile(c, i, hid, wait_free):
                u = c * 4 + U_FF2 + 2 * i
                f = c * 2 + i
                act.wait_ge(up_done, u + 3)
                act.activation(gbuf[:, i, :], bank2(0), ACT.Identity, scale=vec("conv_w_2", f + 44),
                               bias=vec("conv_b_2", f)).then_inc(sem("ff2_gate"), 1)
                act.wait_ge(up_evac, u + 3)
                act.activation(gelu[:, i, :], gbuf[:, i, :], ACT.Gelu_apprx_tanh).then_inc(sem("ff2_gelu"), 1)
                act.wait_ge(up_evac, u + 4)
                if wait_free:
                    act.wait_ge(dn_done, c * 16 - 15 + 16 * C_FF2)
                act.activation(hid_h[:, hid, i, :], gv[:, i, :], ACT.Copy).then_inc(sem("ff2_high"), 1)

            act.wait_ge(sem("x_moved"), 48)
            for i in range(2):
                ff2_tile(0, i, 0, False)
            with act.Fori(0, (CH2 - 1) // 2) as j:
                for e in range(2):
                    for i in range(2):
                        ff2_tile(j * 2 + 1 + e, i, 1 - e, True)
            act.wait_ge(dn_evac, 16 * (C_FF2 + CH2) + 2)
            norm_scalar(act, "out", y2)
            for t in range(TT):
                act.wait_ge(sem("o_turned"), t + 1)
                if t >= 2:
                    act.wait_ge(sem(f"stored{t % 2}"), 16 * (t // 2))
                act.activation(otok[:, t % 2, :], bank2(2 * (t % 2)), ACT.Copy).then_inc(sem("o_ready"), 1)

        @block.vector
        def _(dve):
            steps = 0

            def link(ins):
                nonlocal steps
                steps += 1
                ins.then_inc(sem("step"), 1)
                dve.wait_ge(sem("step"), steps)

            dve.wait_ge(sem("vec_turned"), 1)
            dve.tensor_copy(vcol[:, :], PS[:, 7, 0:VEC_TILES * P]).then_inc(sem("vec_set"), 1)
            dve.wait_ge(sem("silu"), 1)
            for b in range(2):
                for k in range(KT):
                    n = b * KT + k
                    dve.wait_ge(sem(f"ada_in{n % 2}"), 16 * (n // 2 + 1))
                    for v in range(2):
                        acc = ada_acc0[:, 2 * b + v, :]
                        c = silu_c[:, v * KT + k:v * KT + k + 1]
                        if k == 0:
                            ins = dve.tensor_scalar(acc, ada_ring0[:, n % 2, :], c, None, ALU.mult)
                        else:
                            dve.wait_ge(*((sem("ada_acc"), n) if v == 0 else (sem("ada_used"), n + 2)))
                            ins = dve.scalar_tensor_tensor(out=acc, in0=ada_ring0[:, n % 2, :], scalar=c, in1=acc,
                                                           op0=ALU.mult, op1=ALU.add)
                        ins.then_inc(sem("ada_acc") if v == 0 else sem("ada_used"), 1)
                    if n == 3:
                        dve.wait_ge(sem("root10"), 1)
                        dve.reciprocal(rstd10, root10).then_inc(sem("rstd10"), 1)
            dve.wait_ge(sem("ada_sum0"), 2)
            dve.tensor_tensor(mod1[:, 0:16], PS[:, 6, 0:16], vec("ada_b", 0, 16), ALU.add).then_inc(sem("mod1"), 1)
            dve.tensor_tensor(modc, PS[:, 6, 16:32], vec("ada_b", 0, 16), ALU.add).then_inc(sem("mod1"), 1)
            dve.wait_ge(sem("mod1"), 2)
            for g, m in ((gs1, mod1), (gsc, modc)):
                dve.scalar_tensor_tensor(out=g, in0=m[:, 8:16], scalar=1.0, in1=vec("norm1_g", 0, 8), op0=ALU.add,
                                         op1=ALU.mult).then_inc(sem("mod1"), 1)
            dve.wait_ge(sem("mod1"), 4)
            dve.wait_ge(sem("xs_set"), TT + CT)
            for k in range(KT + 1):
                if k < KT:
                    for lo, hi, g, m in ((0, SEQ, gs1, mod1), (SEQ, SEQ + CTX, gsc, modc)):
                        dve.tensor_scalar(xs[:, k, lo:hi], xs[:, k, lo:hi], g[:, k:k + 1], m[:, k:k + 1], ALU.mult,
                                          ALU.add).then_inc(sem("hn1"), 1)
                if k >= 1:
                    dve.wait_ge(sem("hn1_high"), k)
                    dve.tensor_tensor(hn1_l[:, k - 1, :], xs[:, k - 1, :], hn1_h[:, k - 1, :].bitcast(F32),
                                      ALU.subtract).then_inc(sem("hn1_low"), 1)
            dve.memset(vpad_edges(0), 0.0).then_inc(sem("padded"), 1)
            dve.memset(vpad_edges(1), 0.0).then_inc(sem("padded"), 1)
            dve.wait_ge(sem("padded"), 2)
            dve.wait_ge(sem("gate"), 1)
            for c in range(2):
                dve.tensor_tensor(vpad[:, c, PADT:PADT + SEQ], pt1[:, 2 + c, :], pt1[:, 4 + c, :], ALU.mult
                                  ).then_inc(sem("padded"), 1)
            dve.wait_ge(sem("padded"), 4)

            def tap(n, first=False):
                for c in range(2):
                    w = vec("conv_dw_w", n * 2 + c)
                    if first:
                        ins = dve.tensor_scalar(conv_acc[:, c, :], vpad[:, c, n:n + SEQ], w, vec("conv_dw_b", c),
                                                ALU.mult, ALU.add)
                    else:
                        dve.wait_ge(sem("taps"), n * 2 + c - 1)
                        ins = dve.scalar_tensor_tensor(out=conv_acc[:, c, :], in0=vpad[:, c, bass.ds(n, SEQ)], scalar=w,
                                                       in1=conv_acc[:, c, :], op0=ALU.mult, op1=ALU.add)
                    ins.then_inc(sem("taps"), 1)

            tap(0, True)
            tap(1)
            tap(2)
            with dve.Fori(0, 4) as i:
                for b in range(2):
                    for k in range(KT):
                        n = b * KT + k
                        dve.wait_ge(sem(f"ada1_in{k % 2}"), i * 128 + 16 * (n // 2 + 1))
                        c = silu_c[:, k:k + 1]
                        if k == 0:
                            ins = dve.tensor_scalar(ada_acc1[:, :], ada_ring1[:, 0, :], c, None, ALU.mult)
                        else:
                            dve.wait_ge(sem("ada1_used"), i * 16 + n + 2)
                            ins = dve.scalar_tensor_tensor(out=ada_acc1[:, :], in0=ada_ring1[:, k % 2, :], scalar=c,
                                                           in1=ada_acc1[:, :], op0=ALU.mult, op1=ALU.add)
                        ins.then_inc(sem("ada1_used"), 1)
                    for n in range(3 + 4 * b, 3 + min(4 * b + 4, 7)):
                        tap(i * 7 + n)
                    dve.wait_ge(sem("ada1_sum"), i * 2 + b + 1)
                    lo = i * 8 + (16 + 4 * b)
                    dve.tensor_tensor(mod1[:, bass.ds(lo, 4)], PS[:, 7, 4 * b:4 * b + 4],
                                      vec("ada_b", lo, 4), ALU.add).then_inc(sem("ada1_mod"), 1)
            dve.wait_ge(sem("ada1_mod"), 8)
            dve.scalar_tensor_tensor(out=gs2, in0=mod1[:, 32:40], scalar=1.0, in1=vec("norm2_g", 0, 8), op0=ALU.add,
                                     op1=ALU.mult).then_inc(sem("gmix"), 1)
            dve.wait_ge(sem("ln_sums"), 1)
            for c in range(2):
                dve.scalar_tensor_tensor(out=conv_acc[:, c, :], in0=bank2(0), scalar=-1.0 / 256, in1=conv_acc[:, c, :],
                                         op0=ALU.mult, op1=ALU.add).then_inc(sem("ln_d"), 1)
            dve.wait_ge(sem("ln_root"), 1)
            dve.reciprocal(ln_r[:, :], ln_r[:, :]).then_inc(sem("ln_rstd"), 1)
            dve.wait_ge(sem("ln_rstd"), 1)
            for c in range(2):
                dve.tensor_tensor(conv_acc[:, c, :], conv_acc[:, c, :], ln_r[:, :], ALU.mult).then_inc(sem("ln_y"), 1)
            for n in range(2):
                dve.wait_ge(sem("four_e"), 2 * n + 2)
                dve.wait_ge(sem("four_done"), 2 * n + 2)
                odd = PS[:, 7 - 2 * n, :]
                dve.tensor_tensor(four_y[:, n, 0:NYQ], four_e[n][:, :], odd, ALU.subtract).then_inc(sem("four_mir"), 1)
                dve.tensor_tensor(four_y[:, n, SEQ - 1:NYQ:-1], four_e[n][:, 1:NYQ], odd[:, 1:NYQ], ALU.add
                                  ).then_inc(sem("four_mir"), 1)
            with dve.Fori(0, PAIRS // 2) as i:
                for s in range(2):
                    n0 = i * 32 + 16 * s
                    dve.wait_ge(sem("bias_set"), i * 10 + 5 * s + 5)
                    for n in range(18):
                        if n < 16:
                            h, t = divmod(n, 8)
                            w = WIN_N[t]
                            e = n % 2
                            bias = tbm[s][:, h, :] if w == 640 else \
                                tb[s][:, h, (WIN_U[t] - 2 * t + 6) * GRID_W:(WIN_U[t] - 2 * t + 6) * GRID_W + w]
                            dve.wait_ge(sem("na_scored"), n0 + n + 1)
                            if n >= 2:
                                dve.wait_ge(sem("na_exp"), i * 64 + 32 * s + 2 * n - 2)
                            carry(dve)
                            scores = bank2(2 * e)
                            dve.tensor_tensor_reduce(sbias[e][:, 0:w], scores[:, 0:w], bias, 1.0, BIG, ALU.add, ALU.max,
                                                     st_m[:, e:e + 1]).then_inc(sem("na_biased"), 1)
                            dve.tensor_reduce(st_m2[:, e:e + 1], scores[:, w:w + CTX], AX.X, ALU.max).then_inc(sem("na_max2"), 1)
                            dve.wait_ge(sem("na_biased"), n0 + (n + 18))
                            dve.wait_ge(sem("na_max2"), n0 + n + 1)
                            dve.tensor_scalar(st_neg[:, e:e + 1], st_m[:, e:e + 1], st_m2[:, e:e + 1], -1.0, ALU.max,
                                              ALU.mult).then_inc(sem("na_max"), 1)
                            dve.wait_ge(sem("na_exp"), i * 64 + (32 * s + 2 * n + 2))
                            dve.tensor_tensor(st_r[:, e:e + 1], st_d[:, e:e + 1], st_d2[:, e:e + 1], ALU.add
                                              ).then_inc(sem("na_den"), 1)
                            dve.wait_ge(sem("na_den"), i * 64 + (32 * s + 2 * n + 1))
                            dve.reciprocal(st_rr[:, e:e + 1], st_r[:, e:e + 1]).then_inc(sem("na_den"), 1)
                            dve.wait_ge(sem("na_den"), i * 64 + (32 * s + 2 * n + 2))
                            dve.tensor_scalar(rdiag[e][:, :], ident, st_rr[:, e:e + 1], None, ALU.mult).then_inc(sem("na_diag"), 1)
                        if n >= 2:
                            h, t = divmod(n - 2, 8)
                            rows = slice(h * DH, (h + 1) * DH)
                            dve.wait_ge(sem("na_pv"), n0 + n - 1)
                            dve.tensor_copy(ao[rows, bass.ds(i * 2 + s, 1), t * P:(t + 1) * P], PS[rows, 6 + n % 2, 0:P].unsqueeze(1)
                                            ).then_inc(sem("na_o"), 1)
            for k in range(KT):
                dve.wait_ge(sem("mix_high"), k + 1)
                src = four_y[:, k, :] if k < 2 else conv_out[:, k - 2, :] if k < 4 else ao[:, k - 4, :]
                dve.tensor_tensor(mix_l[:, k, :], src, mix_h[:, k, :].bitcast(F32), ALU.subtract).then_inc(sem("mix_low"), 1)
            with dve.Fori(0, KT // 2) as i:
                for s in range(2):
                    dve.wait_ge(up_done, i * 2 + (U_WO1 + 3 + s))
                    dve.wait_ge(sem("xt_set"), i * 2 + s + 1)
                    dve.scalar_tensor_tensor(out=xt[:, i * 2 + s, :], in0=bank2(2 * s), scalar=mod1[:, bass.ds(i * 2 + (16 + s), 1)],
                                             in1=xt[:, i * 2 + s, :], op0=ALU.mult, op1=ALU.add).then_inc(up_evac, 1)
            norm_vector(dve, "mlp")
            modulate_vector(dve, "mlp", xt)

            def ada2_sum(b):
                dve.wait_ge(sem("ada2_in"), b * 16 + 16)
                for k in range(KT):
                    c = silu_c[:, 16 + k:17 + k]
                    if k == 0:
                        ins = dve.tensor_scalar(ada_acc2[:, :], ada_in2[:, 0, :], c, None, ALU.mult)
                    else:
                        dve.wait_ge(sem("ada2_used"), b * KT + (k + 2))
                        ins = dve.scalar_tensor_tensor(out=ada_acc2[:, :], in0=ada_in2[:, k, :], scalar=c,
                                                       in1=ada_acc2[:, :], op0=ALU.mult, op1=ALU.add)
                    ins.then_inc(sem("ada2_used"), 1)

            def ada2_mod(b):
                dve.wait_ge(sem("ada2_sum"), b + 1)
                n = ADA2 // P
                dve.tensor_tensor(mod2[:, bass.ds(b * n, n)], PS[:, 6, 0:n], vec("b_ada_2", b * n, n), ALU.add
                                  ).then_inc(sem("mod2"), 1)

            def ff1_lowhalf(c, s, hid):
                dve.wait_ge(sem("ff1_high"), c * 2 + s + 1)
                dve.tensor_tensor(hid_l[:, hid, s, :], sq[:, s, :], hid_h[:, hid, s, :].bitcast(F32), ALU.subtract
                                  ).then_inc(sem("ff1_low"), 1)

            def ff1_add(c, lo, hi):
                for n in range(lo, hi):
                    m, j = divmod(n, 2)
                    part = xt[:, m, j * HALF:(j + 1) * HALF]
                    dve.wait_ge(dn_done, c * 16 + (16 * C_FF1 + n + 2))
                    dve.scalar_tensor_tensor(out=part, in0=PS[:, 4 + n % 2, :], scalar=mod1[:, 40 + m:41 + m], in1=part,
                                             op0=ALU.mult, op1=ALU.add).then_inc(dn_evac, 1)

            def ff1_step(c, prev, hid):
                ff1_lowhalf(c, 0, hid)
                ff1_lowhalf(c, 1, hid)
                ada2_mod(prev)
                ff1_add(prev, 0, 16)
                ada2_sum(c)

            ada2_sum(0)
            for s in range(2):
                ff1_lowhalf(0, s, 0)
            with dve.Fori(0, (CH1 - 2) // 2) as j:
                for e in range(2):
                    ff1_step(j * 2 + 1 + e, j * 2 + e, 1 - e)
            ff1_step(CH1 - 1, CH1 - 2, 1)
            ada2_mod(CH1 - 1)
            ff1_add(CH1 - 1, 0, 16)
            dve.wait_ge(sem("mod2"), CH1 + 1)
            for g, w, c, op in ((gsm, "g_pre_mix_2", 8, ALU.add), (ggm, "g_post_mix_2", 16, ALU.mult),
                                (gsf, "g_pre_ffn_2", 32, ALU.add), (ggf, "g_post_ffn_2", 40, ALU.mult)):
                dve.scalar_tensor_tensor(out=g, in0=mod2[:, c:c + 8], scalar=1.0, in1=vec(w, 0, 8), op0=op, op1=ALU.mult
                                         ).then_inc(sem("gmix"), 1)
            dve.wait_ge(sem("gmix"), 5)
            norm_vector(dve, "final")
            for k in range(KT):
                dve.scalar_tensor_tensor(out=xt[:, k, :], in0=xt[:, k, :], scalar=vec("final_norm_g", k), in1=bank2(0),
                                         op0=ALU.mult, op1=ALU.mult).then_inc(sem("x1_ready"), 1)
            norm_vector(dve, "mix2")
            modulate_vector(dve, "mix2", xt)
            dve.wait_ge(sem("pos_in"), 16)
            for part, shift in (("sin", 0.0), ("cos", 0.25)):
                out_arg = ang if part == "sin" else turn
                if part == "cos":
                    dve.wait_ge(sem("rot_tab"), 1)
                link(dve.tensor_copy(ang[:, :], pos[:, :]))
                link(dve.tensor_scalar(ang[:, :], ang[:, :], const("inv_freq"), None, ALU.mult))
                link(dve.tensor_scalar(turn[:, :], ang[:, :], 1.0 / (2 * math.pi), shift, ALU.mult, ALU.add))
                link(dve.tensor_copy(turn_i[:, :], turn[:, :]))
                link(dve.tensor_copy(turn[:, :], turn_i[:, :]))
                for step in two_pi_parts():
                    link(dve.scalar_tensor_tensor(out=ang[:, :], in0=turn[:, :], scalar=-step, in1=ang[:, :], op0=ALU.mult,
                                                  op1=ALU.add))
                if part == "cos":
                    link(dve.tensor_scalar(ang[:, :], ang[:, :], math.pi / 2, None, ALU.add))
                lim = float(np.nextafter(np.float32(math.pi), np.float32(0)))
                dve.tensor_scalar(out_arg[:, :], ang[:, :], lim, -lim, ALU.min, ALU.max).then_inc(sem(part + "_arg"), 1)

            dve.wait_ge(up_evac, U_WIN2 + W_IN2_TILES + 2)
            dve.wait_ge(sem("rot_tab"), 2)
            for m in range(12):
                src = pt2[:, Q2 + m, :]
                dve.tensor_tensor(rt[m % 2][:, :], src, cos[:, :], ALU.mult).then_inc(sem("rot_c"), 1)
                dve.wait_ge(sem("rotated"), m + 1)
                dve.tensor_tensor(rt2[m % 2][:, :], bank2(2 * (m % 2)), sin[:, :], ALU.mult).then_inc(sem("rot_s"), 1)
                dve.wait_ge(sem("rot_s"), m + 1)
                dve.wait_ge(sem("rot_c"), m + 1)
                g = m % 6 // 2
                if g == 0:
                    dst = [qk2[:, m, :]]
                    s0, s1 = [rt[m % 2][:, :]], [rt2[m % 2][:, :]]
                elif g == 1:
                    dst = [qk2[:, m, n * HALF:(n + 1) * HALF].rearrange("p (r i) -> p r i", r=4) for n in range(2)]
                    s0, s1 = ([x[:, n * HALF:(n + 1) * HALF].rearrange("p (i r) -> p r i", r=4) for n in range(2)]
                              for x in (rt[m % 2], rt2[m % 2]))
                else:
                    dst = [qk2[:, m, :].rearrange("p (r k) -> p r k", r=8)]
                    s0, s1 = ([x[:, :].rearrange("p (k r) -> p r k", r=8)] for x in (rt[m % 2], rt2[m % 2]))
                for d, x, y in zip(dst, s0, s1):
                    ins = dve.tensor_tensor(d, x, y, ALU.add)
                    ins.then_inc(sem("qk2_set"), 1)
            dve.tensor_tensor(pbias, vec("b_pool_2", 0, 2), vec("pool_scale_2", 0, 2), ALU.mult).then_inc(sem("pool_b"), 1)
            for c in range(2):
                u = pt2[:, c, :]
                bufs = [ps2, ps4]
                src, lo, lag = u, 0, 1
                for n in range(2 if c == 0 else 4):
                    dst = bufs[n % 2]
                    if c == 0 and n == 1 or c == 1 and n == 3:
                        lo = 64
                        old = bufs[(n - 1) % 2]
                        link(dve.tensor_copy(dst[0:64, :], old[0:64, :]))
                    link(dve.tensor_copy(dst[lo:, 0:lag], src[lo:, 0:lag]))
                    link(dve.tensor_tensor(dst[lo:, lag:], src[lo:, lag:], src[lo:, 0:SEQ - lag], ALU.add))
                    src, lag = dst, 2 * lag
                head = const("pool_head")[:, 16 * c:16 * c + 16]
                link(dve.scalar_tensor_tensor(out=pmix[:, c, :], in0=src[:, :], scalar=const("pool_inv")[:, c:c + 1], in1=u,
                                               op0=ALU.mult, op1=ALU.subtract))
                link(dve.tensor_tensor(pmix[:, c, 0:16], src[:, 0:16], head, ALU.mult))
                dve.tensor_tensor(pmix[:, c, 0:16], pmix[:, c, 0:16], u[:, 0:16], ALU.subtract).then_inc(sem("pmix"), 1)
            for c in range(2):
                dve.wait_ge(sem("mix2_high"), c + 1)
                dve.tensor_tensor(mix2_l[:, c, :], pout[:, :], mix2_h[:, c, :].bitcast(F32), ALU.subtract
                                  ).then_inc(sem("mix2_split"), 1)
            for n in range(GROUPS * TT + 2):
                e = n % 2
                if n < GROUPS * TT:
                    w = keys2(n)
                    mask = const("causal16") if n >= 2 * TT else const("causal")[:, 256 - w:]
                    dve.wait_ge(sem("d_scored"), n + 1)
                    if n >= 2:
                        dve.wait_ge(sem("d_exp"), 4 * n - 4)
                    if n >= 4:
                        dve.wait_ge(sem(f"o2_out{n % 4}"), 16 * (n // 4))
                    sc = bank2(2 * e).rearrange("p (h k) -> p h k", h=GH)[:, :, 0:w]
                    dve.tensor_tensor(s2[e][:, :, 0:w], sc, mask.unsqueeze(1).to_broadcast([P, GH, w]), ALU.add
                                      ).then_inc(sem("d_masked"), 1)
                    dve.wait_ge(sem("d_masked"), n + 1)
                    dve.tensor_reduce(og[n % 4][:, GH * DH:GH * DH + GH], s2[e][:, :, 0:w], AX.X, ALU.max).then_inc(sem("d_mx"), 1)
                    dve.wait_ge(sem("d_mx"), n + 1)
                    dve.tensor_scalar(st2_neg[e], og[n % 4][:, GH * DH:GH * DH + GH], -1.0, None, ALU.mult).then_inc(sem("d_max"), 1)
                if n >= 2:
                    j = n - 2
                    dve.wait_ge(sem("d_pv"), j + 1)
                    dve.tensor_copy(og[j % 4][:, 0:GH * DH], PS[:, 6 + j % 2, 0:GH * DH]).then_inc(sem("o2_ready"), 1)
            dve.wait_ge(sem("oall_in"), 16 * GROUPS)
            mx = [oall[:, :, g, GH * DH:GH * DH + GH] for g in range(GROUPS)]
            dn = [oall[:, :, g, GH * DH + GH:] for g in range(GROUPS)]
            link(dve.tensor_tensor(cmax[:, :, :], mx[0], mx[1], ALU.max))
            link(dve.tensor_tensor(cmax[:, :, :], cmax[:, :, :], mx[2], ALU.max))
            for g in range(2):
                link(dve.tensor_tensor(cw[:, :, g, :], mx[g], cmax[:, :, :], ALU.subtract))
            dve.tensor_tensor(cw[:, :, 2, :], mx[2], cmax[:, :, :], ALU.subtract).then_inc(sem("c_diff"), 1)
            dve.wait_ge(sem("c_exp"), 1)
            link(dve.tensor_tensor(cden[:, :, :], cw[:, :, 0, :], dn[0], ALU.mult))
            for g in range(1, GROUPS):
                link(dve.tensor_tensor(cmax[:, :, :], cw[:, :, g, :], dn[g], ALU.mult))
                link(dve.tensor_tensor(cden[:, :, :], cden[:, :, :], cmax[:, :, :], ALU.add))
            link(dve.reciprocal(cden[:, :, :], cden[:, :, :]))
            for g in range(GROUPS):
                link(dve.tensor_tensor(cwn[:, :, g, :].rearrange("p t (a b) -> p t b a", b=2),
                                       cw[:, :, g, :].rearrange("p t (b a) -> p t b a", a=2),
                                       cden[:, :, :].rearrange("p t (b a) -> p t b a", a=2), ALU.mult))
            for t in range(TT):
                for g in range(GROUPS):
                    src = oall[:, t, g, 0:GH * DH].rearrange("p (h d) -> p h d", d=DH)
                    wt = cwn[:, t, g, :].unsqueeze(2).to_broadcast([P, GH, DH])
                    if g == 0:
                        link(dve.tensor_tensor(csum[:, t, :, :], src, wt, ALU.mult))
                    else:
                        link(dve.tensor_tensor(cterm[:, t, :, :], src, wt, ALU.mult))
                        ins = dve.tensor_tensor(csum[:, t, :, :], csum[:, t, :, :], cterm[:, t, :, :], ALU.add)
                        if g == 2:
                            ins.then_inc(sem("c_sum"), 1)
                        else:
                            link(ins)
            for c in range(2):
                dve.wait_ge(sem("mix2_high"), 3 + c)
                dve.tensor_tensor(mix2_l[:, 2 + c, :], bank2(2 * c), mix2_h[:, 2 + c, :].bitcast(F32), ALU.subtract
                                  ).then_inc(sem("mix2_split"), 1)
            norm_vector(dve, "post2")
            dve.wait_ge(sem("x_moved"), 32)
            for k in range(KT):
                dve.scalar_tensor_tensor(out=y2[:, k, :], in0=y2[:, k, :], scalar=ggm[:, k:k + 1], in1=bank2(0), op0=ALU.mult,
                                         op1=ALU.mult).then_inc(sem("y_gated"), 1)
                dve.wait_ge(sem("y_gated"), k + 1)
                dve.tensor_tensor(xt[:, k, :], xt[:, k, :], y2[:, k, :], ALU.add).then_inc(sem("x2_ready"), 1)
            norm_vector(dve, "ffn2")
            modulate_vector(dve, "ffn2", xt)
            dve.memset(y2[:, :, :], 0.0).then_inc(sem("y2_zero"), 1)
            dve.wait_ge(sem("y2_zero"), 1)

            def ff2_gate(c, i):
                u = c * 4 + U_FF2 + 2 * i
                f = c * 2 + i
                dve.wait_ge(sem("ff2_gate"), f + 1)
                dve.scalar_tensor_tensor(out=gbuf[:, i, 1:], in0=bank2(0)[:, 0:SEQ - 1], scalar=vec("conv_w_2", f + 22),
                                         in1=gbuf[:, i, 1:], op0=ALU.mult, op1=ALU.add).then_inc(sem("ff2_tap"), 1)
                dve.wait_ge(sem("ff2_tap"), f + 1)
                dve.scalar_tensor_tensor(out=gbuf[:, i, 2:], in0=bank2(0)[:, 0:SEQ - 2], scalar=vec("conv_w_2", f),
                                         in1=gbuf[:, i, 2:], op0=ALU.mult, op1=ALU.add).then_inc(up_evac, 1)

            def ff2_value(c, i):
                u = c * 4 + U_FF2 + 2 * i + 1
                dve.wait_ge(sem("ff2_gelu"), c * 2 + i + 1)
                dve.wait_ge(up_done, u + 3)
                dve.tensor_tensor(gv[:, i, :], gelu[:, i, :], bank2(2), ALU.mult).then_inc(up_evac, 1)

            def ff2_lowhalf(c, i, hid):
                dve.wait_ge(sem("ff2_high"), c * 2 + i + 1)
                dve.tensor_tensor(hid_l[:, hid, i, :], gv[:, i, :], hid_h[:, hid, i, :].bitcast(F32), ALU.subtract
                                  ).then_inc(sem("ff2_low"), 1)

            def ff2_add(c, lo, hi):
                for n in range(lo, hi):
                    m, j = divmod(n, 2)
                    part = y2[:, m, j * HALF:(j + 1) * HALF]
                    dve.wait_ge(dn_done, c * 16 + (16 * C_FF2 + n + 2))
                    dve.tensor_tensor(part, part, PS[:, 4 + n % 2, :], ALU.add).then_inc(dn_evac, 1)

            for i in range(2):
                ff2_gate(0, i)
                ff2_value(0, i)
                ff2_lowhalf(0, i, 0)
            with dve.Fori(0, (CH2 - 1) // 2) as j:
                for e in range(2):
                    c = j * 2 + 1 + e
                    ff2_gate(c, 0)
                    ff2_value(c, 0)
                    ff2_lowhalf(c, 0, 1 - e)
                    ff2_gate(c, 1)
                    ff2_value(c, 1)
                    ff2_add(j * 2 + e, 0, 4)
                    ff2_lowhalf(c, 1, 1 - e)
                    ff2_add(j * 2 + e, 4, 16)
            ff2_add(CH2 - 1, 0, 16)
            norm_vector(dve, "out")
            dve.wait_ge(sem("x_moved"), 64)
            for k in range(KT):
                dve.scalar_tensor_tensor(out=y2[:, k, :], in0=y2[:, k, :], scalar=ggf[:, k:k + 1], in1=bank2(0), op0=ALU.mult,
                                         op1=ALU.mult).then_inc(sem("y_gated"), 1)
                dve.wait_ge(sem("y_gated"), KT + k + 1)
                dve.tensor_tensor(xt[:, k, :], xt[:, k, :], y2[:, k, :], ALU.add).then_inc(sem("x3_ready"), 1)

        @block.tensor
        def _(pe):
            pe.wait_ge(sem("tables_in"), 32)
            for t in range(VEC_TILES):
                mm = pe.transpose(PS[:, 7, t * P:(t + 1) * P], vrow[:, t, :], ident)
            mm.then_inc(sem("vec_turned"), 1)
            for t in range(TT + CT):
                pe.wait_ge(sem("x_scaled"), t + 1)
                if t >= 2:
                    pe.wait_ge(sem("xs_set"), t - 1)
                for k in range(KT):
                    mm = pe.transpose(bank2(2 * (t % 2))[:, k * P:(k + 1) * P], xtok[:, t, k * P:(k + 1) * P], ident)
                mm.then_inc(sem("x_turned"), 1)
            pe.wait_ge(sem("ones_set"), 3)
            for b in range(2):
                pe.wait_ge(sem("ada_acc"), KT * (b + 1))
                pe.wait_ge(sem("ada_used"), 2 + KT * (b + 1))
                for v in range(2):
                    for f in range(KT):
                        col = v * 16 + b * 8 + f
                        mm = pe.matmul(PS[:, 6, col:col + 1], ada_acc0[:, 2 * b + v, f * P:(f + 1) * P], ones[:, 0:1],
                                       start=True, stop=True)
                mm.then_inc(sem("ada_sum0"), 1)
            pe.wait_ge(sem("hn1_low"), KT)
            with pe.Fori(0, K0 // 2) as i:
                for s in range(2):
                    mul_up(pe, i * 2 + s, s, hn1_h, hn1_l)
            with pe.Fori(0, 4) as i:
                for s in range(2):
                    mul_up(pe, i * 2 + (K0 + s), s, hn1_h, hn1_l, extra=CTX)
                    pe.wait_ge(sem("ada1_used"), i * 16 + (2 + KT * (s + 1)))
                    for f in range(4):
                        mm = pe.matmul(PS[:, 7, 4 * s + f:4 * s + f + 1], ada_acc1[:, f * P:(f + 1) * P], ones[:, 0:1],
                                       start=True, stop=True)
                    mm.then_inc(sem("ada1_sum"), 1)
            pe.wait_ge(sem("four_in"), 32)
            pe.wait_ge(sem("ada1_mod"), 8)
            for c in range(2):
                pe.matmul(PS[:, 6 + c, 0:256], const("dft_c"), wf[:, c, :], start=True, stop=True)
                pe.matmul(PS[:, 6 + c, 256:512], const("dft_s"), wf[:, c, :], start=True, stop=True
                          ).then_inc(sem("four_w"), 1)
            pe.wait_ge(sem("four_ab"), 2)
            pe.wait_ge(up_evac, W_IN_TILES + 2)
            for t in range(TT):
                if t >= 2:
                    pe.wait_ge(sem("zf_set"), t - 1)
                for c in range(2):
                    mm = pe.matmul(PS[:, 4 + t % 2, :], pt1[:, c, t * P:(t + 1) * P], four_ab[:, c, :],
                                   start=(c == 0), stop=(c == 1))
                mm.then_inc(sem("four_z"), 1)
            pe.wait_ge(sem("taps"), 2 * TAPS)
            for j in range(2):
                for c in range(2):
                    mm = pe.matmul(PS[:, j, :], ones[:, :], conv_acc[:, c, j * HALF:(j + 1) * HALF],
                                   start=(c == 0), stop=(c == 1))
            mm.then_inc(sem("ln_sums"), 1)
            pe.wait_ge(sem("ln_sq"), 2)
            for j in range(2):
                for c in range(2):
                    mm = pe.matmul(PS[:, 2 + j, :], ones[:, :], conv_sq[:, c, j * HALF:(j + 1) * HALF],
                                   start=(c == 0), stop=(c == 1))
            mm.then_inc(sem("ln_sums"), 1)
            pe.wait_ge(sem("zf_set"), TT)
            pe.wait_ge(sem("ln_d"), 2)
            for nt in range(2):
                even, odd = PS[:, 6 - 2 * nt, :], PS[:, 7 - 2 * nt, :]
                for tt in range(TT):
                    pe.matmul(even, zf[:, tt, nt * P:(nt + 1) * P], dseq[:, tt, 0:NYQ], start=(tt == 0), stop=(tt == TT - 1))
                for tt in range(TT):
                    mm = pe.matmul(PS[:, nt, 0:1], zf[:, tt, nt * P:(nt + 1) * P], dseq[:, tt, NYQ:NYQ + 1],
                                   start=(tt == 0), stop=(tt == TT - 1))
                mm.then_inc(sem("four_done"), 1)
                for tt in range(TT):
                    mm = pe.matmul(odd, zf[:, tt, 256 + nt * P:256 + (nt + 1) * P], dseq[:, tt, NYQ + 1:],
                                   start=(tt == 0), stop=(tt == TT - 1))
                mm.then_inc(sem("four_done"), 1)
            pe.wait_ge(sem("point_in"), 16)
            pe.wait_ge(sem("conv_s"), 2)
            pe.wait_ge(sem("four_e"), 4)
            for m in range(2):
                for j in range(2):
                    for c in range(2):
                        mm = pe.matmul(PS[:, 2 * m + j, :], pw[:, c, m * P:(m + 1) * P], conv_acc[:, c, j * HALF:(j + 1) * HALF],
                                       start=(c == 0), stop=(c == 1))
                mm.then_inc(sem("conv_pw"), 1)

            pe.wait_ge(sem("conv_done"), 2)
            pe.wait_ge(sem("four_mir"), 4)
            with pe.Fori(0, PAIRS // 2) as i:
                for s in range(2):
                    n0 = i * 32 + 16 * s

                    def scores(n):
                        h, t = divmod(n, 8)
                        w, k0 = WIN_N[t], WIN_U[t] * GRID_W
                        rows = slice(h * DH, (h + 1) * DH)
                        dst = bank2(2 * (n % 2))
                        q = qs[s][rows, t * P:(t + 1) * P]
                        if n >= 2:
                            pe.wait_ge(sem("na_exp"), n0 * 2 + (2 * n - 2))
                        spans = [(0, min(w, HALF), k0), (HALF, w, k0 + HALF), (w, w + CTX, SEQ)]
                        for lo, hi, k in spans:
                            if hi > lo:
                                mm = pe.matmul(dst[:, lo:hi], q, ks[s][rows, k:k + hi - lo], start=True, stop=True)
                        mm.then_inc(sem("na_scored"), 1)

                    def turned(n):
                        pe.wait_ge(sem("na_diag"), n0 + (n + 1))
                        if n:
                            pe.wait_ge(sem("probt_set"), n0 + (n + 1))
                        for c in range((WIN_N[n % 8] + CTX) // P):
                            mm = pe.matmul(bank2(4)[:, c * P:(c + 1) * P], prob[n % 2][:, c * P:(c + 1) * P], rdiag[n % 2][:, :],
                                           start=True, stop=True)
                        mm.then_inc(sem("na_turned"), 1)

                    def values(n):
                        h, t = divmod(n, 8)
                        pe.wait_ge(sem("probt_set"), n0 + (n + 2))
                        if n >= 2:
                            pe.wait_ge(sem("na_o"), n0 + n)
                        tiles = [WIN_U[t] // 2 + c for c in range(WIN_N[t] // P)] + [TT, TT + 1]
                        for c, kt in enumerate(tiles):
                            mm = pe.matmul(PS[h * DH:(h + 1) * DH, 6 + n % 2, 0:P], vt[s][:, kt, h * DH:(h + 1) * DH],
                                           probt[n % 2][:, c * P:(c + 1) * P], start=(c == 0), stop=(c == len(tiles) - 1))
                        mm.then_inc(sem("na_pv"), 1)

                    pe.wait_ge(sem("na_o"), n0 + 1)
                    pe.wait_ge(sem("probt_set"), n0 + 1)
                    pe.wait_ge(sem("staged"), i * 10 + (5 * s + 5))
                    for t in range(TT):
                        mm = pe.transpose(bank2(4)[:, t * P:(t + 1) * P], vs[:, t * P:(t + 1) * P], ident)
                    mm.then_inc(sem("v_turned"), 1)
                    pe.wait_ge(sem("vt_set"), i * 4 + (2 * s + 1))
                    for t in range(CT):
                        mm = pe.transpose(bank2(4)[:, t * P:(t + 1) * P], vs[:, SEQ + t * P:SEQ + (t + 1) * P], ident)
                    mm.then_inc(sem("v_turned"), 1)
                    scores(0)
                    pe.wait_ge(sem("vt_set"), i * 4 + (2 * s + 2))
                    for n in range(16):
                        if n < 15:
                            scores(n + 1)
                        turned(n)
                        if n:
                            values(n - 1)
                    values(15)
            pe.wait_ge(sem("mix_low"), KT)
            with pe.Fori(0, KT // 2) as i:
                for s in range(2):
                    mul_up(pe, i * 2 + (U_WO1 + s), s, mix_h, mix_l)
                    pe.wait_ge(sem(f"slab_in{s}"), i * 16 + 16)
                    for t in range(TT):
                        mm = pe.transpose(bank2(4 + 2 * s)[:, t * P:(t + 1) * P], xslab[:, s, t, :], ident)
                    mm.then_inc(sem("slab_used"), 1)
            norm_tensor(pe, "mlp")
            pe.wait_ge(nsem["low"], KT)

            def ff1_up(c):
                for s in range(2):
                    mul_up(pe, c * 2 + (U_FF1 + s), s, hn_h, hn_l)

            def ff1_dn(c, hid):
                pe.wait_ge(sem("ff1_low"), c * 2 + 2)
                mul_dn(pe, c * 2 + 2 * C_FF1, hid, c * 16 + 16 * C_FF1)

            def ada2_reduce(b):
                pe.wait_ge(sem("ada2_used"), b * KT + (2 + KT))
                pe.wait_ge(sem("mod2"), b + 1)
                for f in range(ADA2 // P):
                    mm = pe.matmul(PS[:, 6, f:f + 1], ada_acc2[:, f * P:(f + 1) * P], ones[:, 0:1], start=True, stop=True)
                mm.then_inc(sem("ada2_sum"), 1)

            ff1_up(0)
            with pe.Fori(0, (CH1 - 2) // 2) as j:
                for e in range(2):
                    ff1_up(j * 2 + 1 + e)
                    ada2_reduce(j * 2 + e)
                    ff1_dn(j * 2 + e, e)
            ff1_up(CH1 - 1)
            ada2_reduce(CH1 - 2)
            ff1_dn(CH1 - 2, 0)
            ada2_reduce(CH1 - 1)
            ff1_dn(CH1 - 1, 1)
            norm_tensor(pe, "final")
            norm_tensor(pe, "mix2")
            pe.wait_ge(nsem["low"], 2 * KT)
            with pe.Fori(0, W_IN2_TILES // 2) as i:
                for s in range(2):
                    mul_up(pe, i * 2 + (U_WIN2 + s), s, hn_h, hn_l)
            pe.wait_ge(up_evac, U_WIN2 + W_IN2_TILES + 2)
            for m in range(12):
                if m >= 2:
                    pe.wait_ge(sem("rot_s"), m - 1)
                for j in range(2):
                    mm = pe.matmul(PS[:, 2 * (m % 2) + j, :], const("rotate"), pt2[:, Q2 + m, j * HALF:(j + 1) * HALF],
                                   start=True, stop=True)
                mm.then_inc(sem("rotated"), 1)
                if m % 2:
                    n = m // 2
                    if n >= 2:
                        pe.wait_ge(sem("v2_set"), n - 1)
                    for gb in range(4 * n, 4 * n + 4):
                        g, b = divmod(gb, TT)
                        for hp in range(2):
                            lo = gb % 4 * 256 + hp * P
                            mm = pe.transpose(bank2(4 + 2 * (n % 2))[:, lo:lo + P], perm(pt2[:, V2 + 2 * g + hp, :], g, b), ident)
                    mm.then_inc(sem("v2_turned"), 1)
            pe.wait_ge(sem("point_in"), 32)
            for c in range(2):
                pe.wait_ge(sem("pmix"), c + 1)
                for j in range(2):
                    mm = pe.matmul(PS[:, 2 * c + j, :], wp[:, c, :], pmix[:, c, j * HALF:(j + 1) * HALF], start=True, stop=True)
                mm.then_inc(sem("pool_y"), 1)

            pe.wait_ge(sem("qk2_set"), 16)
            pe.wait_ge(sem("v2_set"), GROUPS * TT // 4)
            pe.wait_ge(sem("pout"), 2)

            def d_blocks(n):
                g, b = divmod(n, TT)
                return [b - (1 if g == 0 else 4), b] if keys2(n) == 256 else [b]

            def d_scores(n):
                g, b = divmod(n, TT)
                if n >= 2:
                    pe.wait_ge(sem("d_masked"), n - 1)
                for j, h in enumerate(HEAD_AT):
                    rows = slice(DH * (h % 2), DH * (h % 2) + DH)
                    q = qk2[rows, 2 * g + h // 2, b * P:(b + 1) * P]
                    for c, kb in enumerate(d_blocks(n)):
                        lo = j * 256 + c * P
                        mm = pe.matmul(bank2(2 * (n % 2))[:, lo:lo + P], q, qk2[rows, 6 + 2 * g + h // 2, kb * P:(kb + 1) * P],
                                       start=True, stop=True)
                mm.then_inc(sem("d_scored"), 1)

            def d_turned(n):
                nk = keys2(n) // P
                pe.wait_ge(sem("d_exp"), GH * (n + 1))
                if n:
                    pe.wait_ge(sem("pt2_set"), n)
                for j in range(GH):
                    for c in range(nk):
                        lo = (j * nk + c) * P
                        mm = pe.matmul(bank2(4)[:, lo:lo + P], pr2[n % 2][:, j, c * P:(c + 1) * P], ident, start=True, stop=True)
                mm.then_inc(sem("d_turned"), 1)

            def d_values(n):
                g, b = divmod(n, TT)
                blocks = d_blocks(n)
                pe.wait_ge(sem("pt2_set"), n + 1)
                if n >= 2:
                    pe.wait_ge(sem("o2_ready"), n - 1)
                for j, h in enumerate(HEAD_AT):
                    for c, kb in enumerate(blocks):
                        mm = pe.matmul(PS[:, 6 + n % 2, h * DH:(h + 1) * DH], pt2t[n % 2][:, j * len(blocks) + c, :],
                                       v2[:, g * TT + kb, h * DH:(h + 1) * DH], start=(c == 0), stop=(c == len(blocks) - 1))
                mm.then_inc(sem("d_pv"), 1)

            d_scores(0)
            for n in range(GROUPS * TT):
                if n + 1 < GROUPS * TT:
                    d_scores(n + 1)
                d_turned(n)
                if n:
                    d_values(n - 1)
            d_values(GROUPS * TT - 1)
            pe.wait_ge(sem("c_sum"), TT)
            for c in range(2):
                for t in range(TT):
                    mm = pe.transpose(bank2(2 * c)[:, t * P:(t + 1) * P], csum[:, t, 2 * c:2 * c + 2, :].rearrange("p h d -> p (h d)"), ident)
                mm.then_inc(sem("c_turned"), 1)
            pe.wait_ge(sem("mix2_split"), 4)
            with pe.Fori(0, KT // 2) as i:
                for s in range(2):
                    mul_up(pe, i * 2 + (U_WO2 + s), s, mix2_h, mix2_l, kt=4)
            norm_tensor(pe, "post2")
            norm_tensor(pe, "ffn2")
            pe.wait_ge(nsem["low"], 3 * KT)

            def ff2_up(c):
                for i in range(4):
                    mul_up(pe, c * 4 + (U_FF2 + i), i % 2, hn_h, hn_l)

            def ff2_dn(c, hid):
                pe.wait_ge(sem("ff2_low"), c * 2 + 2)
                mul_dn(pe, c * 2 + 2 * C_FF2, hid, c * 16 + 16 * C_FF2)

            ff2_up(0)
            with pe.Fori(0, (CH2 - 1) // 2) as j:
                ff2_up(j * 2 + 1)
                ff2_dn(j * 2, 0)
                ff2_up(j * 2 + 2)
                ff2_dn(j * 2 + 1, 1)
            ff2_dn(CH2 - 1, 0)
            norm_tensor(pe, "out")
            pe.wait_ge(sem("x3_ready"), KT)
            for t in range(TT):
                if t >= 2:
                    pe.wait_ge(sem("o_ready"), t - 1)
                for k in range(KT):
                    mm = pe.transpose(bank2(2 * (t % 2))[:, k * P:(k + 1) * P], xt[:, k, t * P:(t + 1) * P], ident)
                mm.then_inc(sem("o_turned"), 1)


_INS = ["x", "ctx", "ada_w", "w_in", "w_fourier", "conv_pw_w", "w_out", "mlp_w1", "mlp_w2", "w_ada_2", "w_in_2",
        "w_out_2", "w_up_2", "w_down_2"]


def kernel(**inputs):
    import concourse.bacc as bacc
    from concourse.bass_utils import run_bass_kernel_spmd

    arr = {n: np.asarray(v) for n, v in inputs.items()}
    data = {n: np.ascontiguousarray(arr[n].reshape(arr[n].shape[-2:])) for n in _INS}
    data["positions_2"] = np.ascontiguousarray(arr["positions_2"].reshape(1, SEQ))
    vecs = np.zeros((VEC_TILES * P, P), np.float32)
    for name, rows in VECS:
        vecs[VROW[name]:VROW[name] + rows] = arr[name].reshape(rows, P)
    data["vecs"] = vecs
    rpb = np.zeros(2 * RPB_PAD + arr["na_rpb"].size, np.float32)
    rpb[RPB_PAD:-RPB_PAD] = arr["na_rpb"].ravel()
    data["rpb"] = rpb
    wp = np.zeros((2, P, P), np.float32)
    for g in range(4):
        lo = g % 2 * DH
        wp[g // 2, lo:lo + DH, lo:lo + DH] = arr["w_pool_2"].reshape(4, DH, DH)[g]
    data["w_pool"] = wp
    data["consts"] = constants()
    data["dft_seq"] = dft_seq()

    nc = bacc.Bacc("TRN2", target_bir_lowering=False, num_devices=1)
    aps = {n: nc.dram_tensor(n, v.shape, mybir.dt.from_np(v.dtype), kind="ExternalInput").ap() for n, v in data.items()}
    out = nc.dram_tensor("out", [SEQ, D], F32, kind="ExternalOutput").ap()
    bass_two_blocks(nc, aps, out)
    r = run_bass_kernel_spmd(nc, [data], core_ids=[0])
    return r.results[0]["out"].reshape(1, SEQ, D)
```

```python
import math
from contextlib import ExitStack

import numpy as np

import concourse.bass as bass
from concourse import mybir

F32 = mybir.dt.float32
F32R = mybir.dt.float32r
I32 = mybir.dt.int32
ACT = mybir.ActivationFunctionType
ALU = mybir.AluOpType
AX = mybir.AxisListType

P = 128
SEQ = 1024
D = 1024
KT = D // P
TT = SEQ // P
CTX = 256
CT = CTX // P
HALF = 512
GRID_W = 64
HEADS = 8
PAIRS = HEADS // 2
DH = 64
SCALE = DH ** -0.5
D_FF = 4 * D
RMS_EPS = 1e-6
LN_EPS = 1e-5
TAPS = 31
PADT = TAPS // 2
D_IN = 2304
W_IN_TILES = D_IN // P
Q0, K0, V0 = 6, 10, 14
RPB_ROWS, RPB_COLS = 15, 31
RPB_PAD = 64
RPB_LEN = HEADS * RPB_ROWS * RPB_COLS + 2 * RPB_PAD
BIAS_ROWS = 14
BIG = -1e30

D_IN2 = 2560
W_IN2_TILES = D_IN2 // P
Q2, K2, V2 = 2, 8, 14
GROUPS = 3
GH = 4
HEAD_AT = [0, 2, 1, 3]
D_FF2 = 2816
FF2_TILES = D_FF2 // P
ROT = 16
THETA = 500000.0

ADA1 = 512
ADA2 = 6 * D // (D_FF // 256)

VECS = [("ada_b", 48), ("b_ada_2", 48), ("norm1_g", 8), ("norm2_g", 8), ("final_norm_g", 8),
        ("g_pre_mix_2", 8), ("g_post_mix_2", 8), ("g_pre_ffn_2", 8), ("g_post_ffn_2", 8),
        ("c", 8), ("c_ctx", 8), ("c_2", 8), ("conv_dw_w", 62), ("conv_dw_b", 2), ("conv_norm_g", 2),
        ("conv_norm_b", 2), ("conv_pw_b", 2), ("b_pool_2", 2), ("pool_scale_2", 2),
        ("conv_w_2", 66), ("conv_b_2", 22)]
VROW = {}
_n = 0
for _name, _rows in VECS:
    VROW[_name] = _n
    _n += _rows
VEC_TILES = -(-_n // P)

CONSTS = [("ident", 128), ("col_mask", 64), ("causal", 256), ("causal16", 128), ("rotate", 128),
          ("dft_c", 128), ("dft_s", 128), ("inv_freq", 1), ("pool_inv", 2), ("pool_head", 32)]
CCOL = {}
_n = 0
for _name, _cols in CONSTS:
    CCOL[_name] = (_n, _cols)
    _n += _cols
N_CONST = _n


def constants():
    out = np.zeros((P, N_CONST), np.float32)

    def put(name, a):
        c, n = CCOL[name]
        out[:, c:c + n] = a

    put("ident", np.eye(P))
    col = np.arange(GRID_W)
    start = np.clip(col - 8, 0, GRID_W - 16)
    ok = (col[None] >= start[:, None]) & (col[None] < start[:, None] + 16)
    put("col_mask", np.tile(np.where(ok, 0.0, BIG), (2, 1)))
    i = np.arange(P)[:, None]
    j = np.arange(P)[None]
    put("causal", np.concatenate([np.where(j >= i, 0.0, BIG), np.where(j <= i, 0.0, BIG)], 1))
    put("causal16", np.where((j <= i) & ((i - j) % 2 == 0), 0.0, BIG))
    rot = np.zeros((P, P))
    inv = np.zeros((P, 1), np.float32)
    f = np.float32(THETA) ** (-np.arange(0, ROT, 2, dtype=np.float32) / np.float32(ROT))
    for h in range(2):
        for a in range(ROT // 2):
            lo, hi = h * DH + a, h * DH + a + ROT // 2
            rot[hi, lo] = -1.0
            rot[lo, hi] = 1.0
            inv[lo] = inv[hi] = f[a]
    put("rotate", rot)
    put("inv_freq", inv)
    k = np.arange(64)
    ang = 2 * np.pi * ((k[:, None] * k[None]) % 64) / 64
    norm = 1.0 / math.sqrt(SEQ * 64)
    for name, m in (("dft_c", np.cos(ang)), ("dft_s", np.sin(ang))):
        bd = np.zeros((P, P))
        bd[:64, :64] = bd[64:, 64:] = m * norm
        put(name, bd)
    win = np.array([[2, 8], [4, 16]])[np.arange(P) // 64]
    put("pool_inv", 1.0 / win)
    t = np.arange(16)
    put("pool_head", (1.0 / np.minimum(t[None, None] + 1, win[:, :, None])).reshape(P, 32))
    return out


NYQ = SEQ // 2


def dft_seq():
    t = np.arange(SEQ)
    s = np.arange(NYQ + 1)
    ang = 2 * np.pi * ((t[:, None] * s[None]) % SEQ) / SEQ
    return np.concatenate([np.cos(ang), np.sin(ang[:, :NYQ])], 1).astype(np.float32)


WIN_U = [0, 0, 0, 2, 4, 6, 8, 8]
WIN_N = [512, 512, 640, 640, 640, 640, 512, 512]


def perm(ap, g, b):
    if g == 0:
        return ap[:, b * P:(b + 1) * P]
    if g == 1:
        return ap.rearrange("p (n i r) -> p n r i", n=2, r=4)[:, b // 4, b % 4]
    return ap.rearrange("p (k r) -> p r k", r=8)[:, b]


def two_pi_parts():
    parts, rest = [], 2 * math.pi
    for _ in range(3):
        e = 2.0 ** (math.floor(math.log2(rest)) - 7)
        parts.append(math.floor(rest / e) * e)
        rest -= parts[-1]
    return parts + [rest]


def bass_two_blocks(nc, a, out):
    with ExitStack() as ctx:
        base = -(-nc.sbuf_base // 32) * 32

        def at(name, kb, shape, dt=F32):
            return nc.alloc_sbuf_tensor_at("b_" + name, shape, dt, offset=base + int(kb * 1024))

        sems = {}

        def sem(name):
            if name not in sems:
                sems[name] = ctx.enter_context(nc.semaphore("s_" + name))
            return sems[name]

        PS = ctx.enter_context(nc.psum_tensor("ps_all", [P, 8, HALF], F32))

        def bank2(b):
            return PS[:, b:b + 2, :].rearrange("p b n -> p (b n)")

        vcol = at("vcol", 0, [P, VEC_TILES * P])
        cst = at("cst", 1.5, [P, N_CONST])
        ones = at("ones", 5.5, [P, P])
        sm = [at("small0", 6, [P, 256]), at("small1", 207, [P, 200])]
        w_raw = at("w_raw", 183, [P, 2, 1024])
        up_h = at("up_h", 191, [P, 2, 1024], F32R)
        up_l = at("up_l", 199, [P, 2, 1024], F32R)
        dn_h = at("dn_h", 71, [P, 2, 1024], F32R)
        dn_l = at("dn_l", 79, [P, 2, 1024], F32R)

        def vec(name, t=0, n=1):
            return vcol[:, bass.ds(t + VROW[name], n)]

        def const(name):
            c, n = CCOL[name]
            return cst[:, c:c + n]

        ident = const("ident")
        small_at = [0, 0]

        def small(n):
            i = 0 if small_at[0] + n <= 256 else 1
            small_at[i] += n
            return sm[i][:, small_at[i] - n:small_at[i]]

        mod1, modc, mod2 = small(48), small(16), small(48)
        silu_c = small(24)
        gs1, gsc, gs2, gsm, gsf, ggm, ggf = (small(8) for _ in range(7))
        ss10, root10, rstd10 = small(10), small(10), small(10)
        root8, rstd8 = small(8), small(8)
        ms_m, root_m, rstd_m, rstd_fm, gs_fm = (small(8) for _ in range(5))
        pbias = small(2)
        st_m, st_m2, st_neg, st_d, st_d2, st_r = (small(2) for _ in range(6))

        hn1_h = at("hn1_h", 87, [P, KT, SEQ + CTX], F32R)
        hn1_l = at("hn1_l", 127, [P, KT, SEQ + CTX], F32R)
        xtok = at("xtok", 127, [P, TT + CT, D])
        xs = at("xs", 7, [P, KT, SEQ + CTX])
        ada_acc0 = at("ada_acc0", 49, [P, 4, 1024])
        junk = at("junk", 71, [P, 2, 1024])
        vrow = at("vrow", 69, [P, VEC_TILES, P])
        ada_ring0 = at("ada_ring0", 167, [P, 2, 1024])
        ada_in1 = [at(f"ada_in1{s}", 47 + 16 * s, [P, KT, ADA1]) for s in range(2)]
        ada_acc1 = at("ada_acc1", 167, [P, 2, ADA1])
        vpad = at("vpad", 173, [P, 2, SEQ + 2 * PADT])
        pt1 = at("pt1", 7, [P, W_IN_TILES, SEQ])
        ckv = at("ckv", 79, [P, 2 * PAIRS, CTX])
        conv_out = at("conv_out", 15, [P, 2, SEQ])
        conv_sq = conv_out
        conv_acc = at("conv_acc", 23, [P, 2, SEQ])
        pw = at("pw", 177, [P, 2, 256])
        ln_r = at("ln_r", 173, [P, SEQ])
        four_y = at("four_y", 7, [P, 2, SEQ])
        dseq = at("dseq", 87, [P, TT, 2 * NYQ + 1])
        zf = at("zf", 119.875, [P, TT, HALF])
        four_ab = at("four_ab", 167, [P, 2, HALF])
        wf = at("wf", 171, [P, 2, 256])
        four_e = [at("four_e0", 169, [P, HALF]), at("four_e1", 136.5, [P, HALF])]
        qs = [at(f"qs{s}", 87 + 4 * s, [P, SEQ]) for s in range(2)]
        ks = [at(f"ks{s}", 95 + 5 * s, [P, SEQ + CTX]) for s in range(2)]
        vs = at("vs", 105, [P, SEQ + CTX])
        prob = [at(f"prob{s}", 110 + 3.5 * s, [P, 896]) for s in range(2)]
        sbias = [at(f"sbias{s}", 117 + 2.5 * s, [P, 640]) for s in range(2)]
        probt = [at(f"probt{s}", 122 + 3.5 * s, [P, 896]) for s in range(2)]
        vt = [at(f"vt{s}", 129 + 5 * s, [P, TT + CT, P]) for s in range(2)]
        tb = [at(f"tb{s}", 139 + 7 * s, [P, 2, BIAS_ROWS * GRID_W]) for s in range(2)]
        tbm = [at(f"tbm{s}", 153 + 5 * s, [P, 2, 640]) for s in range(2)]
        ao = at("ao", 163, [P, PAIRS, SEQ])
        rdiag = [at(f"rdiag{s}", 179 + 0.5 * s, [P, P]) for s in range(2)]
        mix_h = at("mix_h", 39, [P, KT, SEQ], F32R)
        mix_l = at("mix_l", 87, [P, KT, SEQ], F32R)
        xslab = at("xslab", 119, [P, 2, TT, P])
        xt = at("xt", 7, [P, KT, SEQ])
        hn_h = at("hn_h", 119, [P, KT, SEQ], F32R)
        hn_l = at("hn_l", 151, [P, KT, SEQ], F32R)
        hid_h = at("hid_h", 39, [P, 2, 2, SEQ], F32R)
        hid_l = at("hid_l", 55, [P, 2, 2, SEQ], F32R)
        nsq = at("nsq", 175, [P, 2, SEQ])
        nsq_fm = at("nsq_fm", 167, [P, 4, SEQ])
        nsq_y = at("nsq_y", 119, [P, 2, SEQ])
        sq_sum = at("sq_sum", 171, [P, SEQ])
        sq_sum_y = at("sq_sum_y", 127, [P, SEQ])
        sq_sum_f = at("sq_sum_f", 159, [P, SEQ])
        sq_sum_m = at("sq_sum_m", 163, [P, SEQ])
        ndiag_m = at("ndiag_m", 59, [P, SEQ])
        ndiag = at("ndiag", 47, [P, SEQ])
        nhn = at("nhn", 51, [P, 2, SEQ])
        sq = at("sq", 87, [P, 2, SEQ])
        ada_in2 = at("ada_in2", 95, [P, KT, ADA2])
        ada_acc2 = at("ada_acc2", 107, [P, ADA2])
        pt2 = at("pt2", 7, [P, W_IN2_TILES, SEQ])
        cos = at("cos", 87, [P, SEQ])
        sin = at("sin", 91, [P, SEQ])
        pos = at("pos", 95, [P, SEQ], I32)
        ang = at("ang", 99, [P, SEQ])
        turn = at("turn", 103, [P, SEQ])
        turn_i = at("turn_i", 107, [P, SEQ], I32)
        rt = at("rt", 95, [P, SEQ])
        rt2 = at("rt2", 99, [P, SEQ])
        ps2 = at("pools2", 103, [P, SEQ])
        ps4 = at("pools4", 107, [P, SEQ])
        pmix = at("pmix", 111, [P, 2, SEQ])
        pout = at("pout", 103, [P, 2, SEQ])
        wp = at("wp", 85, [P, 2, P])
        v2 = at("v2", 119, [P, GROUPS * TT, 256])
        s2 = [at(f"sc2{s}", 143 + 4 * s, [P, GH, 256]) for s in range(2)]
        pr2 = [at(f"pr2{s}", 151 + 4 * s, [P, GH, 256]) for s in range(2)]
        pt2t = [at(f"pt2t{s}", 159 + 4 * s, [P, 8, P]) for s in range(2)]
        ROWW = GH * DH + 2 * GH
        og = [at(f"og{s}", 87 + 1.5 * s, [P, ROWW]) for s in range(4)]
        oall = at("oall", 93, [P, TT, GROUPS, ROWW])
        cw = at("cw", 15, [P, TT, GROUPS, GH])
        cmax = at("cmax", 15.5, [P, TT, GH])
        cwn = at("cwn", 32, [P, TT, GROUPS, GH])
        cden = at("cden", 15.75, [P, TT, GH])
        csum = at("csum", 16, [P, TT, GH, DH])
        cterm = at("cterm", 24, [P, TT, GH, DH])
        mix2_h = at("mix2_h", 69, [P, 4, SEQ], F32R)
        mix2_l = at("mix2_l", 167, [P, 4, SEQ], F32R)
        y2 = at("y2", 87, [P, KT, SEQ])
        gbuf = at("gbuf", 7, [P, 2, SEQ])
        gelu = at("gelu", 15, [P, 2, SEQ])
        gv = at("gv", 23, [P, 2, SEQ])
        otok = at("otok", 119, [P, 2, D])

        st2_neg = [small(GH), small(GH)]
        st2_den = [x[:, GH * DH + GH:] for x in og]

        def keys2(n):
            g, b = divmod(n, TT)
            return 256 if (g == 0 and b) or (g == 1 and b >= 4) else P

        st_rr = small(4)

        def vpad_edges(side):
            lo = 0 if side == 0 else PADT + SEQ
            return vpad[:, :, lo:lo + PADT]

        o_rows = nc.dram_tensor("o_rows", [GROUPS, SEQ, ROWW], F32, kind="Internal").ap()
        rpb_rows = nc.dram_tensor("rpb_rows", [GRID_W, RPB_LEN], F32, kind="Internal").ap()
        xt_spill = nc.dram_tensor("xt_spill", [2, P, KT, SEQ], F32, kind="Internal").ap()

        U_G2, U_WO1 = 0, W_IN_TILES
        U_FF1 = U_WO1 + KT
        CH1 = D_FF // (2 * P)
        U_WIN2 = U_FF1 + 2 * CH1
        U_WO2 = U_WIN2 + W_IN2_TILES
        U_FF2 = U_WO2 + KT
        CH2 = FF2_TILES // 2
        C_FF1, C_FF2 = 0, CH1

        w_in = a["w_in"]
        raw_in = [sem("raw_in0"), sem("raw_in1")]
        up_full, dn_full = sem("up_full"), sem("dn_full")
        up_done = sem("up_done")
        up_evac = sem("up_evac")
        dn_done, dn_evac = sem("dn_done"), sem("dn_evac")
        raw_split = sem("raw_high")

        def up_src(w, col, kt=KT):
            return w.rearrange("(k p) f -> p k f", p=P)[:, :, col]

        block = ctx.enter_context(nc.Block())

        def carry(eng):
            eng.sem_inc(sem("carried"), 1)

        def load_up(sp, u, w, m, slot, raw_n, kt=KT, dn_before=None):
            sp.wait_ge(up_full, u + 1)
            if dn_before is not None:
                carry(sp)
                sp.wait_ge(dn_full, dn_before)
            carry(sp)
            sp.dma_start(w_raw[:, slot, 0:kt * P].rearrange("p (k f) -> p k f", k=kt),
                         up_src(w, bass.ts(m, P))).then_inc(raw_in[slot], 16)

        def load_dn(sp, d, w, row, slot, u_before):
            sp.wait_ge(up_full, u_before)
            carry(sp)
            sp.dma_start(w_raw[:, slot, :], w[bass.ts(row, P), :]).then_inc(raw_in[slot], 16)

        def split_up(pool, u, slot, raw_n, n_split, kt=KT):
            n = kt * P
            pool.wait_ge(raw_in[slot], 16 * raw_n)
            pool.wait_ge(up_done, u + 1)
            carry(pool)
            pool.tensor_scalar(up_h[:, slot, 0:n], w_raw[:, slot, 0:n], 0.0, 1.0, ALU.add,
                               ALU.mult).then_inc(raw_split, 1)
            pool.wait_ge(raw_split, n_split)
            pool.tensor_tensor(up_l[:, slot, 0:n], w_raw[:, slot, 0:n],
                               up_h[:, slot, 0:n].bitcast(F32), ALU.subtract).then_inc(up_full, 1)

        def split_dn(pool, d, slot, raw_n, n_split, units_before):
            pool.wait_ge(raw_in[slot], 16 * raw_n)
            pool.wait_ge(dn_done, units_before + 1)
            carry(pool)
            pool.tensor_scalar(dn_h[:, slot, :], w_raw[:, slot, :], 0.0, 1.0, ALU.add,
                               ALU.mult).then_inc(raw_split, 1)
            pool.wait_ge(raw_split, n_split)
            pool.tensor_tensor(dn_l[:, slot, :], w_raw[:, slot, :],
                               dn_h[:, slot, :].bitcast(F32), ALU.subtract).then_inc(dn_full, 1)

        def mul_up(pe, u, slot, xh, xl, kt=KT, extra=None, ready=None):
            pe.wait_ge(up_full, u + 3)
            pe.wait_ge(up_evac, u + 1)
            spans = [(PS[:, 2 * slot + j, :], j * HALF, HALF) for j in range(2)]
            if extra:
                spans.append((PS[:, 4 + slot, 0:extra], SEQ, extra))
            for k in range(kt):
                if ready:
                    pe.wait_ge(*ready(k))
                for n, (w, x) in enumerate(((up_h, xh), (up_h, xl), (up_l, xh))):
                    for dst, c, width in spans:
                        mm = pe.matmul(dst, w[:, slot, k * P:(k + 1) * P], x[:, k, c:c + width],
                                       start=(k == 0 and n == 0), stop=(k == kt - 1 and n == 2))
            mm.then_inc(up_done, 1)

        def mul_dn(pe, d, hid, unit0):
            pe.wait_ge(dn_full, d + 4)
            for m in range(KT):
                for j in range(2):
                    i = 2 * m + j
                    pe.wait_ge(dn_evac, unit0 + i + 1)
                    for k in range(2):
                        for n, (w, x) in enumerate(((dn_h, hid_h), (dn_h, hid_l), (dn_l, hid_h))):
                            mm = pe.matmul(PS[:, 4 + i % 2, :], w[:, k, m * P:(m + 1) * P],
                                           x[:, hid, k, j * HALF:(j + 1) * HALF],
                                           start=(k == 0 and n == 0), stop=(k == 1 and n == 2))
                    mm.then_inc(dn_done, 1)

        SUMS = {"mlp": 0, "final": 1, "post2": 2, "ffn2": 3, "out": 4}
        NORMS = {"mlp": 0, "final": 1, "mix2": 2, "post2": 3, "ffn2": 4, "out": 5}
        MODULATED = {"mlp": 0, "mix2": 1, "ffn2": 2}
        nsem = {s: sem("norm_" + s) for s in ("sq", "acc", "sums", "root", "rstd", "diag", "bc", "hn", "mod", "high", "low")}

        def square(act, n, k, slot, buf, acc, src):
            if isinstance(k, int) and k == 0:
                act.activation(acc[:, :], src, ACT.Square).then_inc(nsem["sq"], 1)
                return
            act.wait_ge(nsem["acc"], k + 7 * SUMS[n])
            if not isinstance(k, int):
                carry(act)
            act.activation(buf[:, slot, :], src, ACT.Square).then_inc(nsem["sq"], 1)

        def add_square(eng, n, k, slot, buf, acc):
            eng.wait_ge(nsem["sq"], k + (KT * SUMS[n] + 1))
            eng.wait_ge(nsem["acc"], k + (7 * SUMS[n] + 1))
            eng.tensor_tensor(acc[:, :], acc[:, :], buf[:, slot, :], ALU.add).then_inc(nsem["acc"], 1)

        def add_sums(pe, n, acc):
            pe.wait_ge(nsem["acc"], 7 * SUMS[n] + 9)
            for t in range(TT):
                mm = pe.matmul(PS[:, 7, t:t + 1], acc[:, t * P:(t + 1) * P], ones[:, 0:1], start=True, stop=True)
            mm.then_inc(nsem["sums"], 1)

        def norm_root(act, n):
            act.wait_ge(nsem["sums"], SUMS[n] + 1)
            act.activation(root8, PS[:, 7, 0:TT], ACT.Sqrt, scale=1.0 / D, bias=eps_rms).then_inc(nsem["root"], 1)

        def norm_rstd(dve, n, out, root):
            dve.wait_ge(nsem["root"], NORMS[n] + 1)
            dve.reciprocal(out, root).then_inc(nsem["rstd"], 1)
            dve.wait_ge(nsem["rstd"], NORMS[n] + 1)

        def norm_diag(dve, buf, r):
            dve.tensor_tensor(buf[:, :].rearrange("p (t c) -> p t c", c=P), ident.unsqueeze(1).to_broadcast([P, TT, P]),
                              r.unsqueeze(2).to_broadcast([P, TT, P]), ALU.mult).then_inc(nsem["diag"], 1)

        def norm_spread(pe, n, buf, bank):
            pe.wait_ge(nsem["diag"], NORMS[n] + 1)
            for j in range(2):
                mm = pe.matmul(PS[:, bank + j, :], ones[:, :], buf[:, j * HALF:(j + 1) * HALF], start=True, stop=True)
            mm.then_inc(nsem["bc"], 1)

        def norm_vector(dve, n):
            norm_rstd(dve, n, rstd8, root8)
            norm_diag(dve, ndiag, rstd8)
            dve.wait_ge(nsem["bc"], NORMS[n] + 1)

        def modulate_vector(dve, n, src):
            n8 = KT * MODULATED[n]
            for k in range(KT + 1):
                if k < KT:
                    if k >= 2:
                        dve.wait_ge(nsem["low"], n8 + k - 1)
                    dve.tensor_tensor(nhn[:, k % 2, :], src[:, k, :], bank2(2), ALU.mult
                                      ).then_inc(nsem["hn"], 1)
                if k >= 1:
                    j = k - 1
                    dve.wait_ge(nsem["high"], n8 + j + 1)
                    dve.tensor_tensor(hn_l[:, j, :], nhn[:, j % 2, :], hn_h[:, j, :].bitcast(F32),
                                      ALU.subtract).then_inc(nsem["low"], 1)

        def modulate_scalar(act, n, gs, sh):
            n8 = KT * MODULATED[n]
            for k in range(KT):
                act.wait_ge(nsem["hn"], n8 + k + 1)
                act.activation(nhn[:, k % 2, :], nhn[:, k % 2, :], ACT.Identity, scale=gs[:, k:k + 1],
                               bias=sh[:, k:k + 1]).then_inc(nsem["mod"], 1)
                act.wait_ge(nsem["mod"], n8 + k + 1)
                act.activation(hn_h[:, k, :], nhn[:, k % 2, :], ACT.Copy).then_inc(nsem["high"], 1)

        eps_rms = small(1)
        eps_ln = small(1)

        @block.sync
        def _(sp):
            sp.dma_start(vrow[:, :, :], a["vecs"].rearrange("(t p) f -> p t f", p=P)).then_inc(sem("tables_in"), 16)
            sp.dma_start(cst[:, :], a["consts"]).then_inc(sem("tables_in"), 16)
            for b in range(2):
                for k in range(KT):
                    n = b * KT + k
                    sp.wait_ge(sem("ada_used"), n + 1)
                    sp.dma_start(ada_ring0[:, n % 2, :], a["ada_w"][bass.ts(k, P), bass.ts(b, 1024)]
                                 ).then_inc(sem(f"ada_in{n % 2}"), 16)
            def ada1(b, s, wait=True):
                if wait:
                    sp.wait_ge(sem("ada1_used"), b * KT - 6)
                    carry(sp)
                sp.dma_start(ada_in1[s][:, :, :], a["ada_w"].rearrange("(k p) f -> p k f", p=P)[:, :, bass.ds(b * ADA1 + 2048, ADA1)]
                             ).then_inc(sem(f"ada1_in{s}"), 16)

            for s in range(2):
                load_up(sp, s, w_in, s, s, None)
            sp.wait_ge(sem("ada_sum0"), 2)
            for s in range(2):
                ada1(s, s, False)
            with sp.Fori(1, 4) as i:
                for s in range(2):
                    load_up(sp, i * 2 + s, w_in, i * 2 + s, s, None)
                for s in range(2):
                    ada1(i * 2 + s, s)
            for s in range(2):
                load_up(sp, 8 + s, w_in, 8 + s, s, None)
            sp.dma_start(wf[:, :, :], a["w_fourier"].rearrange("(t p) f -> p t f", p=P)).then_inc(sem("four_in"), 16)
            with sp.Fori(0, 4) as i:
                for s in range(2):
                    load_up(sp, i * 2 + K0 + s, w_in, i * 2 + K0 + s, s, None)
            sp.dma_start(rpb_rows, bass.AP(a["rpb"].tensor, 0, [[0, GRID_W], [1, RPB_LEN]])).then_inc(sem("rpb_in"), 16)
            for m in range(2):
                load_up(sp, U_WO1 + m, a["w_out"], m, m, None)
            sp.wait_ge(up_done, U_WO1 + 2)
            sp.dma_start(dseq[:, :, :], a["dft_seq"].rearrange("(t p) f -> p t f", p=P)).then_inc(sem("four_in"), 16)
            sp.wait_ge(sem("taps"), 2 * TAPS)
            sp.dma_start(pw[:, :, :], a["conv_pw_w"].rearrange("(t p) f -> p t f", p=P)).then_inc(sem("point_in"), 16)
            sp.wait_ge(sem("rpb_in"), 16)
            for p in range(PAIRS):
                s = p % 2
                if p >= 2:
                    sp.wait_ge(sem("na_biased"), 16 * p + 1)
                for h in range(2):
                    for par in range(2):
                        off = RPB_PAD + (2 * p + h) * RPB_ROWS * RPB_COLS + (1 - par) * RPB_COLS + RPB_COLS // 2
                        src = bass.AP(rpb_rows.tensor, off, [[RPB_LEN - 1, GRID_W], [RPB_COLS, BIAS_ROWS], [1, GRID_W]])
                        dst = tb[s][par * GRID_W:(par + 1) * GRID_W, h, :].rearrange("p (r c) -> p r c", c=GRID_W)
                        sp.dma_start(dst, src).then_inc(sem(f"bias_in{s}"), 16)
            sp.wait_ge(sem("na_o"), 16 * PAIRS + 1)
            for m in range(2):
                sp.dma_start(xslab[:, m, :, :], a["x"].rearrange("(t p) f -> p t f", p=P)[:, :, bass.ts(m, P)]
                             ).then_inc(sem(f"slab_in{m}"), 16)
            with sp.Fori(1, 4) as i:
                for s in range(2):
                    load_up(sp, i * 2 + U_WO1 + s, a["w_out"], i * 2 + s, s, None)
                    sp.wait_ge(sem("slab_used"), i * 2 + s - 1)
                    sp.dma_start(xslab[:, s, :, :], a["x"].rearrange("(t p) f -> p t f", p=P)[:, :, bass.ds((i * 2 + s) * P, P)]
                                 ).then_inc(sem(f"slab_in{s}"), 16)
            def ff1_up(c):
                for s in range(2):
                    load_up(sp, c * 2 + U_FF1 + s, a["mlp_w1"], c * 2 + s, s, None, dn_before=c * 2 + s - 1 + 2 * C_FF1)

            def ff1_dn(c):
                for s in range(2):
                    load_dn(sp, None, a["mlp_w2"], c * 2 + s, s, c * 2 + U_FF1 + 2 + 3 + s)

            def ada2_in(b):
                sp.wait_ge(sem("ada2_used"), b * KT + 2)
                carry(sp)
                sp.dma_start(ada_in2[:, :, :], a["w_ada_2"].rearrange("(k p) f -> p k f", p=P)[:, :, bass.ds(b * ADA2, ADA2)]
                             ).then_inc(sem("ada2_in"), 16)

            for s in range(2):
                load_up(sp, U_FF1 + s, a["mlp_w1"], s, s, None)
            sp.wait_ge(up_done, U_FF1 + 2)
            ada2_in(0)
            with sp.Fori(0, (CH1 - 2) // 2) as j:
                for e in range(2):
                    ff1_up(j * 2 + 1 + e)
                    ada2_in(j * 2 + 1 + e)
                    ff1_dn(j * 2 + e)
            ff1_up(CH1 - 1)
            ada2_in(CH1 - 1)
            ff1_dn(CH1 - 2)
            for s in range(2):
                sp.wait_ge(dn_full, 2 * (CH1 - 2) + s + 3)
                load_dn(sp, None, a["mlp_w2"], 2 * (CH1 - 1) + s, s, U_FF1 + 2 * CH1 + 2)
            def win2(p, m, s, dn_before=None):
                load_up(sp, p + U_WIN2, a["w_in_2"], m, s, None, dn_before=dn_before)

            for s in range(2):
                win2(s, V2 + s, s, dn_before=2 * CH1 + 2)
            sp.wait_ge(dn_done, 16 * CH1 + 1)
            sp.dma_start(pos[:, :], bass.AP(a["positions_2"].tensor, 0, [[0, P], [1, SEQ]])).then_inc(sem("pos_in"), 16)
            with sp.Fori(1, 3) as i:
                for s in range(2):
                    win2(i * 2 + s, i * 2 + (V2 + s), s)
            sp.wait_ge(sem("x1_ready"), KT)
            sp.dma_start(xt_spill[0], xt[:, :, :]).then_inc(sem("x_moved"), 16)
            with sp.Fori(3, 6) as i:
                for s in range(2):
                    win2(i * 2 + s, i * 2 + (K2 - 6 + s), s)
            with sp.Fori(0, 4) as i:
                for s in range(2):
                    win2(i * 2 + (12 + s), i * 2 + s, s)
            for m in range(2):
                load_up(sp, U_WO2 + m, a["w_out_2"], m, m, None, kt=4)
            sp.wait_ge(sem("v2_turned"), GROUPS * TT // 4)
            sp.dma_start(wp[:, :, :], a["w_pool"].rearrange("c p f -> p c f")).then_inc(sem("point_in"), 16)
            for g in range(GROUPS):
                rows = o_rows[g]
                if g == GROUPS - 1:
                    for e in range(4):
                        sp.wait_ge(sem(f"o2_out{e}"), 16 * g * TT // 4)
                    for j in range(g):
                        sp.dma_start(oall[:, :, j, :], o_rows[j].rearrange("(t p) w -> p t w", p=P)).then_inc(sem("oall_in"), 16)
                for b in range(TT):
                    n = g * TT + b
                    sp.wait_ge(sem("o2_ready"), n + 1)
                    if g == 0:
                        dst = rows[b * P:(b + 1) * P]
                    elif g == 1:
                        dst = rows.rearrange("(n i r) w -> n r i w", n=2, r=4)[b // 4, b % 4]
                    else:
                        dst = rows.rearrange("(k r) w -> r k w", r=8)[b]
                    sp.dma_start(dst, og[n % 4][:, :]).then_inc(sem(f"o2_out{n % 4}"), 16)
            for e in range(4):
                sp.wait_ge(sem(f"o2_out{e}"), 16 * GROUPS * TT // 4)
            for g in range(GROUPS - 1, GROUPS):
                sp.dma_start(oall[:, :, g, :], o_rows[g].rearrange("(t p) w -> p t w", p=P)).then_inc(sem("oall_in"), 16)
            with sp.Fori(1, KT // 2) as i:
                for s in range(2):
                    load_up(sp, i * 2 + U_WO2 + s, a["w_out_2"], i * 2 + s, s, None, kt=4)
            sp.wait_ge(sem("mix2_split"), 4)
            sp.wait_ge(sem("x_moved"), 16)
            sp.dma_start(xt[:, :, :], xt_spill[0]).then_inc(sem("x_moved"), 16)
            def ff2_up(c):
                for i in range(4):
                    f = c * 2 + i // 2 + (FF2_TILES if i % 2 else 0)
                    load_up(sp, c * 4 + U_FF2 + i, a["w_up_2"], f, i % 2, None,
                            dn_before=(c * 2 + i - 1 + 2 * C_FF2) if i < 2 else None)

            def ff2_dn(c):
                for s in range(2):
                    load_dn(sp, None, a["w_down_2"], c * 2 + s, s, c * 4 + U_FF2 + 4 + 5 + s)

            ff2_up(0)
            sp.wait_ge(sem("x2_ready"), KT)
            sp.dma_start(xt_spill[1], xt[:, :, :]).then_inc(sem("x_moved"), 16)
            with sp.Fori(0, (CH2 - 1) // 2) as j:
                ff2_up(j * 2 + 1)
                ff2_dn(j * 2)
                ff2_up(j * 2 + 2)
                ff2_dn(j * 2 + 1)
            for s in range(2):
                sp.wait_ge(dn_full, 2 * (C_FF2 + CH2 - 2) + s + 3)
                load_dn(sp, None, a["w_down_2"], 2 * (CH2 - 1) + s, s, U_FF2 + 4 * CH2 + 2)
            sp.wait_ge(sem("ff2_low"), 2 * CH2)
            sp.wait_ge(sem("x_moved"), 48)
            sp.dma_start(xt[:, :, :], xt_spill[1]).then_inc(sem("x_moved"), 16)
            for t in range(TT):
                sp.wait_ge(sem("o_ready"), t + 1)
                sp.dma_start(out[t * P:(t + 1) * P, :], otok[:, t % 2, :]).then_inc(sem(f"stored{t % 2}"), 16)
            for s in range(2):
                sp.wait_ge(sem(f"stored{s}"), 16 * TT // 2)

        @block.gpsimd
        def _(pool):
            pool.sem_inc(up_full, 2)
            pool.sem_inc(dn_full, 2)
            pool.sem_inc(up_done, 2)
            pool.sem_inc(up_evac, 2)
            pool.sem_inc(dn_evac, 2)
            pool.sem_inc(sem("ada_used"), 2)
            pool.sem_inc(sem("ada1_used"), 2)
            pool.sem_inc(sem("ada2_used"), 2)
            pool.sem_inc(sem("mod2"), 1)
            pool.sem_inc(nsem["acc"], 2)
            pool.sem_inc(sem("ada1_sum"), 2)
            pool.sem_inc(sem("rot_s"), 2)
            pool.sem_inc(sem("na_biased"), 17)
            pool.sem_inc(dn_done, 1)
            pool.sem_inc(sem("v_turned"), 1)
            pool.sem_inc(sem("probt_set"), 1)
            pool.sem_inc(sem("na_o"), 1)
            pool.memset(ones[:, :], 1.0).then_inc(sem("ones_set"), 1)
            pool.memset(eps_rms, RMS_EPS).then_inc(sem("ones_set"), 1)
            pool.memset(eps_ln, LN_EPS).then_inc(sem("ones_set"), 1)
            with pool.Fori(0, W_IN_TILES // 2) as i:
                for s in range(2):
                    split_up(pool, i * 2 + s, s, i + 1, i * 2 + s + 1)
            for s in range(2):
                split_up(pool, U_WO1 + s, s, U_WO1 // 2 + 1, U_WO1 + s + 1)
            with pool.Fori(0, PAIRS // 2) as i:
                for s in range(2):
                    pool.wait_ge(up_evac, W_IN_TILES + 2)
                    pool.wait_ge(sem("four_done"), 4)
                    pool.wait_ge(sem("na_biased"), i * 32 + (16 * s + 1))
                    pool.tensor_copy(qs[s][:, :], pt1[:, i * 2 + (Q0 + s), :]).then_inc(sem("staged"), 1)
                    pool.tensor_copy(ks[s][:, 0:SEQ], pt1[:, i * 2 + (K0 + s), :]).then_inc(sem("staged"), 1)
                    pool.tensor_copy(ks[s][:, SEQ:], ckv[:, i * 2 + s, :]).then_inc(sem("staged"), 1)
                    pool.wait_ge(sem("v_turned"), i * 4 + (2 * s + 1))
                    pool.tensor_copy(vs[:, 0:SEQ], pt1[:, i * 2 + (V0 + s), :]).then_inc(sem("staged"), 1)
                    pool.tensor_copy(vs[:, SEQ:], ckv[:, i * 2 + (PAIRS + s), :]).then_inc(sem("staged"), 1)
                    pool.wait_ge(sem(f"bias_in{s}"), i * 64 + 64)
                    tbv = tb[s][:, :, :].rearrange("p h (r c) -> p (h r) c", c=GRID_W)
                    pool.tensor_tensor(tbv, tbv, const("col_mask").unsqueeze(1).to_broadcast([P, 2 * BIAS_ROWS, GRID_W]),
                                       ALU.add).then_inc(sem("bias_set"), 1)
                    pool.wait_ge(sem("bias_set"), i * 10 + 5 * s + 1)
                    carry(pool)
                    pool.tensor_copy(tbm[s][:, :, :], tb[s][:, :, 2 * GRID_W:12 * GRID_W]).then_inc(sem("bias_set"), 1)
                    pool.wait_ge(sem("bias_set"), i * 10 + 5 * s + 2)
                    carry(pool)
                    pool.memset(tbm[s][0:64, :, 8 * GRID_W:], BIG).then_inc(sem("bias_set"), 1)
                    pool.memset(tbm[s][64:P, :, 0:GRID_W], BIG).then_inc(sem("bias_set"), 1)
                    pool.memset(tbm[s][64:P, :, 9 * GRID_W:], BIG).then_inc(sem("bias_set"), 1)
                    pool.wait_ge(sem("bias_set"), i * 10 + 5 * s + 5)
            with pool.Fori(1, KT // 2) as i:
                for s in range(2):
                    split_up(pool, i * 2 + U_WO1 + s, s, i + U_WO1 // 2 + 1, i * 2 + U_WO1 + s + 1)

            r0 = U_FF1

            def ff1_up(c, r):
                for s in range(2):
                    split_up(pool, c * 2 + U_FF1 + s, s, r + 1, r * 2 + s + 1)

            def ff1_dn(c, r):
                for s in range(2):
                    split_dn(pool, None, s, r + 1, r * 2 + s + 1, c * 16)

            ff1_up(0, r0 // 2)
            with pool.Fori(0, (CH1 - 2) // 2) as j:
                ff1_up(j * 2 + 1, j * 4 + r0 // 2 + 1)
                ff1_dn(j * 2, j * 4 + r0 // 2 + 2)
                ff1_up(j * 2 + 2, j * 4 + r0 // 2 + 3)
                ff1_dn(j * 2 + 1, j * 4 + r0 // 2 + 4)
            n = 2 * (CH1 - 2) + r0 // 2 + 1
            ff1_up(CH1 - 1, n)
            ff1_dn(CH1 - 2, n + 1)
            ff1_dn(CH1 - 1, n + 2)
            r1 = r0 + 4 * CH1
            for s in range(2):
                split_up(pool, U_WIN2 + s, s, r1 // 2 + 1, r1 + s + 1)
            for k in range(1, KT):
                pool.wait_ge(nsem["sq"], KT * SUMS["final"] + k + 1)
                if k >= 2:
                    pool.wait_ge(sem("acc_m"), k - 1)
                pool.tensor_tensor(sq_sum_m[:, :], sq_sum_m[:, :], nsq_fm[:, 2 * (k % 2) + 1, :], ALU.add
                                   ).then_inc(sem("acc_m"), 1)
            with pool.Fori(1, W_IN2_TILES // 2) as i:
                for s in range(2):
                    split_up(pool, i * 2 + U_WIN2 + s, s, i + r1 // 2 + 1, i * 2 + r1 + s + 1)
            r2 = r1 + W_IN2_TILES
            for s in range(2):
                split_up(pool, U_WO2 + s, s, r2 // 2 + 1, r2 + s + 1, kt=4)
            with pool.Fori(1, KT // 2) as i:
                for s in range(2):
                    split_up(pool, i * 2 + U_WO2 + s, s, i + r2 // 2 + 1, i * 2 + r2 + s + 1, kt=4)
            r3 = r2 + KT

            def ff2_up(c, r, pieces=range(4)):
                for i in pieces:
                    split_up(pool, c * 4 + U_FF2 + i, i % 2, r + 1 + i // 2, r * 2 + i + 1)

            def ff2_dn(c, r):
                for s in range(2):
                    split_dn(pool, None, s, r + 1, r * 2 + s + 1, c * 16 + 16 * C_FF2)

            ff2_up(0, r3 // 2, range(2))
            for k in range(1, KT):
                add_square(pool, "ffn2", k, k % 2, nsq, sq_sum)
            ff2_up(0, r3 // 2, range(2, 4))
            with pool.Fori(0, (CH2 - 1) // 2) as j:
                ff2_up(j * 2 + 1, j * 6 + r3 // 2 + 2)
                ff2_dn(j * 2, j * 6 + r3 // 2 + 4)
                ff2_up(j * 2 + 2, j * 6 + r3 // 2 + 5)
                ff2_dn(j * 2 + 1, j * 6 + r3 // 2 + 7)
            ff2_dn(CH2 - 1, 3 * (CH2 - 1) + r3 // 2 + 2)

        @block.scalar
        def _(act):
            for t in range(0, TT + CT, 2):
                src = a["x"][t * P:(t + 2) * P, :] if t < TT else a["ctx"]
                act.dma_start(xtok[:, t:t + 2, :], src.rearrange("(t p) f -> p t f", p=P)).then_inc(sem(f"x_in{t // 2}"), 16)
            act.wait_ge(sem("ones_set"), 3)
            for t in range(TT + CT):
                act.wait_ge(sem(f"x_in{t // 2}"), 16)
                if t >= 2:
                    act.wait_ge(sem("ss"), t - 1)
                act.activation(junk[:, t % 2, :], xtok[:, t, :], ACT.Square, accum_out=ss10[:, t:t + 1]).then_inc(sem("ss"), 1)
            act.wait_ge(sem("ss"), TT + CT)
            act.activation(root10, ss10, ACT.Sqrt, scale=1.0 / D, bias=eps_rms).then_inc(sem("root10"), 1)
            act.wait_ge(sem("vec_set"), 1)
            act.activation(silu_c, vec("c", 0, 24), ACT.Silu).then_inc(sem("silu"), 1)
            act.wait_ge(sem("rstd10"), 1)
            for t in range(TT + CT + 1):
                if t < TT + CT:
                    act.activation(xtok[:, t, :], xtok[:, t, :], ACT.Copy, scale=rstd10[:, t:t + 1]
                                   ).then_inc(sem("x_scaled"), 1)
                if t >= 1:
                    act.wait_ge(sem("x_turned"), t)
                    act.activation(xs[:, :, (t - 1) * P:t * P],
                                   bank2(2 * ((t - 1) % 2)).rearrange("p (k n) -> p k n", n=P), ACT.Copy
                                   ).then_inc(sem("xs_set"), 1)
            for k in range(KT):
                act.wait_ge(sem("hn1"), 2 * (k + 1))
                act.activation(hn1_h[:, k, :], xs[:, k, :], ACT.Copy).then_inc(sem("hn1_high"), 1)

            def out1(u, scale=1.0, ctx_tile=None, slot=0):
                act.wait_ge(up_done, u + 3)
                if ctx_tile is not None:
                    act.activation(ckv[:, ctx_tile, :], PS[:, 4 + slot, 0:CTX], ACT.Copy).then_inc(sem("ckv_set"), 1)
                act.activation(pt1[:, u, :], bank2(2 * slot), ACT.Copy, scale=scale).then_inc(up_evac, 1)

            act.wait_ge(sem("hn1_low"), KT)
            with act.Fori(0, Q0 // 2) as i:
                for s in range(2):
                    out1(i * 2 + s, slot=s)
            act.wait_ge(up_evac, Q0 + 2)
            act.activation(pt1[:, 4:6, :], pt1[:, 4:6, :], ACT.Sigmoid).then_inc(sem("gate"), 1)
            with act.Fori(Q0 // 2, K0 // 2) as i:
                for s in range(2):
                    out1(i * 2 + s, scale=SCALE, slot=s)
            act.wait_ge(sem("ada1_used"), 8 * KT + 2)

            def out_kv(j, s):
                out1(j + K0, ctx_tile=j, slot=s)

            for s in range(2):
                out_kv(s, s)
            for c in range(2):
                act.wait_ge(sem("four_w"), c + 1)
                act.activation(four_ab[:, c, :], PS[:, 6 + c, :], ACT.Copy).then_inc(sem("four_ab"), 1)
            with act.Fori(1, 3) as i:
                for s in range(2):
                    out_kv(i * 2 + s, s)
            for c in range(2):
                act.wait_ge(sem("ln_d"), c + 1)
                act.activation(conv_sq[:, c, :], conv_acc[:, c, :], ACT.Square).then_inc(sem("ln_sq"), 1)
            out_kv(6, 0)
            act.wait_ge(sem("ln_sums"), 2)
            act.activation(ln_r[:, :], bank2(6), ACT.Sqrt, scale=1.0 / 256, bias=eps_ln).then_inc(sem("ln_root"), 1)
            out_kv(7, 1)
            for t in range(TT):
                act.wait_ge(sem("four_z"), t + 1)
                act.activation(zf[:, t, :], PS[:, 4 + t % 2, :], ACT.Copy).then_inc(sem("zf_set"), 1)
            for c in range(2):
                act.wait_ge(sem("ln_y"), c + 1)
                act.activation(conv_acc[:, c, :], conv_acc[:, c, :], ACT.Silu, scale=vec("conv_norm_g", c),
                               bias=vec("conv_norm_b", c)).then_inc(sem("conv_s"), 1)
            for n in range(2):
                act.wait_ge(sem("four_done"), 2 * n + 1)
                act.activation(four_e[n][:, :], PS[:, 6 - 2 * n, :], ACT.Copy).then_inc(sem("four_e"), 1)
                act.activation(four_y[:, n, NYQ:NYQ + 1], PS[:, n, 0:1], ACT.Copy).then_inc(sem("four_e"), 1)
            for m in range(2):
                act.wait_ge(sem("conv_pw"), m + 1)
                act.activation(conv_out[:, m, :], bank2(2 * m), ACT.Identity, bias=vec("conv_pw_b", m)
                               ).then_inc(sem("conv_done"), 1)
            act.wait_ge(sem("four_mir"), 4)
            with act.Fori(0, PAIRS // 2) as i:
                for s in range(2):
                    n0 = i * 32 + 16 * s
                    for r in range(2):
                        lo, cnt = 8 * r, 8 if r == 0 else 2
                        act.wait_ge(sem("v_turned"), i * 4 + (2 * s + r + 2))
                        act.activation(vt[s][:, lo:lo + cnt, :], bank2(4)[:, 0:cnt * P].rearrange("p (t c) -> p t c", c=P),
                                       ACT.Copy).then_inc(sem("vt_set"), 1)
                    for n in range(17):
                        if n < 16:
                            w = WIN_N[n % 8]
                            act.wait_ge(sem("na_max"), n0 + n + 1)
                            act.activation(prob[n % 2][:, 0:w], sbias[n % 2][:, 0:w], ACT.Exp,
                                           bias=st_neg[:, n % 2:n % 2 + 1], accum_out=st_d[:, n % 2:n % 2 + 1]
                                           ).then_inc(sem("na_exp"), 1)
                            act.activation(prob[n % 2][:, w:w + CTX], bank2(2 * (n % 2))[:, w:w + CTX], ACT.Exp,
                                           bias=st_neg[:, n % 2:n % 2 + 1], accum_out=st_d2[:, n % 2:n % 2 + 1]
                                           ).then_inc(sem("na_exp"), 1)
                        if n >= 1:
                            w = WIN_N[(n - 1) % 8] + CTX
                            act.wait_ge(sem("na_turned"), n0 + n)
                            act.activation(probt[(n - 1) % 2][:, 0:w], bank2(4)[:, 0:w], ACT.Copy).then_inc(sem("probt_set"), 1)
            for k in range(4):
                act.wait_ge(sem("four_mir"), 4)
                src = four_y[:, k, :] if k < 2 else conv_out[:, k - 2, :]
                if k == 0:
                    act.wait_ge(sem("na_o"), 16 * PAIRS + 1)
                    act.wait_ge(sem("four_e"), 4)
                act.activation(mix_h[:, k, :], src, ACT.Copy).then_inc(sem("mix_high"), 1)
            for f in range(4):
                act.activation(mix_h[:, 4 + f, :], ao[:, f, :], ACT.Copy).then_inc(sem("mix_high"), 1)
            act.wait_ge(sem("mix_low"), KT)
            def x_tile(u, s):
                act.wait_ge(sem("slab_used"), u + 1)
                act.activation(xt[:, u, :], bank2(4), ACT.Copy).then_inc(sem("xt_set"), 1)

            def x_square(u, s):
                act.wait_ge(up_evac, u + (U_WO1 + 3))
                square(act, "mlp", u, s, nsq, sq_sum, xt[:, u, :])

            for s in range(2):
                x_tile(s, s)
            x_square(0, 0)
            with act.Fori(1, KT // 2) as i:
                for s in range(2):
                    x_tile(i * 2 + s, s)
                    x_square(i * 2 + (s - 1), 1 - s)
            x_square(KT - 1, 1)
            norm_root(act, "mlp")
            modulate_scalar(act, "mlp", gs2, mod1[:, 24:32])

            def ff1_square(c, s, hid, wait_free):
                act.wait_ge(up_done, c * 2 + U_FF1 + s + 3)
                if wait_free:
                    act.wait_ge(sem("ff1_low"), c * 2 + s - 1)
                act.activation(sq[:, s, :], bank2(2 * s), ACT.Relu).then_inc(up_evac, 1)
                act.wait_ge(up_evac, c * 2 + U_FF1 + s + 3)
                act.activation(sq[:, s, :], sq[:, s, :], ACT.Square).then_inc(sem("ff1_sq"), 1)
                act.wait_ge(sem("ff1_sq"), c * 2 + s + 1)
                if wait_free:
                    act.wait_ge(dn_done, c * 16 - 15 + 16 * C_FF1)
                act.activation(hid_h[:, hid, s, :], sq[:, s, :], ACT.Copy).then_inc(sem("ff1_high"), 1)

            for s in range(2):
                ff1_square(0, s, 0, False)
            with act.Fori(0, (CH1 - 2) // 2) as j:
                for e in range(2):
                    for s in range(2):
                        ff1_square(j * 2 + 1 + e, s, 1 - e, True)
            for s in range(2):
                ff1_square(CH1 - 1, s, 1, True)
            for k in range(KT):
                act.wait_ge(dn_evac, 16 * (CH1 - 1) + 2 * k + 4)
                if k >= 3:
                    act.wait_ge(nsem["acc"], 7 * SUMS["final"] + k)
                    act.wait_ge(sem("acc_m"), k - 2)
                act.activation(nsq_fm[:, 2 * (k % 2), :] if k else sq_sum_f[:, :], xt[:, k, :], ACT.Square)
                act.activation(nsq_fm[:, 2 * (k % 2) + 1, :] if k else sq_sum_m[:, :], xt[:, k, :], ACT.Square,
                               scale=vec("final_norm_g", k)).then_inc(nsem["sq"], 1)
            norm_root(act, "final")
            act.wait_ge(sem("ms_m"), 2)
            act.activation(root_m, ms_m, ACT.Sqrt, scale=1.0 / D, bias=eps_rms).then_inc(nsem["root"], 1)
            modulate_scalar(act, "mix2", gs_fm, mod2[:, 0:8])

            def out2(p, m, scale, slot):
                act.wait_ge(up_done, p + (U_WIN2 + 3))
                act.activation(pt2[:, m, :], bank2(2 * slot), ACT.Copy, scale=scale).then_inc(up_evac, 1)

            with act.Fori(0, 3) as i:
                for s in range(2):
                    out2(i * 2 + s, i * 2 + (V2 + s), 1.0, s)
            act.wait_ge(sem("sin_arg"), 1)
            act.activation(sin[:, :], ang[:, :], ACT.Sin).then_inc(sem("rot_tab"), 1)
            act.wait_ge(sem("cos_arg"), 1)
            act.activation(cos[:, :], turn[:, :], ACT.Sin).then_inc(sem("rot_tab"), 1)
            with act.Fori(3, 6) as i:
                for s in range(2):
                    out2(i * 2 + s, i * 2 + (K2 - 6 + s), 1.0, s)
            act.wait_ge(sem("x_moved"), 16)
            for s in range(2):
                out2(12 + s, s, 1.0, s)
            with act.Fori(1, 4) as i:
                for s in range(2):
                    out2(i * 2 + (12 + s), i * 2 + s, SCALE, s)
            for n in range(GROUPS * TT // 4):
                act.wait_ge(sem("v2_turned"), n + 1)
                act.activation(v2[:, 4 * n:4 * n + 4, :], bank2(2 * (n % 2)).rearrange("p (t c) -> p t c", c=256), ACT.Copy
                               ).then_inc(sem("v2_set"), 1)
            for c in range(2):
                act.wait_ge(sem("pool_y"), c + 1)
                act.wait_ge(sem("pool_b"), 1)
                act.activation(pout[:, c, :], bank2(4 + 2 * c), ACT.Identity, scale=vec("pool_scale_2", c),
                               bias=pbias[:, c:c + 1]).then_inc(sem("pout"), 1)
                act.wait_ge(sem("pout"), c + 1)
                act.activation(mix2_h[:, c, :], pout[:, c, :], ACT.Copy).then_inc(sem("mix2_high"), 1)
            for n in range(GROUPS * TT + 1):
                if n < GROUPS * TT:
                    w = keys2(n)
                    act.wait_ge(sem("d_max"), n + 1)
                    for h in range(GH):
                        act.activation(pr2[n % 2][:, h, 0:w], s2[n % 2][:, h, 0:w], ACT.Exp, bias=st2_neg[n % 2][:, h:h + 1],
                                       accum_out=st2_den[n % 4][:, h:h + 1]).then_inc(sem("d_exp"), 1)
                if n >= 1:
                    w = keys2(n - 1) // P * GH
                    act.wait_ge(sem("d_turned"), n)
                    act.activation(pt2t[(n - 1) % 2][:, 0:w, :], bank2(4)[:, 0:w * P].rearrange("p (k q) -> p k q", q=P),
                                   ACT.Copy).then_inc(sem("pt2_set"), 1)
            act.wait_ge(sem("c_diff"), 1)
            act.activation(cw[:, :, :, :], cw[:, :, :, :], ACT.Exp).then_inc(sem("c_exp"), 1)
            for c in range(2):
                act.wait_ge(sem("c_turned"), c + 1)
                act.activation(mix2_h[:, 2 + c, :], bank2(2 * c), ACT.Copy).then_inc(sem("mix2_high"), 1)
            def y_tile(u, s):
                act.wait_ge(up_done, u + (U_WO2 + 3))
                square(act, "post2", u, s, nsq_y, sq_sum_y, bank2(2 * s))
                act.activation(y2[:, u, :], bank2(2 * s), ACT.Copy).then_inc(up_evac, 1)

            for s in range(2):
                y_tile(s, s)
            with act.Fori(1, KT // 2) as i:
                for s in range(2):
                    y_tile(i * 2 + s, s)
            norm_root(act, "post2")
            for k in range(KT):
                act.wait_ge(sem("x2_ready"), k + 1)
                square(act, "ffn2", k, k % 2, nsq, sq_sum, xt[:, k, :])
            norm_root(act, "ffn2")
            modulate_scalar(act, "ffn2", gsf, mod2[:, 24:32])

            def ff2_tile(c, i, hid, wait_free):
                u = c * 4 + U_FF2 + 2 * i
                f = c * 2 + i
                act.wait_ge(up_done, u + 3)
                act.activation(gbuf[:, i, :], bank2(0), ACT.Identity, scale=vec("conv_w_2", f + 44),
                               bias=vec("conv_b_2", f)).then_inc(sem("ff2_gate"), 1)
                act.wait_ge(up_evac, u + 3)
                act.activation(gelu[:, i, :], gbuf[:, i, :], ACT.Gelu_apprx_tanh).then_inc(sem("ff2_gelu"), 1)
                act.wait_ge(up_evac, u + 4)
                if wait_free:
                    act.wait_ge(dn_done, c * 16 - 15 + 16 * C_FF2)
                act.activation(hid_h[:, hid, i, :], gv[:, i, :], ACT.Copy).then_inc(sem("ff2_high"), 1)

            act.wait_ge(sem("x_moved"), 48)
            for i in range(2):
                ff2_tile(0, i, 0, False)
            with act.Fori(0, (CH2 - 1) // 2) as j:
                for e in range(2):
                    for i in range(2):
                        ff2_tile(j * 2 + 1 + e, i, 1 - e, True)
            for k in range(KT):
                act.wait_ge(dn_evac, 16 * (C_FF2 + CH2 - 1) + 2 * k + 4)
                square(act, "out", k, k % 2, nsq, sq_sum, y2[:, k, :])
            norm_root(act, "out")
            for t in range(TT):
                act.wait_ge(sem("o_turned"), t + 1)
                if t >= 2:
                    act.wait_ge(sem(f"stored{t % 2}"), 16 * (t // 2))
                act.activation(otok[:, t % 2, :], bank2(2 * (t % 2)), ACT.Copy).then_inc(sem("o_ready"), 1)

        @block.vector
        def _(dve):
            steps = 0

            def link(ins):
                nonlocal steps
                steps += 1
                ins.then_inc(sem("step"), 1)
                dve.wait_ge(sem("step"), steps)

            dve.wait_ge(sem("vec_turned"), 1)
            dve.tensor_copy(vcol[:, :], PS[:, 7, 0:VEC_TILES * P]).then_inc(sem("vec_set"), 1)
            dve.wait_ge(sem("silu"), 1)
            for b in range(2):
                for k in range(KT):
                    n = b * KT + k
                    dve.wait_ge(sem(f"ada_in{n % 2}"), 16 * (n // 2 + 1))
                    for v in range(2):
                        acc = ada_acc0[:, 2 * b + v, :]
                        c = silu_c[:, v * KT + k:v * KT + k + 1]
                        if k == 0:
                            ins = dve.tensor_scalar(acc, ada_ring0[:, n % 2, :], c, None, ALU.mult)
                        else:
                            dve.wait_ge(*((sem("ada_acc"), n) if v == 0 else (sem("ada_used"), n + 2)))
                            ins = dve.scalar_tensor_tensor(out=acc, in0=ada_ring0[:, n % 2, :], scalar=c, in1=acc,
                                                           op0=ALU.mult, op1=ALU.add)
                        ins.then_inc(sem("ada_acc") if v == 0 else sem("ada_used"), 1)
                    if n == 3:
                        dve.wait_ge(sem("root10"), 1)
                        dve.reciprocal(rstd10, root10).then_inc(sem("rstd10"), 1)
            dve.wait_ge(sem("ada_sum0"), 2)
            dve.tensor_tensor(mod1[:, 0:16], PS[:, 6, 0:16], vec("ada_b", 0, 16), ALU.add).then_inc(sem("mod1"), 1)
            dve.tensor_tensor(modc, PS[:, 6, 16:32], vec("ada_b", 0, 16), ALU.add).then_inc(sem("mod1"), 1)
            dve.wait_ge(sem("mod1"), 2)
            for g, m in ((gs1, mod1), (gsc, modc)):
                dve.scalar_tensor_tensor(out=g, in0=m[:, 8:16], scalar=1.0, in1=vec("norm1_g", 0, 8), op0=ALU.add,
                                         op1=ALU.mult).then_inc(sem("mod1"), 1)
            dve.wait_ge(sem("mod1"), 4)
            dve.wait_ge(sem("xs_set"), TT + CT)
            for k in range(KT + 1):
                if k < KT:
                    for lo, hi, g, m in ((0, SEQ, gs1, mod1), (SEQ, SEQ + CTX, gsc, modc)):
                        dve.tensor_scalar(xs[:, k, lo:hi], xs[:, k, lo:hi], g[:, k:k + 1], m[:, k:k + 1], ALU.mult,
                                          ALU.add).then_inc(sem("hn1"), 1)
                if k >= 1:
                    dve.wait_ge(sem("hn1_high"), k)
                    dve.tensor_tensor(hn1_l[:, k - 1, :], xs[:, k - 1, :], hn1_h[:, k - 1, :].bitcast(F32),
                                      ALU.subtract).then_inc(sem("hn1_low"), 1)
            with dve.Fori(0, 4) as i:
                for s in range(2):
                    dve.wait_ge(sem(f"ada1_in{s}"), i * 16 + 16)
                    dve.wait_ge(sem("ada1_sum"), i * 2 + (s + 1))
                    for k in range(KT):
                        c = silu_c[:, k:k + 1]
                        if k == 0:
                            ins = dve.tensor_scalar(ada_acc1[:, s, :], ada_in1[s][:, 0, :], c, None, ALU.mult)
                        else:
                            dve.wait_ge(sem("ada1_used"), i * 16 + (s * KT + k + 2))
                            ins = dve.scalar_tensor_tensor(out=ada_acc1[:, s, :], in0=ada_in1[s][:, k, :], scalar=c,
                                                           in1=ada_acc1[:, s, :], op0=ALU.mult, op1=ALU.add)
                        ins.then_inc(sem("ada1_used"), 1)
            dve.memset(vpad_edges(0), 0.0).then_inc(sem("padded"), 1)
            dve.memset(vpad_edges(1), 0.0).then_inc(sem("padded"), 1)
            dve.wait_ge(sem("padded"), 2)
            dve.wait_ge(sem("gate"), 1)
            for c in range(2):
                dve.tensor_tensor(vpad[:, c, PADT:PADT + SEQ], pt1[:, 2 + c, :], pt1[:, 4 + c, :], ALU.mult
                                  ).then_inc(sem("padded"), 1)
            dve.wait_ge(sem("padded"), 4)
            for c in range(2):
                dve.tensor_scalar(conv_acc[:, c, :], vpad[:, c, 0:SEQ], vec("conv_dw_w", c), vec("conv_dw_b", c),
                                  ALU.mult, ALU.add).then_inc(sem("taps"), 1)

            def tap(n):
                for c in range(2):
                    dve.wait_ge(sem("taps"), n * 2 + (c - 1))
                    dve.scalar_tensor_tensor(out=conv_acc[:, c, :], in0=vpad[:, c, bass.ds(n, SEQ)],
                                             scalar=vec("conv_dw_w", n * 2 + c), in1=conv_acc[:, c, :],
                                             op0=ALU.mult, op1=ALU.add).then_inc(sem("taps"), 1)

            with dve.Fori(1, 11) as n:
                tap(n)
            dve.wait_ge(sem("ada1_sum"), 8 + 2)
            dve.tensor_tensor(mod1[:, 16:48], PS[:, 7, 0:32], vec("ada_b", 16, 32), ALU.add).then_inc(sem("ada1_mod"), 1)
            with dve.Fori(11, TAPS) as n:
                tap(n)
            dve.wait_ge(sem("ada1_mod"), 1)
            dve.scalar_tensor_tensor(out=gs2, in0=mod1[:, 32:40], scalar=1.0, in1=vec("norm2_g", 0, 8), op0=ALU.add,
                                     op1=ALU.mult).then_inc(sem("gmix"), 1)
            dve.wait_ge(sem("ln_sums"), 1)
            for c in range(2):
                dve.scalar_tensor_tensor(out=conv_acc[:, c, :], in0=bank2(6), scalar=-1.0 / 256, in1=conv_acc[:, c, :],
                                         op0=ALU.mult, op1=ALU.add).then_inc(sem("ln_d"), 1)
            dve.wait_ge(sem("ln_root"), 1)
            dve.reciprocal(ln_r[:, :], ln_r[:, :]).then_inc(sem("ln_rstd"), 1)
            dve.wait_ge(sem("ln_rstd"), 1)
            for c in range(2):
                dve.tensor_tensor(conv_acc[:, c, :], conv_acc[:, c, :], ln_r[:, :], ALU.mult).then_inc(sem("ln_y"), 1)
            for n in range(2):
                dve.wait_ge(sem("four_e"), 2 * n + 2)
                dve.wait_ge(sem("four_done"), 2 * n + 2)
                odd = PS[:, 7 - 2 * n, :]
                dve.tensor_tensor(four_y[:, n, 0:NYQ], four_e[n][:, :], odd, ALU.subtract).then_inc(sem("four_mir"), 1)
                dve.tensor_tensor(four_y[:, n, SEQ - 1:NYQ:-1], four_e[n][:, 1:NYQ], odd[:, 1:NYQ], ALU.add
                                  ).then_inc(sem("four_mir"), 1)
            with dve.Fori(0, PAIRS // 2) as i:
                for s in range(2):
                    n0 = i * 32 + 16 * s
                    dve.wait_ge(sem("bias_set"), i * 10 + 5 * s + 5)
                    for n in range(18):
                        if n < 16:
                            h, t = divmod(n, 8)
                            w = WIN_N[t]
                            e = n % 2
                            bias = tbm[s][:, h, :] if w == 640 else \
                                tb[s][:, h, (WIN_U[t] - 2 * t + 6) * GRID_W:(WIN_U[t] - 2 * t + 6) * GRID_W + w]
                            dve.wait_ge(sem("na_scored"), n0 + n + 1)
                            if n >= 2:
                                dve.wait_ge(sem("na_exp"), i * 64 + 32 * s + 2 * n - 2)
                            carry(dve)
                            scores = bank2(2 * e)
                            dve.tensor_tensor_reduce(sbias[e][:, 0:w], scores[:, 0:w], bias, 1.0, BIG, ALU.add, ALU.max,
                                                     st_m[:, e:e + 1]).then_inc(sem("na_biased"), 1)
                            dve.tensor_reduce(st_m2[:, e:e + 1], scores[:, w:w + CTX], AX.X, ALU.max).then_inc(sem("na_max2"), 1)
                            dve.wait_ge(sem("na_biased"), n0 + (n + 18))
                            dve.wait_ge(sem("na_max2"), n0 + n + 1)
                            dve.tensor_scalar(st_neg[:, e:e + 1], st_m[:, e:e + 1], st_m2[:, e:e + 1], -1.0, ALU.max,
                                              ALU.mult).then_inc(sem("na_max"), 1)
                            dve.wait_ge(sem("na_exp"), i * 64 + (32 * s + 2 * n + 2))
                            dve.tensor_tensor(st_r[:, e:e + 1], st_d[:, e:e + 1], st_d2[:, e:e + 1], ALU.add
                                              ).then_inc(sem("na_den"), 1)
                            dve.wait_ge(sem("na_den"), i * 64 + (32 * s + 2 * n + 1))
                            dve.reciprocal(st_rr[:, e:e + 1], st_r[:, e:e + 1]).then_inc(sem("na_den"), 1)
                            dve.wait_ge(sem("na_den"), i * 64 + (32 * s + 2 * n + 2))
                            dve.tensor_scalar(rdiag[e][:, :], ident, st_rr[:, e:e + 1], None, ALU.mult).then_inc(sem("na_diag"), 1)
                        if n >= 2:
                            h, t = divmod(n - 2, 8)
                            rows = slice(h * DH, (h + 1) * DH)
                            dve.wait_ge(sem("na_pv"), n0 + n - 1)
                            dve.tensor_copy(ao[rows, bass.ds(i * 2 + s, 1), t * P:(t + 1) * P], PS[rows, 6 + n % 2, 0:P].unsqueeze(1)
                                            ).then_inc(sem("na_o"), 1)
            for k in range(KT):
                dve.wait_ge(sem("mix_high"), k + 1)
                src = four_y[:, k, :] if k < 2 else conv_out[:, k - 2, :] if k < 4 else ao[:, k - 4, :]
                dve.tensor_tensor(mix_l[:, k, :], src, mix_h[:, k, :].bitcast(F32), ALU.subtract).then_inc(sem("mix_low"), 1)
            def x_add(u, s):
                dve.wait_ge(up_done, u + (U_WO1 + 3))
                dve.wait_ge(sem("xt_set"), u + 1)
                dve.scalar_tensor_tensor(out=xt[:, u, :], in0=bank2(2 * s), scalar=mod1[:, bass.ds(u + 16, 1)],
                                         in1=xt[:, u, :], op0=ALU.mult, op1=ALU.add).then_inc(up_evac, 1)

            x_add(0, 0)
            x_add(1, 1)
            with dve.Fori(1, KT // 2) as i:
                for s in range(2):
                    x_add(i * 2 + s, s)
                    add_square(dve, "mlp", i * 2 + (s - 1), 1 - s, nsq, sq_sum)
            add_square(dve, "mlp", KT - 1, 1, nsq, sq_sum)
            norm_vector(dve, "mlp")
            modulate_vector(dve, "mlp", xt)

            def ada2_sum(b):
                dve.wait_ge(sem("ada2_in"), b * 16 + 16)
                for k in range(KT):
                    c = silu_c[:, 16 + k:17 + k]
                    if k == 0:
                        ins = dve.tensor_scalar(ada_acc2[:, :], ada_in2[:, 0, :], c, None, ALU.mult)
                    else:
                        dve.wait_ge(sem("ada2_used"), b * KT + (k + 2))
                        ins = dve.scalar_tensor_tensor(out=ada_acc2[:, :], in0=ada_in2[:, k, :], scalar=c,
                                                       in1=ada_acc2[:, :], op0=ALU.mult, op1=ALU.add)
                    ins.then_inc(sem("ada2_used"), 1)

            def ada2_mod(b):
                dve.wait_ge(sem("ada2_sum"), b + 1)
                n = ADA2 // P
                dve.tensor_tensor(mod2[:, bass.ds(b * n, n)], PS[:, 6, 0:n], vec("b_ada_2", b * n, n), ALU.add
                                  ).then_inc(sem("mod2"), 1)

            def ff1_lowhalf(c, s, hid):
                dve.wait_ge(sem("ff1_high"), c * 2 + s + 1)
                dve.tensor_tensor(hid_l[:, hid, s, :], sq[:, s, :], hid_h[:, hid, s, :].bitcast(F32), ALU.subtract
                                  ).then_inc(sem("ff1_low"), 1)

            def ff1_add(c, lo, hi):
                for n in range(lo, hi):
                    m, j = divmod(n, 2)
                    part = xt[:, m, j * HALF:(j + 1) * HALF]
                    dve.wait_ge(dn_done, c * 16 + (16 * C_FF1 + n + 2))
                    dve.scalar_tensor_tensor(out=part, in0=PS[:, 4 + n % 2, :], scalar=mod1[:, 40 + m:41 + m], in1=part,
                                             op0=ALU.mult, op1=ALU.add).then_inc(dn_evac, 1)

            def ff1_step(c, prev, hid):
                ff1_lowhalf(c, 0, hid)
                ff1_lowhalf(c, 1, hid)
                ada2_mod(prev)
                ff1_add(prev, 0, 16)
                ada2_sum(c)

            ada2_sum(0)
            for s in range(2):
                ff1_lowhalf(0, s, 0)
            with dve.Fori(0, (CH1 - 2) // 2) as j:
                for e in range(2):
                    ff1_step(j * 2 + 1 + e, j * 2 + e, 1 - e)
            ff1_step(CH1 - 1, CH1 - 2, 1)
            dve.wait_ge(sem("mod2"), CH1)
            def gain(g, w, c, op):
                dve.scalar_tensor_tensor(out=g, in0=mod2[:, c:c + 8], scalar=1.0, in1=vec(w, 0, 8), op0=op, op1=ALU.mult
                                         ).then_inc(sem("gmix"), 1)

            gain(gsm, "g_pre_mix_2", 8, ALU.add)
            gain(ggm, "g_post_mix_2", 16, ALU.mult)
            gain(gsf, "g_pre_ffn_2", 32, ALU.add)
            dve.wait_ge(sem("gmix"), 4)
            dve.tensor_tensor(gs_fm, gsm, vec("final_norm_g", 0, 8), ALU.mult).then_inc(sem("gmix"), 1)
            for m in range(KT):
                ff1_add(CH1 - 1, 2 * m, 2 * m + 2)
                if m >= 2:
                    add_square(dve, "final", m - 1, (m - 1) % 2 * 2, nsq_fm, sq_sum_f)
            add_square(dve, "final", KT - 1, 2, nsq_fm, sq_sum_f)
            norm_rstd(dve, "final", rstd8, root8)
            dve.tensor_tensor(ms_m, PS[:, 7, TT:2 * TT], rstd8, ALU.mult).then_inc(sem("ms_m"), 1)
            dve.wait_ge(sem("ms_m"), 1)
            dve.tensor_tensor(ms_m, ms_m, rstd8, ALU.mult).then_inc(sem("ms_m"), 1)
            norm_diag(dve, ndiag, rstd8)
            norm_rstd(dve, "mix2", rstd_m, root_m)
            dve.tensor_tensor(rstd_fm, rstd_m, rstd8, ALU.mult).then_inc(sem("ms_m"), 1)
            dve.wait_ge(sem("ms_m"), 3)
            norm_diag(dve, ndiag_m, rstd_fm)
            dve.wait_ge(nsem["bc"], NORMS["mix2"] + 1)
            modulate_vector(dve, "mix2", xt)
            for k in range(KT):
                dve.scalar_tensor_tensor(out=xt[:, k, :], in0=xt[:, k, :], scalar=vec("final_norm_g", k), in1=bank2(4),
                                         op0=ALU.mult, op1=ALU.mult).then_inc(sem("x1_ready"), 1)
            ada2_mod(CH1 - 1)
            dve.wait_ge(sem("mod2"), CH1 + 1)
            gain(ggf, "g_post_ffn_2", 40, ALU.mult)
            dve.wait_ge(sem("pos_in"), 16)
            for part, shift in (("sin", 0.0), ("cos", 0.25)):
                out_arg = ang if part == "sin" else turn
                if part == "cos":
                    dve.wait_ge(sem("rot_tab"), 1)
                link(dve.tensor_copy(ang[:, :], pos[:, :]))
                link(dve.tensor_scalar(ang[:, :], ang[:, :], const("inv_freq"), None, ALU.mult))
                link(dve.tensor_scalar(turn[:, :], ang[:, :], 1.0 / (2 * math.pi), shift, ALU.mult, ALU.add))
                link(dve.tensor_copy(turn_i[:, :], turn[:, :]))
                link(dve.tensor_copy(turn[:, :], turn_i[:, :]))
                for step in two_pi_parts():
                    link(dve.scalar_tensor_tensor(out=ang[:, :], in0=turn[:, :], scalar=-step, in1=ang[:, :], op0=ALU.mult,
                                                  op1=ALU.add))
                if part == "cos":
                    link(dve.tensor_scalar(ang[:, :], ang[:, :], math.pi / 2, None, ALU.add))
                lim = float(np.nextafter(np.float32(math.pi), np.float32(0)))
                dve.tensor_scalar(out_arg[:, :], ang[:, :], lim, -lim, ALU.min, ALU.max).then_inc(sem(part + "_arg"), 1)

            def rotary(r, p, m):
                dve.wait_ge(up_evac, U_WIN2 + p + 3)
                if r:
                    dve.wait_ge(sem("qk2_set"), r)
                dve.tensor_tensor(rt[:, :], pt2[:, m, :], cos[:, :], ALU.mult).then_inc(sem("rot_c"), 1)
                dve.wait_ge(sem("rotated"), r + 1)
                dve.tensor_tensor(rt2[:, :], bank2(4 + 2 * (r % 2)), sin[:, :], ALU.mult).then_inc(sem("rot_s"), 1)
                dve.wait_ge(sem("rot_s"), r + 3)
                dve.wait_ge(sem("rot_c"), r + 1)
                dve.tensor_tensor(pt2[:, m, :], rt[:, :], rt2[:, :], ALU.add).then_inc(sem("qk2_set"), 1)

            dve.wait_ge(sem("rot_tab"), 2)
            for r in range(6):
                rotary(r, 6 + r, K2 + r)
            dve.wait_ge(up_evac, U_WIN2 + 13 + 3)
            dve.tensor_tensor(pbias, vec("b_pool_2", 0, 2), vec("pool_scale_2", 0, 2), ALU.mult).then_inc(sem("pool_b"), 1)
            for c in range(2):
                u = pt2[:, c, :]
                bufs = [ps2, ps4]
                src, lo, lag = u, 0, 1
                for n in range(2 if c == 0 else 4):
                    dst = bufs[n % 2]
                    if c == 0 and n == 1 or c == 1 and n == 3:
                        lo = 64
                        old = bufs[(n - 1) % 2]
                        link(dve.tensor_copy(dst[0:64, :], old[0:64, :]))
                    link(dve.tensor_copy(dst[lo:, 0:lag], src[lo:, 0:lag]))
                    link(dve.tensor_tensor(dst[lo:, lag:], src[lo:, lag:], src[lo:, 0:SEQ - lag], ALU.add))
                    src, lag = dst, 2 * lag
                head = const("pool_head")[:, 16 * c:16 * c + 16]
                link(dve.scalar_tensor_tensor(out=pmix[:, c, :], in0=src[:, :], scalar=const("pool_inv")[:, c:c + 1], in1=u,
                                               op0=ALU.mult, op1=ALU.subtract))
                link(dve.tensor_tensor(pmix[:, c, 0:16], src[:, 0:16], head, ALU.mult))
                dve.tensor_tensor(pmix[:, c, 0:16], pmix[:, c, 0:16], u[:, 0:16], ALU.subtract).then_inc(sem("pmix"), 1)
            for r in range(6, 12):
                rotary(r, 8 + r, Q2 + r - 6)
            for c in range(2):
                dve.wait_ge(sem("mix2_high"), c + 1)
                dve.tensor_tensor(mix2_l[:, c, :], pout[:, c, :], mix2_h[:, c, :].bitcast(F32), ALU.subtract
                                  ).then_inc(sem("mix2_split"), 1)
            for n in range(GROUPS * TT + 2):
                e = n % 2
                if n < GROUPS * TT:
                    w = keys2(n)
                    mask = const("causal16") if n >= 2 * TT else const("causal")[:, 256 - w:]
                    dve.wait_ge(sem("d_scored"), n + 1)
                    if n >= 2:
                        dve.wait_ge(sem("d_exp"), 4 * n - 4)
                    if n >= 4:
                        dve.wait_ge(sem(f"o2_out{n % 4}"), 16 * (n // 4))
                    sc = bank2(2 * e).rearrange("p (h k) -> p h k", h=GH)[:, :, 0:w]
                    dve.tensor_tensor(s2[e][:, :, 0:w], sc, mask.unsqueeze(1).to_broadcast([P, GH, w]), ALU.add
                                      ).then_inc(sem("d_masked"), 1)
                    dve.wait_ge(sem("d_masked"), n + 1)
                    dve.tensor_reduce(og[n % 4][:, GH * DH:GH * DH + GH], s2[e][:, :, 0:w], AX.X, ALU.max).then_inc(sem("d_mx"), 1)
                    dve.wait_ge(sem("d_mx"), n + 1)
                    dve.tensor_scalar(st2_neg[e], og[n % 4][:, GH * DH:GH * DH + GH], -1.0, None, ALU.mult).then_inc(sem("d_max"), 1)
                if n >= 2:
                    j = n - 2
                    dve.wait_ge(sem("d_pv"), j + 1)
                    dve.tensor_copy(og[j % 4][:, 0:GH * DH], PS[:, 6 + j % 2, 0:GH * DH]).then_inc(sem("o2_ready"), 1)
            dve.wait_ge(sem("oall_in"), 16 * GROUPS)
            mx = [oall[:, :, g, GH * DH:GH * DH + GH] for g in range(GROUPS)]
            dn = [oall[:, :, g, GH * DH + GH:] for g in range(GROUPS)]
            link(dve.tensor_tensor(cmax[:, :, :], mx[0], mx[1], ALU.max))
            link(dve.tensor_tensor(cmax[:, :, :], cmax[:, :, :], mx[2], ALU.max))
            for g in range(2):
                link(dve.tensor_tensor(cw[:, :, g, :], mx[g], cmax[:, :, :], ALU.subtract))
            dve.tensor_tensor(cw[:, :, 2, :], mx[2], cmax[:, :, :], ALU.subtract).then_inc(sem("c_diff"), 1)
            dve.wait_ge(sem("c_exp"), 1)
            link(dve.tensor_tensor(cden[:, :, :], cw[:, :, 0, :], dn[0], ALU.mult))
            for g in range(1, GROUPS):
                link(dve.tensor_tensor(cmax[:, :, :], cw[:, :, g, :], dn[g], ALU.mult))
                link(dve.tensor_tensor(cden[:, :, :], cden[:, :, :], cmax[:, :, :], ALU.add))
            link(dve.reciprocal(cden[:, :, :], cden[:, :, :]))
            for g in range(GROUPS):
                link(dve.tensor_tensor(cwn[:, :, g, :].rearrange("p t (a b) -> p t b a", b=2),
                                       cw[:, :, g, :].rearrange("p t (b a) -> p t b a", a=2),
                                       cden[:, :, :].rearrange("p t (b a) -> p t b a", a=2), ALU.mult))
            for half in range(2):
                ts = slice(half * TT // 2, (half + 1) * TT // 2)
                acc, term = csum[:, ts, :, :], cterm[:, ts, :, :]
                for g in range(GROUPS):
                    src = oall[:, ts, g, 0:GH * DH].rearrange("p t (h d) -> p t h d", d=DH)
                    wt = cwn[:, ts, g, :].unsqueeze(3).to_broadcast([P, TT // 2, GH, DH])
                    if g == 0:
                        link(dve.tensor_tensor(acc, src, wt, ALU.mult))
                    else:
                        link(dve.tensor_tensor(term, src, wt, ALU.mult))
                        ins = dve.tensor_tensor(acc, acc, term, ALU.add)
                        if g == 2:
                            ins.then_inc(sem("c_sum"), 1)
                        else:
                            link(ins)
            for c in range(2):
                dve.wait_ge(sem("mix2_high"), 3 + c)
                dve.tensor_tensor(mix2_l[:, 2 + c, :], bank2(2 * c), mix2_h[:, 2 + c, :].bitcast(F32), ALU.subtract
                                  ).then_inc(sem("mix2_split"), 1)
            for k in range(1, KT):
                add_square(dve, "post2", k, k % 2, nsq_y, sq_sum_y)
            norm_vector(dve, "post2")
            dve.wait_ge(sem("x_moved"), 32)
            for k in range(KT):
                dve.scalar_tensor_tensor(out=y2[:, k, :], in0=y2[:, k, :], scalar=ggm[:, k:k + 1], in1=bank2(2), op0=ALU.mult,
                                         op1=ALU.mult).then_inc(sem("y_gated"), 1)
                dve.wait_ge(sem("y_gated"), k + 1)
                dve.tensor_tensor(xt[:, k, :], xt[:, k, :], y2[:, k, :], ALU.add).then_inc(sem("x2_ready"), 1)
            norm_vector(dve, "ffn2")
            modulate_vector(dve, "ffn2", xt)
            dve.memset(y2[:, :, :], 0.0).then_inc(sem("y2_zero"), 1)
            dve.wait_ge(sem("y2_zero"), 1)

            def ff2_gate(c, i):
                u = c * 4 + U_FF2 + 2 * i
                f = c * 2 + i
                dve.wait_ge(sem("ff2_gate"), f + 1)
                dve.scalar_tensor_tensor(out=gbuf[:, i, 1:], in0=bank2(0)[:, 0:SEQ - 1], scalar=vec("conv_w_2", f + 22),
                                         in1=gbuf[:, i, 1:], op0=ALU.mult, op1=ALU.add).then_inc(sem("ff2_tap"), 1)
                dve.wait_ge(sem("ff2_tap"), f + 1)
                dve.scalar_tensor_tensor(out=gbuf[:, i, 2:], in0=bank2(0)[:, 0:SEQ - 2], scalar=vec("conv_w_2", f),
                                         in1=gbuf[:, i, 2:], op0=ALU.mult, op1=ALU.add).then_inc(up_evac, 1)

            def ff2_value(c, i):
                u = c * 4 + U_FF2 + 2 * i + 1
                dve.wait_ge(sem("ff2_gelu"), c * 2 + i + 1)
                dve.wait_ge(up_done, u + 3)
                dve.tensor_tensor(gv[:, i, :], gelu[:, i, :], bank2(2), ALU.mult).then_inc(up_evac, 1)

            def ff2_lowhalf(c, i, hid):
                dve.wait_ge(sem("ff2_high"), c * 2 + i + 1)
                dve.tensor_tensor(hid_l[:, hid, i, :], gv[:, i, :], hid_h[:, hid, i, :].bitcast(F32), ALU.subtract
                                  ).then_inc(sem("ff2_low"), 1)

            def ff2_add(c, lo, hi):
                for n in range(lo, hi):
                    m, j = divmod(n, 2)
                    part = y2[:, m, j * HALF:(j + 1) * HALF]
                    dve.wait_ge(dn_done, c * 16 + (16 * C_FF2 + n + 2))
                    dve.tensor_tensor(part, part, PS[:, 4 + n % 2, :], ALU.add).then_inc(dn_evac, 1)

            for i in range(2):
                ff2_gate(0, i)
                ff2_value(0, i)
                ff2_lowhalf(0, i, 0)
            with dve.Fori(0, (CH2 - 1) // 2) as j:
                for e in range(2):
                    c = j * 2 + 1 + e
                    ff2_gate(c, 0)
                    ff2_value(c, 0)
                    ff2_lowhalf(c, 0, 1 - e)
                    ff2_gate(c, 1)
                    ff2_value(c, 1)
                    ff2_add(j * 2 + e, 0, 4)
                    ff2_lowhalf(c, 1, 1 - e)
                    ff2_add(j * 2 + e, 4, 16)
            for m in range(KT):
                ff2_add(CH2 - 1, 2 * m, 2 * m + 2)
                if m >= 2:
                    add_square(dve, "out", m - 1, (m - 1) % 2, nsq, sq_sum)
            add_square(dve, "out", KT - 1, 1, nsq, sq_sum)
            norm_vector(dve, "out")
            dve.wait_ge(sem("x_moved"), 64)
            for k in range(KT):
                dve.scalar_tensor_tensor(out=y2[:, k, :], in0=y2[:, k, :], scalar=ggf[:, k:k + 1], in1=bank2(2), op0=ALU.mult,
                                         op1=ALU.mult).then_inc(sem("y_gated"), 1)
                dve.wait_ge(sem("y_gated"), KT + k + 1)
                dve.tensor_tensor(xt[:, k, :], xt[:, k, :], y2[:, k, :], ALU.add).then_inc(sem("x3_ready"), 1)

        @block.tensor
        def _(pe):
            pe.wait_ge(sem("tables_in"), 32)
            for t in range(VEC_TILES):
                mm = pe.transpose(PS[:, 7, t * P:(t + 1) * P], vrow[:, t, :], ident)
            mm.then_inc(sem("vec_turned"), 1)
            for t in range(TT + CT):
                pe.wait_ge(sem("x_scaled"), t + 1)
                if t >= 2:
                    pe.wait_ge(sem("xs_set"), t - 1)
                for k in range(KT):
                    mm = pe.transpose(bank2(2 * (t % 2))[:, k * P:(k + 1) * P], xtok[:, t, k * P:(k + 1) * P], ident)
                mm.then_inc(sem("x_turned"), 1)
            pe.wait_ge(sem("ones_set"), 3)
            for b in range(2):
                pe.wait_ge(sem("ada_acc"), KT * (b + 1))
                pe.wait_ge(sem("ada_used"), 2 + KT * (b + 1))
                for v in range(2):
                    for f in range(KT):
                        col = v * 16 + b * 8 + f
                        mm = pe.matmul(PS[:, 6, col:col + 1], ada_acc0[:, 2 * b + v, f * P:(f + 1) * P], ones[:, 0:1],
                                       start=True, stop=True)
                mm.then_inc(sem("ada_sum0"), 1)
            mul_up(pe, 0, 0, hn1_h, hn1_l, ready=lambda k: (sem("hn1_low"), k + 1))
            mul_up(pe, 1, 1, hn1_h, hn1_l)
            with pe.Fori(1, K0 // 2) as i:
                for s in range(2):
                    mul_up(pe, i * 2 + s, s, hn1_h, hn1_l)
                    pe.wait_ge(sem("ada1_used"), i * 16 + (s * KT - 6))
                    for f in range(ADA1 // P):
                        mm = pe.matmul(PS[:, 7, bass.ds(i * 8 + (4 * s + f - 8), 1)], ada_acc1[:, s, f * P:(f + 1) * P],
                                       ones[:, 0:1], start=True, stop=True)
                    mm.then_inc(sem("ada1_sum"), 1)
            for s in range(2):
                mul_up(pe, K0 + s, s, hn1_h, hn1_l, extra=CTX)
            pe.wait_ge(sem("four_in"), 16)
            pe.wait_ge(sem("ada1_mod"), 1)
            for c in range(2):
                pe.matmul(PS[:, 6 + c, 0:256], const("dft_c"), wf[:, c, :], start=True, stop=True)
                pe.matmul(PS[:, 6 + c, 256:512], const("dft_s"), wf[:, c, :], start=True, stop=True
                          ).then_inc(sem("four_w"), 1)
            with pe.Fori(1, 3) as i:
                for s in range(2):
                    mul_up(pe, i * 2 + (K0 + s), s, hn1_h, hn1_l, extra=CTX)
            pe.wait_ge(sem("taps"), 2 * TAPS)
            pe.wait_ge(sem("four_ab"), 2)
            for j in range(2):
                for c in range(2):
                    mm = pe.matmul(PS[:, 6 + j, :], ones[:, :], conv_acc[:, c, j * HALF:(j + 1) * HALF],
                                   start=(c == 0), stop=(c == 1))
            mm.then_inc(sem("ln_sums"), 1)
            mul_up(pe, K0 + 6, 0, hn1_h, hn1_l, extra=CTX)
            pe.wait_ge(sem("ln_sq"), 2)
            for j in range(2):
                for c in range(2):
                    mm = pe.matmul(PS[:, 6 + j, :], ones[:, :], conv_sq[:, c, j * HALF:(j + 1) * HALF],
                                   start=(c == 0), stop=(c == 1))
            mm.then_inc(sem("ln_sums"), 1)
            mul_up(pe, K0 + 7, 1, hn1_h, hn1_l, extra=CTX)
            pe.wait_ge(up_evac, W_IN_TILES + 2)
            for t in range(TT):
                if t >= 2:
                    pe.wait_ge(sem("zf_set"), t - 1)
                for c in range(2):
                    mm = pe.matmul(PS[:, 4 + t % 2, :], pt1[:, c, t * P:(t + 1) * P], four_ab[:, c, :],
                                   start=(c == 0), stop=(c == 1))
                mm.then_inc(sem("four_z"), 1)
            pe.wait_ge(sem("four_in"), 32)
            pe.wait_ge(sem("zf_set"), TT)
            pe.wait_ge(sem("ln_root"), 1)
            for nt in range(2):
                even, odd = PS[:, 6 - 2 * nt, :], PS[:, 7 - 2 * nt, :]
                for tt in range(TT):
                    pe.matmul(even, zf[:, tt, nt * P:(nt + 1) * P], dseq[:, tt, 0:NYQ], start=(tt == 0), stop=(tt == TT - 1))
                for tt in range(TT):
                    mm = pe.matmul(PS[:, nt, 0:1], zf[:, tt, nt * P:(nt + 1) * P], dseq[:, tt, NYQ:NYQ + 1],
                                   start=(tt == 0), stop=(tt == TT - 1))
                mm.then_inc(sem("four_done"), 1)
                for tt in range(TT):
                    mm = pe.matmul(odd, zf[:, tt, 256 + nt * P:256 + (nt + 1) * P], dseq[:, tt, NYQ + 1:],
                                   start=(tt == 0), stop=(tt == TT - 1))
                mm.then_inc(sem("four_done"), 1)
            pe.wait_ge(sem("point_in"), 16)
            pe.wait_ge(sem("conv_s"), 2)
            pe.wait_ge(sem("four_e"), 4)
            for m in range(2):
                for j in range(2):
                    for c in range(2):
                        mm = pe.matmul(PS[:, 2 * m + j, :], pw[:, c, m * P:(m + 1) * P], conv_acc[:, c, j * HALF:(j + 1) * HALF],
                                       start=(c == 0), stop=(c == 1))
                mm.then_inc(sem("conv_pw"), 1)

            pe.wait_ge(sem("conv_done"), 2)
            pe.wait_ge(sem("four_mir"), 4)
            with pe.Fori(0, PAIRS // 2) as i:
                for s in range(2):
                    n0 = i * 32 + 16 * s

                    def scores(n):
                        h, t = divmod(n, 8)
                        w, k0 = WIN_N[t], WIN_U[t] * GRID_W
                        rows = slice(h * DH, (h + 1) * DH)
                        dst = bank2(2 * (n % 2))
                        q = qs[s][rows, t * P:(t + 1) * P]
                        if n >= 2:
                            pe.wait_ge(sem("na_exp"), n0 * 2 + (2 * n - 2))
                        spans = [(0, min(w, HALF), k0), (HALF, w, k0 + HALF), (w, w + CTX, SEQ)]
                        for lo, hi, k in spans:
                            if hi > lo:
                                mm = pe.matmul(dst[:, lo:hi], q, ks[s][rows, k:k + hi - lo], start=True, stop=True)
                        mm.then_inc(sem("na_scored"), 1)

                    def turned(n):
                        pe.wait_ge(sem("na_diag"), n0 + (n + 1))
                        if n:
                            pe.wait_ge(sem("probt_set"), n0 + (n + 1))
                        for c in range((WIN_N[n % 8] + CTX) // P):
                            mm = pe.matmul(bank2(4)[:, c * P:(c + 1) * P], prob[n % 2][:, c * P:(c + 1) * P], rdiag[n % 2][:, :],
                                           start=True, stop=True)
                        mm.then_inc(sem("na_turned"), 1)

                    def values(n):
                        h, t = divmod(n, 8)
                        pe.wait_ge(sem("probt_set"), n0 + (n + 2))
                        if n >= 2:
                            pe.wait_ge(sem("na_o"), n0 + n)
                        tiles = [WIN_U[t] // 2 + c for c in range(WIN_N[t] // P)] + [TT, TT + 1]
                        for c, kt in enumerate(tiles):
                            mm = pe.matmul(PS[h * DH:(h + 1) * DH, 6 + n % 2, 0:P], vt[s][:, kt, h * DH:(h + 1) * DH],
                                           probt[n % 2][:, c * P:(c + 1) * P], start=(c == 0), stop=(c == len(tiles) - 1))
                        mm.then_inc(sem("na_pv"), 1)

                    pe.wait_ge(sem("na_o"), n0 + 1)
                    pe.wait_ge(sem("probt_set"), n0 + 1)
                    pe.wait_ge(sem("staged"), i * 10 + (5 * s + 5))
                    for t in range(TT):
                        mm = pe.transpose(bank2(4)[:, t * P:(t + 1) * P], vs[:, t * P:(t + 1) * P], ident)
                    mm.then_inc(sem("v_turned"), 1)
                    pe.wait_ge(sem("vt_set"), i * 4 + (2 * s + 1))
                    for t in range(CT):
                        mm = pe.transpose(bank2(4)[:, t * P:(t + 1) * P], vs[:, SEQ + t * P:SEQ + (t + 1) * P], ident)
                    mm.then_inc(sem("v_turned"), 1)
                    scores(0)
                    pe.wait_ge(sem("vt_set"), i * 4 + (2 * s + 2))
                    for n in range(16):
                        if n < 15:
                            scores(n + 1)
                        turned(n)
                        if n:
                            values(n - 1)
                    values(15)
            def wo1(u, s, slab, ready=None):
                mul_up(pe, u + U_WO1, s, mix_h, mix_l, ready=ready)
                pe.wait_ge(sem(f"slab_in{s}"), slab)
                if not isinstance(u, int) or u:
                    pe.wait_ge(sem("xt_set"), u)
                for t in range(TT):
                    mm = pe.transpose(bank2(4)[:, t * P:(t + 1) * P], xslab[:, s, t, :], ident)
                mm.then_inc(sem("slab_used"), 1)

            wo1(0, 0, 16, lambda k: (sem("mix_low"), k + 1))
            wo1(1, 1, 16)
            with pe.Fori(1, KT // 2) as i:
                for s in range(2):
                    wo1(i * 2 + s, s, i * 16 + 16)
            add_sums(pe, "mlp", sq_sum)
            norm_spread(pe, "mlp", ndiag, 2)

            def split_tile(n):
                return lambda k: (nsem["low"], KT * MODULATED[n] + k + 1)

            def ff1_up(c, ready=None):
                for s in range(2):
                    mul_up(pe, c * 2 + (U_FF1 + s), s, hn_h, hn_l, ready=None if s else ready)

            def ff1_dn(c, hid):
                pe.wait_ge(sem("ff1_low"), c * 2 + 2)
                mul_dn(pe, c * 2 + 2 * C_FF1, hid, c * 16 + 16 * C_FF1)

            def ada2_reduce(b):
                pe.wait_ge(sem("ada2_used"), b * KT + (2 + KT))
                pe.wait_ge(sem("mod2"), b + 1)
                for f in range(ADA2 // P):
                    mm = pe.matmul(PS[:, 6, f:f + 1], ada_acc2[:, f * P:(f + 1) * P], ones[:, 0:1], start=True, stop=True)
                mm.then_inc(sem("ada2_sum"), 1)

            ff1_up(0, split_tile("mlp"))
            with pe.Fori(0, (CH1 - 2) // 2) as j:
                for e in range(2):
                    ff1_up(j * 2 + 1 + e)
                    ada2_reduce(j * 2 + e)
                    ff1_dn(j * 2 + e, e)
            ff1_up(CH1 - 1)
            ada2_reduce(CH1 - 2)
            ff1_dn(CH1 - 2, 0)

            ff1_dn(CH1 - 1, 1)
            pe.wait_ge(nsem["acc"], 7 * SUMS["final"] + 9)
            pe.wait_ge(sem("acc_m"), KT - 1)
            for j, acc in enumerate((sq_sum_f, sq_sum_m)):
                for t in range(TT):
                    mm = pe.matmul(PS[:, 7, j * TT + t:j * TT + t + 1], acc[:, t * P:(t + 1) * P], ones[:, 0:1],
                                   start=True, stop=True)
            mm.then_inc(nsem["sums"], 1)
            norm_spread(pe, "final", ndiag, 4)
            norm_spread(pe, "mix2", ndiag_m, 2)
            def win2(p, s, ready=None):
                mul_up(pe, p + U_WIN2, s, hn_h, hn_l, ready=ready)

            def rotate(r, p, m, s):
                pe.wait_ge(up_evac, p + (U_WIN2 + 3))
                pe.wait_ge(sem("rot_s"), r + 1)
                for j in range(2):
                    mm = pe.matmul(PS[:, 4 + 2 * s + j, :], const("rotate"), pt2[:, m, j * HALF:(j + 1) * HALF],
                                   start=True, stop=True)
                mm.then_inc(sem("rotated"), 1)

            win2(0, 0, split_tile("mix2"))
            win2(1, 1)
            ada2_reduce(CH1 - 1)
            with pe.Fori(1, 4) as i:
                for s in range(2):
                    win2(i * 2 + s, s)
            pe.wait_ge(sem("x1_ready"), KT)
            pe.wait_ge(sem("mod2"), CH1 + 1)
            with pe.Fori(4, 7) as i:
                win2(i * 2, 0)
                for s in range(2):
                    rotate(i * 2 + (s - 8), i * 2 + (s - 2), i * 2 + (K2 - 8 + s), s)
                win2(i * 2 + 1, 1)
            for s in range(2):
                win2(14 + s, s)
            with pe.Fori(8, 10) as i:
                win2(i * 2, 0)
                for s in range(2):
                    rotate(i * 2 + (s - 10), i * 2 + (s - 2), i * 2 + (Q2 - 16 + s), s)
                win2(i * 2 + 1, 1)
            pe.wait_ge(up_evac, U_WIN2 + W_IN2_TILES + 1)
            for n in range(GROUPS * TT // 4):
                if n == 1:
                    pe.wait_ge(up_evac, U_WIN2 + W_IN2_TILES + 2)
                    for s in range(2):
                        rotate(10 + s, 18 + s, Q2 + 4 + s, s)
                if n >= 2:
                    pe.wait_ge(sem("v2_set"), n - 1)
                for gb in range(4 * n, 4 * n + 4):
                    g, b = divmod(gb, TT)
                    for hp in range(2):
                        lo = gb % 4 * 256 + hp * P
                        mm = pe.transpose(bank2(2 * (n % 2))[:, lo:lo + P], perm(pt2[:, V2 + 2 * g + hp, :], g, b), ident)
                mm.then_inc(sem("v2_turned"), 1)
            pe.wait_ge(sem("point_in"), 32)
            for c in range(2):
                pe.wait_ge(sem("pmix"), c + 1)
                pe.wait_ge(sem("rot_s"), 10 + c + 3)
                for j in range(2):
                    mm = pe.matmul(PS[:, 4 + 2 * c + j, :], wp[:, c, :], pmix[:, c, j * HALF:(j + 1) * HALF], start=True, stop=True)
                mm.then_inc(sem("pool_y"), 1)

            pe.wait_ge(sem("v2_set"), GROUPS * TT // 4)

            def d_blocks(n):
                g, b = divmod(n, TT)
                return [b - (1 if g == 0 else 4), b] if keys2(n) == 256 else [b]

            def d_scores(n):
                g, b = divmod(n, TT)
                if b == 0:
                    pe.wait_ge(sem("qk2_set"), 8 + 2 * g)
                if n >= 2:
                    pe.wait_ge(sem("d_masked"), n - 1)
                for j, h in enumerate(HEAD_AT):
                    rows = slice(DH * (h % 2), DH * (h % 2) + DH)
                    q = perm(pt2[rows, Q2 + 2 * g + h // 2, :], g, b)
                    k = pt2[rows, K2 + 2 * g + h // 2, :]
                    for c, kb in enumerate(d_blocks(n)):
                        lo = j * 256 + c * P
                        mm = pe.matmul(bank2(2 * (n % 2))[:, lo:lo + P], q, perm(k, g, kb),
                                       start=True, stop=True)
                mm.then_inc(sem("d_scored"), 1)

            def d_turned(n):
                nk = keys2(n) // P
                pe.wait_ge(sem("d_exp"), GH * (n + 1))
                if n:
                    pe.wait_ge(sem("pt2_set"), n)
                else:
                    pe.wait_ge(sem("pout"), 2)
                for j in range(GH):
                    for c in range(nk):
                        lo = (j * nk + c) * P
                        mm = pe.matmul(bank2(4)[:, lo:lo + P], pr2[n % 2][:, j, c * P:(c + 1) * P], ident, start=True, stop=True)
                mm.then_inc(sem("d_turned"), 1)

            def d_values(n):
                g, b = divmod(n, TT)
                blocks = d_blocks(n)
                pe.wait_ge(sem("pt2_set"), n + 1)
                if n >= 2:
                    pe.wait_ge(sem("o2_ready"), n - 1)
                for j, h in enumerate(HEAD_AT):
                    for c, kb in enumerate(blocks):
                        mm = pe.matmul(PS[:, 6 + n % 2, h * DH:(h + 1) * DH], pt2t[n % 2][:, j * len(blocks) + c, :],
                                       v2[:, g * TT + kb, h * DH:(h + 1) * DH], start=(c == 0), stop=(c == len(blocks) - 1))
                mm.then_inc(sem("d_pv"), 1)

            d_scores(0)
            for n in range(GROUPS * TT):
                if n + 1 < GROUPS * TT:
                    d_scores(n + 1)
                d_turned(n)
                if n:
                    d_values(n - 1)
            d_values(GROUPS * TT - 1)
            pe.wait_ge(sem("c_sum"), 2)
            for c in range(2):
                for t in range(TT):
                    mm = pe.transpose(bank2(2 * c)[:, t * P:(t + 1) * P], csum[:, t, 2 * c:2 * c + 2, :].rearrange("p h d -> p (h d)"), ident)
                mm.then_inc(sem("c_turned"), 1)
            pe.wait_ge(sem("mix2_split"), 4)
            for s in range(2):
                mul_up(pe, U_WO2 + s, s, mix2_h, mix2_l, kt=4)
            with pe.Fori(1, KT // 2) as i:
                for s in range(2):
                    mul_up(pe, i * 2 + (U_WO2 + s), s, mix2_h, mix2_l, kt=4)
            add_sums(pe, "post2", sq_sum_y)
            norm_spread(pe, "post2", ndiag, 2)
            add_sums(pe, "ffn2", sq_sum)
            norm_spread(pe, "ffn2", ndiag, 2)

            def ff2_up(c, ready=None):
                for i in range(4):
                    mul_up(pe, c * 4 + (U_FF2 + i), i % 2, hn_h, hn_l, ready=None if i else ready)

            def ff2_dn(c, hid):
                pe.wait_ge(sem("ff2_low"), c * 2 + 2)
                mul_dn(pe, c * 2 + 2 * C_FF2, hid, c * 16 + 16 * C_FF2)

            ff2_up(0, split_tile("ffn2"))
            with pe.Fori(0, (CH2 - 1) // 2) as j:
                ff2_up(j * 2 + 1)
                ff2_dn(j * 2, 0)
                ff2_up(j * 2 + 2)
                ff2_dn(j * 2 + 1, 1)
            ff2_dn(CH2 - 1, 0)
            add_sums(pe, "out", sq_sum)
            norm_spread(pe, "out", ndiag, 2)
            pe.wait_ge(sem("x3_ready"), KT)
            for t in range(TT):
                if t >= 2:
                    pe.wait_ge(sem("o_ready"), t - 1)
                for k in range(KT):
                    mm = pe.transpose(bank2(2 * (t % 2))[:, k * P:(k + 1) * P], xt[:, k, t * P:(t + 1) * P], ident)
                mm.then_inc(sem("o_turned"), 1)


_INS = ["x", "ctx", "ada_w", "w_in", "w_fourier", "conv_pw_w", "w_out", "mlp_w1", "mlp_w2", "w_ada_2", "w_in_2",
        "w_out_2", "w_up_2", "w_down_2"]


def kernel(**inputs):
    import concourse.bacc as bacc
    from concourse.bass_utils import run_bass_kernel_spmd

    arr = {n: np.asarray(v) for n, v in inputs.items()}
    data = {n: np.ascontiguousarray(arr[n].reshape(arr[n].shape[-2:])) for n in _INS}
    data["positions_2"] = np.ascontiguousarray(arr["positions_2"].reshape(1, SEQ))
    vecs = np.zeros((VEC_TILES * P, P), np.float32)
    for name, rows in VECS:
        vecs[VROW[name]:VROW[name] + rows] = arr[name].reshape(rows, P)
    data["vecs"] = vecs
    rpb = np.zeros(2 * RPB_PAD + arr["na_rpb"].size, np.float32)
    rpb[RPB_PAD:-RPB_PAD] = arr["na_rpb"].ravel()
    data["rpb"] = rpb
    wp = np.zeros((2, P, P), np.float32)
    for g in range(4):
        lo = g % 2 * DH
        wp[g // 2, lo:lo + DH, lo:lo + DH] = arr["w_pool_2"].reshape(4, DH, DH)[g]
    data["w_pool"] = wp
    data["consts"] = constants()
    data["dft_seq"] = dft_seq()

    nc = bacc.Bacc("TRN2", target_bir_lowering=False, num_devices=1)
    aps = {n: nc.dram_tensor(n, v.shape, mybir.dt.from_np(v.dtype), kind="ExternalInput").ap() for n, v in data.items()}
    out = nc.dram_tensor("out", [SEQ, D], F32, kind="ExternalOutput").ap()
    bass_two_blocks(nc, aps, out)
    r = run_bass_kernel_spmd(nc, [data], core_ids=[0])
    return r.results[0]["out"].reshape(1, SEQ, D)
```

```python
import math
from contextlib import ExitStack

import numpy as np

import concourse.bass as bass
from concourse import mybir

F32 = mybir.dt.float32
F32R = mybir.dt.float32r
I32 = mybir.dt.int32
ACT = mybir.ActivationFunctionType
ALU = mybir.AluOpType
AX = mybir.AxisListType

P = 128
SEQ = 1024
D = 1024
KT = D // P
TT = SEQ // P
CTX = 256
CT = CTX // P
HALF = 512
GRID_W = 64
HEADS = 8
PAIRS = HEADS // 2
DH = 64
SCALE = DH ** -0.5
D_FF = 4 * D
RMS_EPS = 1e-6
LN_EPS = 1e-5
TAPS = 31
PADT = TAPS // 2
D_IN = 2304
W_IN_TILES = D_IN // P
Q0, K0, V0 = 6, 10, 14
RPB_ROWS, RPB_COLS = 15, 31
RPB_PAD = 64
RPB_LEN = HEADS * RPB_ROWS * RPB_COLS + 2 * RPB_PAD
BIAS_ROWS = 14
BIG = -1e30

D_IN2 = 2560
W_IN2_TILES = D_IN2 // P
Q2, K2, V2 = 2, 8, 14
GROUPS = 3
GH = 4
HEAD_AT = [0, 2, 1, 3]
D_FF2 = 2816
FF2_TILES = D_FF2 // P
ROT = 16
THETA = 500000.0

ADA1 = 512
ADA2 = 6 * D // (D_FF // 256)

VECS = [("ada_b", 48), ("b_ada_2", 48), ("norm1_g", 8), ("norm2_g", 8), ("final_norm_g", 8),
        ("g_pre_mix_2", 8), ("g_post_mix_2", 8), ("g_pre_ffn_2", 8), ("g_post_ffn_2", 8),
        ("c", 8), ("c_ctx", 8), ("c_2", 8), ("conv_dw_w", 62), ("conv_dw_b", 2), ("conv_norm_g", 2),
        ("conv_norm_b", 2), ("conv_pw_b", 2), ("b_pool_2", 2), ("pool_scale_2", 2),
        ("conv_w_2", 66), ("conv_b_2", 22)]
VROW = {}
_n = 0
for _name, _rows in VECS:
    VROW[_name] = _n
    _n += _rows
VEC_TILES = -(-_n // P)

CONSTS = [("ident", 128), ("col_mask", 64), ("causal", 256), ("causal16", 128),
          ("dft_c", 128), ("dft_s", 128), ("inv_freq", 1), ("inv_signed", 1), ("pool_inv", 2), ("pool_head", 32)]
CCOL = {}
_n = 0
for _name, _cols in CONSTS:
    CCOL[_name] = (_n, _cols)
    _n += _cols
N_CONST = _n


def constants():
    out = np.zeros((P, N_CONST), np.float32)

    def put(name, a):
        c, n = CCOL[name]
        out[:, c:c + n] = a

    put("ident", np.eye(P))
    col = np.arange(GRID_W)
    start = np.clip(col - 8, 0, GRID_W - 16)
    ok = (col[None] >= start[:, None]) & (col[None] < start[:, None] + 16)
    put("col_mask", np.tile(np.where(ok, 0.0, BIG), (2, 1)))
    i = np.arange(P)[:, None]
    j = np.arange(P)[None]
    put("causal", np.concatenate([np.where(j >= i, 0.0, BIG), np.where(j <= i, 0.0, BIG)], 1))
    put("causal16", np.where((j <= i) & ((i - j) % 2 == 0), 0.0, BIG))
    inv = np.zeros((P, 1), np.float32)
    signed = np.zeros((P, 1), np.float32)
    f = np.float32(THETA) ** (-np.arange(0, ROT, 2, dtype=np.float32) / np.float32(ROT))
    for h in range(2):
        for a in range(ROT // 2):
            lo, hi = h * DH + a, h * DH + a + ROT // 2
            inv[lo] = inv[hi] = f[a]
            signed[lo], signed[hi] = -f[a], f[a]
    put("inv_freq", inv)
    put("inv_signed", signed)
    k = np.arange(64)
    ang = 2 * np.pi * ((k[:, None] * k[None]) % 64) / 64
    norm = 1.0 / math.sqrt(SEQ * 64)
    for name, m in (("dft_c", np.cos(ang)), ("dft_s", np.sin(ang))):
        bd = np.zeros((P, P))
        bd[:64, :64] = bd[64:, 64:] = m * norm
        put(name, bd)
    win = np.array([[2, 8], [4, 16]])[np.arange(P) // 64]
    put("pool_inv", 1.0 / win)
    t = np.arange(16)
    put("pool_head", (1.0 / np.minimum(t[None, None] + 1, win[:, :, None])).reshape(P, 32))
    return out


NYQ = SEQ // 2


def dft_seq():
    t = np.arange(SEQ)
    s = np.arange(NYQ + 1)
    ang = 2 * np.pi * ((t[:, None] * s[None]) % SEQ) / SEQ
    return np.concatenate([np.cos(ang), np.sin(ang[:, :NYQ])], 1).astype(np.float32)


WIN_U = [0, 0, 0, 2, 4, 6, 8, 8]
WIN_N = [512, 512, 640, 640, 640, 640, 512, 512]
V_STEP = 7


def perm(ap, g, b):
    if g == 0:
        return ap[:, b * P:(b + 1) * P]
    if g == 1:
        return ap.rearrange("p (n i r) -> p n r i", n=2, r=4)[:, b // 4, b % 4]
    return ap.rearrange("p (k r) -> p r k", r=8)[:, b]


def two_pi_parts():
    parts, rest = [], 2 * math.pi
    for _ in range(3):
        e = 2.0 ** (math.floor(math.log2(rest)) - 7)
        parts.append(math.floor(rest / e) * e)
        rest -= parts[-1]
    return parts + [rest]


def bass_two_blocks(nc, a, out):
    with ExitStack() as ctx:
        base = -(-nc.sbuf_base // 32) * 32

        def at(name, kb, shape, dt=F32):
            return nc.alloc_sbuf_tensor_at("b_" + name, shape, dt, offset=base + int(kb * 1024))

        sems = {}

        def sem(name):
            if name not in sems:
                sems[name] = ctx.enter_context(nc.semaphore("s_" + name))
            return sems[name]

        PS = ctx.enter_context(nc.psum_tensor("ps_all", [P, 8, HALF], F32))

        def bank2(b):
            return PS[:, b:b + 2, :].rearrange("p b n -> p (b n)")

        vcol = at("vcol", 0, [P, VEC_TILES * P])
        cst = at("cst", 1.5, [P, N_CONST])
        ones = at("ones", 5.5, [P, P])
        sm = [at("small0", 6, [P, 256]), at("small1", 207, [P, 200])]
        w_raw = at("w_raw", 183, [P, 2, 1024])
        up_h = at("up_h", 191, [P, 2, 1024], F32R)
        up_l = at("up_l", 199, [P, 2, 1024], F32R)
        dn_h = at("dn_h", 71, [P, 2, 1024], F32R)
        dn_l = at("dn_l", 79, [P, 2, 1024], F32R)

        def vec(name, t=0, n=1):
            return vcol[:, bass.ds(t + VROW[name], n)]

        def const(name):
            c, n = CCOL[name]
            return cst[:, c:c + n]

        ident = const("ident")
        small_at = [0, 0]

        def small(n):
            i = 0 if small_at[0] + n <= 256 else 1
            small_at[i] += n
            return sm[i][:, small_at[i] - n:small_at[i]]

        mod1, modc, mod2 = small(48), small(16), small(48)
        silu_c = small(24)
        gs1, gsc, gs2, gsm, gsf, ggm, ggf = (small(8) for _ in range(7))
        ss10, root10, rstd10 = small(10), small(10), small(10)
        root8, rstd8 = small(8), small(8)
        ms_m, root_m, rstd_m, rstd_fm, gs_fm = (small(8) for _ in range(5))
        pbias = small(2)
        st_m, st_m2, st_neg, st_d, st_d2, st_r = (small(2) for _ in range(6))

        hn1_h = at("hn1_h", 87, [P, KT, SEQ + CTX], F32R)
        hn1_l = at("hn1_l", 127, [P, KT, SEQ + CTX], F32R)
        xtok = at("xtok", 127, [P, TT + CT, D])
        xs = at("xs", 7, [P, KT, SEQ + CTX])
        ada_acc0 = at("ada_acc0", 49, [P, 2, 1024])
        xdiag = at("xdiag", 57, [P, TT + CT, P])
        ada_rows = at("ada_rows", 63, [P, 1024])
        junk = at("junk", 71, [P, 2, 1024])
        vrow = at("vrow", 69, [P, VEC_TILES, P])
        ada_shift = [at("ada_shift0", 119, [P, 2, 1024]), at("ada_shift1", 167, [P, 2, 1024])]
        ada_scale = at("ada_scale", 87, [P, KT, 1024])
        ada_in1 = [at(f"ada_in1{s}", 47 + 16 * s, [P, KT, ADA1]) for s in range(2)]
        ada_acc1 = at("ada_acc1", 167, [P, 2, ADA1])
        vpad = at("vpad", 173, [P, 2, SEQ + 2 * PADT])
        pt1 = at("pt1", 7, [P, W_IN_TILES, SEQ])
        ckv = at("ckv", 79, [P, 2 * PAIRS, CTX])
        conv_out = at("conv_out", 15, [P, 2, SEQ])
        conv_sq = conv_out
        conv_acc = at("conv_acc", 23, [P, 2, SEQ])
        pw = at("pw", 177, [P, 2, 256])
        ln_r = at("ln_r", 173, [P, SEQ])
        four_y = at("four_y", 7, [P, 2, SEQ])
        dseq = at("dseq", 87, [P, TT, 2 * NYQ + 1])
        zf = at("zf", 119.875, [P, TT, HALF])
        four_ab = at("four_ab", 167, [P, 2, HALF])
        wf = at("wf", 171, [P, 2, 256])
        four_e = [at("four_e0", 169, [P, HALF]), at("four_e1", 136.5, [P, HALF])]
        qs = [at(f"qs{s}", 87 + 4 * s, [P, SEQ]) for s in range(2)]
        ks = [at(f"ks{s}", 95 + 5 * s, [P, SEQ + CTX]) for s in range(2)]
        vs = at("vs", 105, [P, SEQ + CTX])
        prob = [at(f"prob{s}", 110 + 3.5 * s, [P, 896]) for s in range(2)]
        sbias = [at(f"sbias{s}", 117 + 2.5 * s, [P, 640]) for s in range(2)]
        probt = [at(f"probt{s}", 122 + 3.5 * s, [P, 896]) for s in range(2)]
        vt = [at(f"vt{s}", 129 + 5 * s, [P, TT + CT, P]) for s in range(2)]
        tb = [at(f"tb{s}", 139 + 7 * s, [P, 2, BIAS_ROWS * GRID_W]) for s in range(2)]
        tbm = [at(f"tbm{s}", 153 + 5 * s, [P, 2, 640]) for s in range(2)]
        ao = at("ao", 163, [P, PAIRS, SEQ])
        rdiag = [at(f"rdiag{s}", 179 + 0.5 * s, [P, P]) for s in range(2)]
        mix_h = at("mix_h", 39, [P, KT, SEQ], F32R)
        mix_l = at("mix_l", 87, [P, KT, SEQ], F32R)
        xslab = at("xslab", 119, [P, 2, TT, P])
        xt = at("xt", 7, [P, KT, SEQ])
        hn_h = at("hn_h", 119, [P, KT, SEQ], F32R)
        hn_l = at("hn_l", 151, [P, KT, SEQ], F32R)
        hid_h = at("hid_h", 39, [P, 2, 2, SEQ], F32R)
        hid_l = at("hid_l", 55, [P, 2, 2, SEQ], F32R)
        nsq = at("nsq", 175, [P, 2, SEQ])
        nsq_fm = at("nsq_fm", 167, [P, 4, SEQ])
        nsq_y = at("nsq_y", 119, [P, 2, SEQ])
        sq_sum = at("sq_sum", 171, [P, SEQ])
        sq_sum_y = at("sq_sum_y", 127, [P, SEQ])
        sq_sum_f = at("sq_sum_f", 159, [P, SEQ])
        sq_sum_m = at("sq_sum_m", 163, [P, SEQ])
        ndiag_m = at("ndiag_m", 59, [P, SEQ])
        ndiag = at("ndiag", 47, [P, SEQ])
        nhn = at("nhn", 51, [P, 2, SEQ])
        sq = at("sq", 87, [P, 2, SEQ])
        ada_in2 = at("ada_in2", 95, [P, KT, ADA2])
        ada_acc2 = at("ada_acc2", 107, [P, ADA2])
        pt2 = at("pt2", 7, [P, W_IN2_TILES, SEQ])
        cos = at("cos", 87, [P, SEQ])
        sin = at("sin", 91, [P, SEQ])
        pos = at("pos", 95, [P, SEQ], I32)
        ang = at("ang", 99, [P, SEQ])
        turn = at("turn", 103, [P, SEQ])
        turn_i = at("turn_i", 107, [P, SEQ], I32)
        rt = at("rt", 95, [P, SEQ])
        rt2 = at("rt2", 99, [P, SEQ])
        ps2 = at("pools2", 103, [P, SEQ])
        ps4 = at("pools4", 107, [P, SEQ])
        pmix = at("pmix", 111, [P, 2, SEQ])
        pout = at("pout", 103, [P, 2, SEQ])
        wp = at("wp", 175, [P, 2, P])
        v2 = at("v2", 119, [P, GROUPS * TT, 256])
        s2 = [at(f"sc2{s}", 143 + 4 * s, [P, GH, 256]) for s in range(2)]
        pr2 = [at(f"pr2{s}", 151 + 4 * s, [P, GH, 256]) for s in range(2)]
        pt2t = [at(f"pt2t{s}", 159 + 4 * s, [P, 8, P]) for s in range(2)]
        ROWW = GH * DH + 2 * GH
        OG = 6
        og = [at(f"og{s}", 87 + 1.0625 * s, [P, ROWW]) for s in range(OG)]
        oall = at("oall", 93.5, [P, TT, GROUPS, ROWW])
        cw = at("cw", 15, [P, TT, GROUPS, GH])
        cmax = at("cmax", 15.5, [P, TT, GH])
        cwn = at("cwn", 32, [P, TT, GROUPS, GH])
        cden = at("cden", 15.75, [P, TT, GH])
        csum = at("csum", 16, [P, TT, GH, DH])
        cterm = at("cterm", 24, [P, TT, GH, DH])
        mix2_h = at("mix2_h", 69, [P, 4, SEQ], F32R)
        mix2_l = at("mix2_l", 167, [P, 4, SEQ], F32R)
        y2 = at("y2", 87, [P, KT, SEQ])
        gbuf = at("gbuf", 7, [P, 2, SEQ])
        gelu = at("gelu", 15, [P, 2, SEQ])
        gv = at("gv", 23, [P, 2, SEQ])
        otok = at("otok", 119, [P, 2, D])

        st2_neg = [small(GH), small(GH)]
        st2_den = [x[:, GH * DH + GH:] for x in og]

        def keys2_of(g, b):
            return 256 if (g == 0 and b) or (g == 1 and b >= 4) else P

        D_ORDER = [divmod(n, TT) for n in range(GROUPS * TT)]
        D_FIRST = [min(n for n, (h, b) in enumerate(D_ORDER) if h == g) for g in range(GROUPS)]
        D_LAST = [max(n for n, (h, b) in enumerate(D_ORDER) if h == g) for g in range(GROUPS)]

        def keys2(n):
            return keys2_of(*D_ORDER[n])

        POOL_AT = (1, 3)
        C_SPLIT = 6

        def c_group(g, ts):
            return (oall[:, ts, g, 0:GH * DH].rearrange("p t (h d) -> p t h d", d=DH),
                    cwn[:, ts, g, :].unsqueeze(3).to_broadcast([P, ts.stop - ts.start, GH, DH]))

        st_rr = small(4)

        def vpad_edges(side):
            lo = 0 if side == 0 else PADT + SEQ
            return vpad[:, :, lo:lo + PADT]

        o_rows = nc.dram_tensor("o_rows", [GROUPS, SEQ, ROWW], F32, kind="Internal").ap()
        rpb_rows = nc.dram_tensor("rpb_rows", [GRID_W, RPB_LEN], F32, kind="Internal").ap()
        xt_spill = nc.dram_tensor("xt_spill", [2, P, KT, SEQ], F32, kind="Internal").ap()

        U_G2, U_WO1 = 0, W_IN_TILES
        U_FF1 = U_WO1 + KT
        CH1 = D_FF // (2 * P)
        U_WIN2 = U_FF1 + 2 * CH1
        U_WO2 = U_WIN2 + W_IN2_TILES
        U_FF2 = U_WO2 + KT
        CH2 = FF2_TILES // 2
        C_FF1, C_FF2 = 0, CH1

        w_in = a["w_in"]
        raw_in = [sem("raw_in0"), sem("raw_in1")]
        up_full, dn_full = sem("up_full"), sem("dn_full")
        up_done = sem("up_done")
        up_evac = sem("up_evac")
        dn_done, dn_evac = sem("dn_done"), sem("dn_evac")
        raw_split = sem("raw_high")

        def up_src(w, col, kt=KT):
            return w.rearrange("(k p) f -> p k f", p=P)[:, :, col]

        block = ctx.enter_context(nc.Block())

        def carry(eng):
            eng.sem_inc(sem("carried"), 1)

        def load_up(sp, u, w, m, slot, raw_n, kt=KT, dn_before=None):
            sp.wait_ge(up_full, u + 1)
            if dn_before is not None:
                carry(sp)
                sp.wait_ge(dn_full, dn_before)
            carry(sp)
            sp.dma_start(w_raw[:, slot, 0:kt * P].rearrange("p (k f) -> p k f", k=kt),
                         up_src(w, bass.ts(m, P))).then_inc(raw_in[slot], 16)

        def load_dn(sp, d, w, row, slot, u_before):
            sp.wait_ge(up_full, u_before)
            carry(sp)
            sp.dma_start(w_raw[:, slot, :], w[bass.ts(row, P), :]).then_inc(raw_in[slot], 16)

        def split_up(pool, u, slot, raw_n, n_split, kt=KT):
            n = kt * P
            pool.wait_ge(raw_in[slot], 16 * raw_n)
            pool.wait_ge(up_done, u + 1)
            carry(pool)
            pool.tensor_scalar(up_h[:, slot, 0:n], w_raw[:, slot, 0:n], 0.0, 1.0, ALU.add,
                               ALU.mult).then_inc(raw_split, 1)
            pool.wait_ge(raw_split, n_split)
            pool.tensor_tensor(up_l[:, slot, 0:n], w_raw[:, slot, 0:n],
                               up_h[:, slot, 0:n].bitcast(F32), ALU.subtract).then_inc(up_full, 1)

        def split_dn(pool, d, slot, raw_n, n_split, units_before, up_before=None):
            high, low = (dn_h, dn_l) if up_before is None else (up_h, up_l)
            pool.wait_ge(raw_in[slot], 16 * raw_n)
            if up_before is None:
                pool.wait_ge(dn_done, units_before + 1)
            else:
                pool.wait_ge(up_done, up_before + 3)
            carry(pool)
            pool.tensor_scalar(high[:, slot, :], w_raw[:, slot, :], 0.0, 1.0, ALU.add,
                               ALU.mult).then_inc(raw_split, 1)
            pool.wait_ge(raw_split, n_split)
            pool.tensor_tensor(low[:, slot, :], w_raw[:, slot, :],
                               high[:, slot, :].bitcast(F32), ALU.subtract).then_inc(dn_full, 1)

        def mul_up(pe, u, slot, xh, xl, kt=KT, extra=None, ready=None, ks=None):
            pe.wait_ge(up_full, u + 3)
            pe.wait_ge(up_evac, u + 1)
            spans = [(PS[:, 2 * slot + j, :], j * HALF, HALF) for j in range(2)]
            if extra:
                spans.append((PS[:, 4 + slot, 0:extra], SEQ, extra))
            ks = ks or range(kt)
            for k in ks:
                if ready:
                    pe.wait_ge(*ready(k))
                for n, (w, x) in enumerate(((up_h, xh), (up_h, xl), (up_l, xh))):
                    for dst, c, width in spans:
                        mm = pe.matmul(dst, w[:, slot, k * P:(k + 1) * P], x[:, k, c:c + width],
                                       start=(k == 0 and n == 0), stop=(k == kt - 1 and n == 2))
            if ks[-1] == kt - 1:
                mm.then_inc(up_done, 1)

        def mul_first(pe, u, xh, xl, ready):
            pe.wait_ge(up_full, u + 4)
            pe.wait_ge(up_evac, u + 2)
            steps = [(k, slot) for k in range(KT - 2) for slot in range(2)]
            steps += [(k, slot) for slot in range(2) for k in range(KT - 2, KT)]
            for k, slot in steps:
                if slot == 0:
                    pe.wait_ge(*ready(k))
                for n, (w, x) in enumerate(((up_h, xh), (up_h, xl), (up_l, xh))):
                    for j in range(2):
                        mm = pe.matmul(PS[:, 2 * slot + j, :], w[:, slot, k * P:(k + 1) * P],
                                       x[:, k, j * HALF:(j + 1) * HALF], start=(k == 0 and n == 0),
                                       stop=(k == KT - 1 and n == 2))
                if k == KT - 1:
                    mm.then_inc(up_done, 1)

        def first_half(pe, u, xh, xl, h, k, slot):
            for n, (w, x) in enumerate(((up_h, xh), (up_h, xl), (up_l, xh))):
                mm = pe.matmul(PS[:, 2 * slot + h, :], w[:, slot, k * P:(k + 1) * P], x[:, k, h * HALF:(h + 1) * HALF],
                               start=(k == 0 and n == 0), stop=(k == KT - 1 and n == 2))
            if h == 1 and k == KT - 1:
                mm.then_inc(up_done, 1)

        def dn_unit(pe, i, m, j, hid, unit0, wh, wl):
            pe.wait_ge(dn_evac, unit0 + i + 1)
            for k in range(2):
                for n, (w, x) in enumerate(((wh, hid_h), (wh, hid_l), (wl, hid_h))):
                    mm = pe.matmul(PS[:, 4 + i % 2, :], w[:, k, m * P:(m + 1) * P],
                                   x[:, hid, k, j * HALF:(j + 1) * HALF],
                                   start=(k == 0 and n == 0), stop=(k == 1 and n == 2))
            mm.then_inc(dn_done, 1)

        def mul_dn(pe, d, hid, unit0, wh=dn_h, wl=dn_l):
            pe.wait_ge(dn_full, d + 4)
            for i in range(2 * KT):
                dn_unit(pe, i, i // 2, i % 2, hid, unit0, wh, wl)

        SUMS = {"mlp": 0, "final": 1, "post2": 2, "ffn2": 3}
        NORMS = {"mlp": 0, "final": 1, "mix2": 2, "post2": 3, "ffn2": 4}
        SPREADS = {"mlp": 0, "mix2": 1, "final": 2, "post2": 3}
        MODULATED = {"mlp": 0, "mix2": 1, "ffn2": 2}
        nsem = {s: sem("norm_" + s) for s in ("sq", "acc", "sums", "root", "rstd", "diag", "bc", "hn", "mod", "high", "low")}

        def square(act, n, k, slot, buf, acc, src):
            if isinstance(k, int) and k == 0:
                act.activation(acc[:, :], src, ACT.Square).then_inc(nsem["sq"], 1)
                return
            act.wait_ge(nsem["acc"], k + 7 * SUMS[n])
            if not isinstance(k, int):
                carry(act)
            act.activation(buf[:, slot, :], src, ACT.Square).then_inc(nsem["sq"], 1)

        def add_square(eng, n, k, slot, buf, acc):
            eng.wait_ge(nsem["sq"], k + (KT * SUMS[n] + 1))
            eng.wait_ge(nsem["acc"], k + (7 * SUMS[n] + 1))
            eng.tensor_tensor(acc[:, :], acc[:, :], buf[:, slot, :], ALU.add).then_inc(nsem["acc"], 1)

        def add_sums(pe, n, acc):
            pe.wait_ge(nsem["acc"], 7 * SUMS[n] + 9)
            for t in range(TT):
                mm = pe.matmul(PS[:, 7, t:t + 1], acc[:, t * P:(t + 1) * P], ones[:, 0:1], start=True, stop=True)
            mm.then_inc(nsem["sums"], 1)

        def norm_root(act, n):
            act.wait_ge(nsem["sums"], SUMS[n] + 1)
            act.activation(root8, PS[:, 7, 0:TT], ACT.Sqrt, scale=1.0 / D, bias=eps_rms).then_inc(nsem["root"], 1)

        def norm_rstd(dve, n, out, root):
            dve.wait_ge(nsem["root"], NORMS[n] + 1)
            dve.reciprocal(out, root).then_inc(nsem["rstd"], 1)
            dve.wait_ge(nsem["rstd"], NORMS[n] + 1)

        def norm_diag(dve, buf, r):
            dve.tensor_tensor(buf[:, :].rearrange("p (t c) -> p t c", c=P), ident.unsqueeze(1).to_broadcast([P, TT, P]),
                              r.unsqueeze(2).to_broadcast([P, TT, P]), ALU.mult).then_inc(nsem["diag"], 1)

        def norm_spread(pe, n, buf, bank):
            pe.wait_ge(nsem["diag"], SPREADS[n] + 1)
            for j in range(2):
                mm = pe.matmul(PS[:, bank + j, :], ones[:, :], buf[:, j * HALF:(j + 1) * HALF], start=True, stop=True)
            mm.then_inc(nsem["bc"], 1)

        def norm_vector(dve, n):
            norm_rstd(dve, n, rstd8, root8)
            norm_diag(dve, ndiag, rstd8)
            dve.wait_ge(nsem["bc"], SPREADS[n] + 1)

        def by_half(t, h):
            return t[:, h * HALF:(h + 1) * HALF]

        HALF_SQ = {"ffn2": KT * SUMS["ffn2"], "out": KT * SUMS["ffn2"] + 2 * KT}
        HALF_ACC = {"ffn2": 7 * SUMS["ffn2"] + 2, "out": 7 * SUMS["ffn2"] + 16}
        HALF_SUMS = {"ffn2": SUMS["ffn2"], "out": SUMS["ffn2"] + 2}
        HALF_NORM = {"ffn2": NORMS["ffn2"], "out": NORMS["ffn2"] + 2}
        HALF_SPREAD = {"post2": SPREADS["post2"], "ffn2": SPREADS["post2"] + 2, "out": SPREADS["post2"] + 4}
        OUT_UNITS = 16 * (C_FF2 + CH2 - 1)

        def half_square(act, n, i, src):
            h, k = divmod(i, KT)
            if k >= 3:
                act.wait_ge(nsem["acc"], HALF_ACC[n] + 7 * h + k - 2)
            act.activation(by_half(sq_sum, h) if k == 0 else by_half(nsq[:, k % 2, :], h), by_half(src, h), ACT.Square
                           ).then_inc(nsem["sq"], 1)

        def add_half_square(eng, n, i):
            h, k = divmod(i, KT)
            if k:
                eng.wait_ge(nsem["sq"], HALF_SQ[n] + i + 1)
                eng.wait_ge(nsem["acc"], HALF_ACC[n] + 7 * h + k - 1)
                eng.tensor_tensor(by_half(sq_sum, h), by_half(sq_sum, h), by_half(nsq[:, k % 2, :], h), ALU.add
                                  ).then_inc(nsem["acc"], 1)

        def half_sums(pe, n, h):
            pe.wait_ge(nsem["acc"], HALF_ACC[n] + 7 * (h + 1))
            for t in range(h * TT // 2, (h + 1) * TT // 2):
                mm = pe.matmul(PS[:, 7, t:t + 1], sq_sum[:, t * P:(t + 1) * P], ones[:, 0:1], start=True, stop=True)
            mm.then_inc(nsem["sums"], 1)

        def half_root(act, n, h):
            tiles = slice(h * TT // 2, (h + 1) * TT // 2)
            act.wait_ge(nsem["sums"], HALF_SUMS[n] + h + 1)
            act.activation(root8[:, tiles], PS[:, 7, tiles], ACT.Sqrt, scale=1.0 / D, bias=eps_rms).then_inc(nsem["root"], 1)

        def half_diag(dve, n, h):
            tiles = slice(h * TT // 2, (h + 1) * TT // 2)
            dve.wait_ge(nsem["root"], HALF_NORM[n] + h + 1)
            dve.reciprocal(rstd8[:, tiles], root8[:, tiles]).then_inc(nsem["rstd"], 1)
            dve.wait_ge(nsem["rstd"], HALF_NORM[n] + h + 1)
            diag_half(dve, h)

        def diag_half(dve, h):
            tiles = slice(h * TT // 2, (h + 1) * TT // 2)
            dve.tensor_tensor(by_half(ndiag, h).rearrange("p (t c) -> p t c", c=P),
                              ident.unsqueeze(1).to_broadcast([P, TT // 2, P]),
                              rstd8[:, tiles].unsqueeze(2).to_broadcast([P, TT // 2, P]), ALU.mult).then_inc(nsem["diag"], 1)

        def half_spread(pe, n, h, bank):
            pe.wait_ge(nsem["diag"], HALF_SPREAD[n] + h + 1)
            pe.matmul(PS[:, bank + h, :], ones[:, :], by_half(ndiag, h), start=True, stop=True).then_inc(nsem["bc"], 1)

        def modulate_vector(dve, n, src, bank):
            n8 = KT * MODULATED[n]
            for k in range(KT + 1):
                if k < KT:
                    if k >= 2:
                        dve.wait_ge(nsem["low"], n8 + k - 1)
                    dve.tensor_tensor(nhn[:, k % 2, :], src[:, k, :], bank2(bank), ALU.mult
                                      ).then_inc(nsem["hn"], 1)
                if k >= 1:
                    j = k - 1
                    dve.wait_ge(nsem["high"], n8 + j + 1)
                    dve.tensor_tensor(hn_l[:, j, :], nhn[:, j % 2, :], hn_h[:, j, :].bitcast(F32),
                                      ALU.subtract).then_inc(nsem["low"], 1)

        def modulate_scalar(act, n, gs, sh):
            n8 = KT * MODULATED[n]
            for k in range(KT):
                act.wait_ge(nsem["hn"], n8 + k + 1)
                act.activation(nhn[:, k % 2, :], nhn[:, k % 2, :], ACT.Identity, scale=gs[:, k:k + 1],
                               bias=sh[:, k:k + 1]).then_inc(nsem["mod"], 1)
                act.wait_ge(nsem["mod"], n8 + k + 1)
                act.activation(hn_h[:, k, :], nhn[:, k % 2, :], ACT.Copy).then_inc(nsem["high"], 1)

        eps_rms = small(1)
        eps_ln = small(1)

        @block.sync
        def _(sp):
            sp.dma_start(vrow[:, :, :], a["vecs"].rearrange("(t p) f -> p t f", p=P)).then_inc(sem("tables_in"), 16)
            sp.dma_start(cst[:, :], a["consts"]).then_inc(sem("tables_in"), 16)
            ada_rows_of = a["ada_w"].rearrange("(k p) f -> p k f", p=P)

            def shift_in(j):
                if j >= 2:
                    sp.wait_ge(sem("ada_used"), 2 * j)
                sp.dma_start(ada_shift[j % 2][:, :, :], ada_rows_of[:, 2 * j:2 * j + 2, 0:1024]
                             ).then_inc(sem(f"ada_in{j % 2}"), 16)

            def scale_in(j):
                sp.dma_start(ada_scale[:, 4 * j:4 * j + 4, :], ada_rows_of[:, 4 * j:4 * j + 4, 1024:2048]
                             ).then_inc(sem(f"ada_sc{j}"), 16)

            shift_in(0)
            shift_in(1)
            scale_in(0)
            shift_in(2)
            scale_in(1)
            shift_in(3)
            def ada1(b, s, wait=True):
                if wait:
                    sp.wait_ge(sem("ada1_used"), b * KT - 6)
                    carry(sp)
                sp.dma_start(ada_in1[s][:, :, :], a["ada_w"].rearrange("(k p) f -> p k f", p=P)[:, :, bass.ds(b * ADA1 + 2048, ADA1)]
                             ).then_inc(sem(f"ada1_in{s}"), 16)

            for s in range(2):
                load_up(sp, s, w_in, s, s, None)
            sp.wait_ge(sem("ada_sum0"), 2)
            for s in range(2):
                ada1(s, s, False)
            with sp.Fori(1, 4) as i:
                for s in range(2):
                    load_up(sp, i * 2 + s, w_in, i * 2 + s, s, None)
                for s in range(2):
                    ada1(i * 2 + s, s)
            for s in range(2):
                load_up(sp, 8 + s, w_in, 8 + s, s, None)
            sp.dma_start(wf[:, :, :], a["w_fourier"].rearrange("(t p) f -> p t f", p=P)).then_inc(sem("four_in"), 16)
            with sp.Fori(0, 4) as i:
                for s in range(2):
                    load_up(sp, i * 2 + K0 + s, w_in, i * 2 + K0 + s, s, None)
            sp.dma_start(rpb_rows, bass.AP(a["rpb"].tensor, 0, [[0, GRID_W], [1, RPB_LEN]])).then_inc(sem("rpb_in"), 16)
            for m in range(2):
                load_up(sp, U_WO1 + m, a["w_out"], m, m, None)
            sp.wait_ge(up_done, U_WO1 + 2)
            sp.dma_start(dseq[:, :, :], a["dft_seq"].rearrange("(t p) f -> p t f", p=P)).then_inc(sem("four_in"), 16)
            sp.wait_ge(sem("taps"), 2 * TAPS)
            sp.dma_start(pw[:, :, :], a["conv_pw_w"].rearrange("(t p) f -> p t f", p=P)).then_inc(sem("point_in"), 16)
            sp.wait_ge(sem("rpb_in"), 16)
            for p in range(PAIRS):
                s = p % 2
                if p >= 2:
                    sp.wait_ge(sem("na_biased"), 16 * p + 1)
                for h in range(2):
                    for par in range(2):
                        off = RPB_PAD + (2 * p + h) * RPB_ROWS * RPB_COLS + (1 - par) * RPB_COLS + RPB_COLS // 2
                        src = bass.AP(rpb_rows.tensor, off, [[RPB_LEN - 1, GRID_W], [RPB_COLS, BIAS_ROWS], [1, GRID_W]])
                        dst = tb[s][par * GRID_W:(par + 1) * GRID_W, h, :].rearrange("p (r c) -> p r c", c=GRID_W)
                        sp.dma_start(dst, src).then_inc(sem(f"bias_in{s}"), 16)
            sp.wait_ge(sem("na_o"), 16 * PAIRS + 1)
            for m in range(2):
                sp.dma_start(xslab[:, m, :, :], a["x"].rearrange("(t p) f -> p t f", p=P)[:, :, bass.ts(m, P)]
                             ).then_inc(sem(f"slab_in{m}"), 16)
            with sp.Fori(1, 4) as i:
                for s in range(2):
                    load_up(sp, i * 2 + U_WO1 + s, a["w_out"], i * 2 + s, s, None)
                    sp.wait_ge(sem("slab_used"), i * 2 + s - 1)
                    sp.dma_start(xslab[:, s, :, :], a["x"].rearrange("(t p) f -> p t f", p=P)[:, :, bass.ds((i * 2 + s) * P, P)]
                                 ).then_inc(sem(f"slab_in{s}"), 16)
            def ff1_up(c):
                for s in range(2):
                    load_up(sp, c * 2 + U_FF1 + s, a["mlp_w1"], c * 2 + s, s, None, dn_before=c * 2 + s - 1 + 2 * C_FF1)

            def ff1_dn(c):
                for s in range(2):
                    load_dn(sp, None, a["mlp_w2"], c * 2 + s, s, c * 2 + U_FF1 + 2 + 3 + s)

            def ada2_in(b):
                sp.wait_ge(sem("ada2_used"), b * KT + 2)
                carry(sp)
                sp.dma_start(ada_in2[:, :, :], a["w_ada_2"].rearrange("(k p) f -> p k f", p=P)[:, :, bass.ds(b * ADA2, ADA2)]
                             ).then_inc(sem("ada2_in"), 16)

            for s in range(2):
                load_up(sp, U_FF1 + s, a["mlp_w1"], s, s, None)
            sp.wait_ge(up_done, U_FF1 + 2)
            ada2_in(0)
            with sp.Fori(0, (CH1 - 2) // 2) as j:
                for e in range(2):
                    ff1_up(j * 2 + 1 + e)
                    ada2_in(j * 2 + 1 + e)
                    ff1_dn(j * 2 + e)
            ff1_up(CH1 - 1)
            ada2_in(CH1 - 1)
            ff1_dn(CH1 - 2)
            for s in range(2):
                sp.wait_ge(dn_full, 2 * (CH1 - 2) + s + 3)
                load_dn(sp, None, a["mlp_w2"], 2 * (CH1 - 1) + s, s, U_FF1 + 2 * CH1 + 2)
            def win2(p, m, s, dn_before=None):
                load_up(sp, p + U_WIN2, a["w_in_2"], m, s, None, dn_before=dn_before)

            for s in range(2):
                win2(s, V2 + s, s, dn_before=2 * CH1 + 2)
            sp.wait_ge(dn_done, 16 * CH1 + 1)
            sp.dma_start(pos[:, :], bass.AP(a["positions_2"].tensor, 0, [[0, P], [1, SEQ]])).then_inc(sem("pos_in"), 16)
            with sp.Fori(1, 3) as i:
                for s in range(2):
                    win2(i * 2 + s, i * 2 + (V2 + s), s)
            sp.wait_ge(sem("x1_ready"), KT)
            sp.dma_start(xt_spill[0], xt[:, :, :]).then_inc(sem("x_moved"), 16)
            with sp.Fori(3, 6) as i:
                for s in range(2):
                    win2(i * 2 + s, i * 2 + (K2 - 6 + s), s)
            with sp.Fori(0, 4) as i:
                for s in range(2):
                    win2(i * 2 + (12 + s), i * 2 + s, s)
            for m in range(2):
                load_up(sp, U_WO2 + m, a["w_out_2"], m, m, None, kt=4)
            sp.wait_ge(up_done, U_WIN2 + W_IN2_TILES + 2)
            sp.dma_start(wp[:, :, :], a["w_pool"].rearrange("c p f -> p c f")).then_inc(sem("point_in"), 16)
            def rows_back(g):
                for e in range(OG):
                    sp.wait_ge(sem(f"o2_out{e}"), 16 * ((D_LAST[g] - e) // OG + 1))
                sp.dma_start(oall[:, :, g, :], o_rows[g].rearrange("(t p) w -> p t w", p=P)).then_inc(sem("oall_in"), 16)

            for n, (g, b) in enumerate(D_ORDER):
                rows = o_rows[g]
                sp.wait_ge(sem("o2_ready"), n + 1)
                if g == 0:
                    dst = rows[b * P:(b + 1) * P]
                elif g == 1:
                    dst = rows.rearrange("(n i r) w -> n r i w", n=2, r=4)[b // 4, b % 4]
                else:
                    dst = rows.rearrange("(k r) w -> r k w", r=8)[b]
                sp.dma_start(dst, og[n % OG][:, :]).then_inc(sem(f"o2_out{n % OG}"), 16)
                if n - 3 in D_LAST:
                    rows_back(D_LAST.index(n - 3))
            for g in range(GROUPS):
                if D_LAST[g] + 3 >= GROUPS * TT:
                    rows_back(g)
            with sp.Fori(1, KT // 2) as i:
                for s in range(2):
                    load_up(sp, i * 2 + U_WO2 + s, a["w_out_2"], i * 2 + s, s, None, kt=4)
            sp.wait_ge(sem("mix2_split"), 4)
            sp.wait_ge(sem("x_moved"), 16)
            sp.dma_start(xt[:, :, :], xt_spill[0]).then_inc(sem("x_moved"), 16)
            def ff2_up(c):
                for i in range(4):
                    f = c * 2 + i // 2 + (FF2_TILES if i % 2 else 0)
                    load_up(sp, c * 4 + U_FF2 + i, a["w_up_2"], f, i % 2, None,
                            dn_before=(c * 2 + i - 1 + 2 * C_FF2) if i < 2 else None)

            def ff2_dn(c):
                for s in range(2):
                    load_dn(sp, None, a["w_down_2"], c * 2 + s, s, c * 4 + U_FF2 + 4 + 5 + s)

            ff2_up(0)
            sp.wait_ge(sem("x_ready"), 2 * KT)
            sp.dma_start(xt_spill[1], xt[:, :, :]).then_inc(sem("x_moved"), 16)
            with sp.Fori(0, (CH2 - 1) // 2) as j:
                ff2_up(j * 2 + 1)
                ff2_dn(j * 2)
                ff2_up(j * 2 + 2)
                ff2_dn(j * 2 + 1)
            for s in range(2):
                sp.wait_ge(dn_full, 2 * (C_FF2 + CH2 - 2) + s + 3)
                load_dn(sp, None, a["w_down_2"], 2 * (CH2 - 1) + s, s, U_FF2 + 4 * CH2 + 2)
            sp.wait_ge(sem("ff2_low"), 2 * CH2)
            sp.wait_ge(sem("x_moved"), 48)
            sp.dma_start(xt[:, :, :], xt_spill[1]).then_inc(sem("x_moved"), 16)
            for t in range(TT):
                sp.wait_ge(sem("o_ready"), t + 1)
                sp.dma_start(out[t * P:(t + 1) * P, :], otok[:, t % 2, :]).then_inc(sem(f"stored{t % 2}"), 16)
            for s in range(2):
                sp.wait_ge(sem(f"stored{s}"), 16 * TT // 2)

        @block.gpsimd
        def _(pool):
            pool.sem_inc(up_full, 2)
            pool.sem_inc(dn_full, 2)
            pool.sem_inc(up_done, 2)
            pool.sem_inc(up_evac, 2)
            pool.sem_inc(dn_evac, 2)
            pool.sem_inc(sem("ada_used"), 2)
            pool.sem_inc(sem("ada1_used"), 2)
            pool.sem_inc(sem("ada2_used"), 2)
            pool.sem_inc(sem("mod2"), 1)
            pool.sem_inc(nsem["acc"], 2)
            pool.sem_inc(sem("ada1_sum"), 2)
            pool.sem_inc(sem("na_biased"), 17)
            pool.sem_inc(dn_done, 1)
            pool.sem_inc(sem("v_turned"), 1)
            pool.sem_inc(sem("probt_set"), 1)
            pool.sem_inc(sem("na_o"), 1)
            pool.memset(ones[:, :], 1.0).then_inc(sem("ones_set"), 1)
            pool.memset(eps_rms, RMS_EPS).then_inc(sem("ones_set"), 1)
            pool.memset(eps_ln, LN_EPS).then_inc(sem("ones_set"), 1)
            with pool.Fori(0, W_IN_TILES // 2) as i:
                for s in range(2):
                    split_up(pool, i * 2 + s, s, i + 1, i * 2 + s + 1)
            for s in range(2):
                split_up(pool, U_WO1 + s, s, U_WO1 // 2 + 1, U_WO1 + s + 1)
            with pool.Fori(0, PAIRS // 2) as i:
                for s in range(2):
                    pool.wait_ge(sem("na_biased"), i * 32 + (16 * s + 1))
                    pool.wait_ge(sem(f"bias_in{s}"), i * 64 + 64)
                    tbv = tb[s][:, :, :].rearrange("p h (r c) -> p (h r) c", c=GRID_W)
                    pool.tensor_tensor(tbv, tbv, const("col_mask").unsqueeze(1).to_broadcast([P, 2 * BIAS_ROWS, GRID_W]),
                                       ALU.add).then_inc(sem("bias_set"), 1)
                    pool.wait_ge(sem("bias_set"), i * 10 + 5 * s + 1)
                    carry(pool)
                    pool.tensor_copy(tbm[s][:, :, :], tb[s][:, :, 2 * GRID_W:12 * GRID_W]).then_inc(sem("bias_set"), 1)
                    pool.wait_ge(sem("bias_set"), i * 10 + 5 * s + 2)
                    carry(pool)
                    pool.memset(tbm[s][0:64, :, 8 * GRID_W:], BIG).then_inc(sem("bias_set"), 1)
                    pool.memset(tbm[s][64:P, :, 0:GRID_W], BIG).then_inc(sem("bias_set"), 1)
                    pool.memset(tbm[s][64:P, :, 9 * GRID_W:], BIG).then_inc(sem("bias_set"), 1)
                    pool.wait_ge(sem("bias_set"), i * 10 + 5 * s + 5)
                    pool.wait_ge(up_evac, W_IN_TILES + 2)
                    pool.wait_ge(sem("four_done"), 4)
                    pool.tensor_copy(qs[s][:, :], pt1[:, i * 2 + (Q0 + s), :]).then_inc(sem("staged"), 1)
                    pool.tensor_copy(ks[s][:, 0:SEQ], pt1[:, i * 2 + (K0 + s), :]).then_inc(sem("staged"), 1)
                    pool.tensor_copy(ks[s][:, SEQ:], ckv[:, i * 2 + s, :]).then_inc(sem("staged"), 1)
                    pool.wait_ge(sem("v_turned"), i * 4 + (2 * s + 1))
                    pool.tensor_copy(vs[:, 0:SEQ], pt1[:, i * 2 + (V0 + s), :]).then_inc(sem("staged"), 1)
                    pool.tensor_copy(vs[:, SEQ:], ckv[:, i * 2 + (PAIRS + s), :]).then_inc(sem("staged"), 1)
            with pool.Fori(1, KT // 2) as i:
                for s in range(2):
                    split_up(pool, i * 2 + U_WO1 + s, s, i + U_WO1 // 2 + 1, i * 2 + U_WO1 + s + 1)

            r0 = U_FF1

            def ff1_up(c, r):
                for s in range(2):
                    split_up(pool, c * 2 + U_FF1 + s, s, r + 1, r * 2 + s + 1)

            def ff1_dn(c, r, last=False):
                for s in range(2):
                    split_dn(pool, None, s, r + 1, r * 2 + s + 1, c * 16, U_FF1 + 2 * CH1 - 2 + s if last else None)

            ff1_up(0, r0 // 2)
            with pool.Fori(0, (CH1 - 2) // 2) as j:
                ff1_up(j * 2 + 1, j * 4 + r0 // 2 + 1)
                ff1_dn(j * 2, j * 4 + r0 // 2 + 2)
                ff1_up(j * 2 + 2, j * 4 + r0 // 2 + 3)
                ff1_dn(j * 2 + 1, j * 4 + r0 // 2 + 4)
            n = 2 * (CH1 - 2) + r0 // 2 + 1
            ff1_up(CH1 - 1, n)
            ff1_dn(CH1 - 2, n + 1)
            ff1_dn(CH1 - 1, n + 2, last=True)
            r1 = r0 + 4 * CH1
            for k in range(1, KT):
                pool.wait_ge(nsem["sq"], KT * SUMS["final"] + k + 1)
                if k >= 2:
                    pool.wait_ge(sem("acc_m"), k - 1)
                pool.tensor_tensor(sq_sum_m[:, :], sq_sum_m[:, :], nsq_fm[:, 2 * (k % 2) + 1, :], ALU.add
                                   ).then_inc(sem("acc_m"), 1)
            pool.wait_ge(dn_done, 16 * CH1 + 1)
            for s in range(2):
                split_up(pool, U_WIN2 + s, s, r1 // 2 + 1, r1 + s + 1)
            with pool.Fori(1, W_IN2_TILES // 2) as i:
                for s in range(2):
                    split_up(pool, i * 2 + U_WIN2 + s, s, i + r1 // 2 + 1, i * 2 + r1 + s + 1)
            r2 = r1 + W_IN2_TILES
            for s in range(2):
                split_up(pool, U_WO2 + s, s, r2 // 2 + 1, r2 + s + 1, kt=4)
            pool.wait_ge(sem("c_weight"), 2)
            ts = slice(C_SPLIT, TT)
            for g in range(GROUPS):
                src, wt = c_group(g, ts)
                pool.tensor_tensor(cterm[:, ts, :, :] if g else csum[:, ts, :, :], src, wt, ALU.mult).then_inc(sem("c_sum"), 1)
                if g:
                    pool.wait_ge(sem("c_sum"), 2 * g)
                    pool.tensor_tensor(csum[:, ts, :, :], csum[:, ts, :, :], cterm[:, ts, :, :], ALU.add
                                       ).then_inc(sem("c_sum"), 1)
                    pool.wait_ge(sem("c_sum"), 2 * g + 1)
            with pool.Fori(1, KT // 2) as i:
                for s in range(2):
                    split_up(pool, i * 2 + U_WO2 + s, s, i + r2 // 2 + 1, i * 2 + r2 + s + 1, kt=4)
            r3 = r2 + KT

            def ff2_up(c, r, pieces=range(4)):
                for i in pieces:
                    split_up(pool, c * 4 + U_FF2 + i, i % 2, r + 1 + i // 2, r * 2 + i + 1)

            def ff2_dn(c, r, last=False):
                for s in range(2):
                    split_dn(pool, None, s, r + 1, r * 2 + s + 1, c * 16 + 16 * C_FF2, U_FF2 + 4 * CH2 - 2 + s if last else None)

            ff2_up(0, r3 // 2, range(2))
            for i in range(2 * KT):
                add_half_square(pool, "ffn2", i)
            pool.wait_ge(sem("x_ready"), 2 * KT)
            pool.memset(y2[:, :, :], 0.0).then_inc(sem("y2_zero"), 1)
            ff2_up(0, r3 // 2, range(2, 4))
            with pool.Fori(0, (CH2 - 1) // 2) as j:
                ff2_up(j * 2 + 1, j * 6 + r3 // 2 + 2)
                ff2_dn(j * 2, j * 6 + r3 // 2 + 4)
                ff2_up(j * 2 + 2, j * 6 + r3 // 2 + 5)
                ff2_dn(j * 2 + 1, j * 6 + r3 // 2 + 7)
            ff2_dn(CH2 - 1, 3 * (CH2 - 1) + r3 // 2 + 2, last=True)
            pool.wait_ge(sem("x_moved"), 64)
            for k in range(KT):
                pool.wait_ge(sem("y_gated"), 2 * KT + k + 1)
                x = by_half(xt[:, k, :], 0)
                pool.tensor_tensor(x, x, by_half(y2[:, k, :], 0), ALU.add).then_inc(sem("x_ready"), 1)

        @block.scalar
        def _(act):
            for t in range(0, TT + CT, 2):
                src = a["x"][t * P:(t + 2) * P, :] if t < TT else a["ctx"]
                act.dma_start(xtok[:, t:t + 2, :], src.rearrange("(t p) f -> p t f", p=P)).then_inc(sem(f"x_in{t // 2}"), 16)
            act.wait_ge(sem("ones_set"), 3)

            def squares(lo, hi):
                for t in range(lo, hi):
                    act.wait_ge(sem(f"x_in{t // 2}"), 16)
                    if t >= 2:
                        act.wait_ge(sem("ss"), t - 1)
                    act.activation(junk[:, t % 2, :], xtok[:, t, :], ACT.Square, accum_out=ss10[:, t:t + 1]).then_inc(sem("ss"), 1)

            def roots(lo, hi):
                act.wait_ge(sem("ss"), hi)
                act.activation(root10[:, lo:hi], ss10[:, lo:hi], ACT.Sqrt, scale=1.0 / D, bias=eps_rms).then_inc(sem("root10"), 1)

            def turned_out(lo, hi):
                for t in range(lo, hi):
                    act.wait_ge(sem("x_turned"), t + 1)
                    act.activation(xs[:, :, t * P:(t + 1) * P], bank2(2 * (t % 2)).rearrange("p (k n) -> p k n", n=P), ACT.Copy
                                   ).then_inc(sem("xs_set"), 1)

            squares(0, 2)
            act.wait_ge(sem("vec_set"), 1)
            act.activation(silu_c, vec("c", 0, 24), ACT.Silu).then_inc(sem("silu"), 1)
            squares(2, 4)
            roots(0, 4)
            squares(4, 8)
            roots(4, 8)
            turned_out(0, 6)
            squares(8, 10)
            roots(8, 10)
            turned_out(6, 10)
            act.wait_ge(sem("ada_row"), 1)
            act.activation(ada_rows[0:2, :], bank2(4)[0:2, :], ACT.Copy).then_inc(sem("ada_row"), 1)
            for k in range(KT):
                act.wait_ge(sem("hn1"), 2 * (k + 1))
                act.activation(hn1_h[:, k, :], xs[:, k, :], ACT.Copy).then_inc(sem("hn1_high"), 1)

            def out1(u, scale=1.0, ctx_tile=None, slot=0):
                act.wait_ge(up_done, u + 3)
                if ctx_tile is not None:
                    act.activation(ckv[:, ctx_tile, :], PS[:, 4 + slot, 0:CTX], ACT.Copy).then_inc(sem("ckv_set"), 1)
                act.activation(pt1[:, u, :], bank2(2 * slot), ACT.Copy, scale=scale).then_inc(up_evac, 1)

            act.wait_ge(sem("hn1_low"), KT)
            with act.Fori(0, Q0 // 2) as i:
                for s in range(2):
                    out1(i * 2 + s, slot=s)
            act.wait_ge(up_evac, Q0 + 2)
            act.activation(pt1[:, 4:6, :], pt1[:, 4:6, :], ACT.Sigmoid).then_inc(sem("gate"), 1)
            with act.Fori(Q0 // 2, K0 // 2) as i:
                for s in range(2):
                    out1(i * 2 + s, scale=SCALE, slot=s)
            act.wait_ge(sem("ada1_used"), 8 * KT + 2)

            def out_kv(j, s):
                out1(j + K0, ctx_tile=j, slot=s)

            for s in range(2):
                out_kv(s, s)
            for c in range(2):
                act.wait_ge(sem("four_w"), c + 1)
                act.activation(four_ab[:, c, :], PS[:, 6 + c, :], ACT.Copy).then_inc(sem("four_ab"), 1)
            with act.Fori(1, 3) as i:
                for s in range(2):
                    out_kv(i * 2 + s, s)
            for c in range(2):
                act.wait_ge(sem("ln_d"), c + 1)
                act.activation(conv_sq[:, c, :], conv_acc[:, c, :], ACT.Square).then_inc(sem("ln_sq"), 1)
            out_kv(6, 0)
            act.wait_ge(sem("ln_sums"), 2)
            act.activation(ln_r[:, :], bank2(6), ACT.Sqrt, scale=1.0 / 256, bias=eps_ln).then_inc(sem("ln_root"), 1)
            out_kv(7, 1)
            for t in range(TT):
                act.wait_ge(sem("four_z"), t + 1)
                act.activation(zf[:, t, :], PS[:, 4 + t % 2, :], ACT.Copy).then_inc(sem("zf_set"), 1)
            for c in range(2):
                act.wait_ge(sem("ln_y"), c + 1)
                act.activation(conv_acc[:, c, :], conv_acc[:, c, :], ACT.Silu, scale=vec("conv_norm_g", c),
                               bias=vec("conv_norm_b", c)).then_inc(sem("conv_s"), 1)
            for n in range(2):
                act.wait_ge(sem("four_done"), 2 * n + 1)
                act.activation(four_e[n][:, :], PS[:, 6 - 2 * n, :], ACT.Copy).then_inc(sem("four_e"), 1)
                act.activation(four_y[:, n, NYQ:NYQ + 1], PS[:, n, 0:1], ACT.Copy).then_inc(sem("four_e"), 1)
            for m in range(2):
                act.wait_ge(sem("conv_pw"), m + 1)
                act.activation(conv_out[:, m, :], bank2(2 * m), ACT.Identity, bias=vec("conv_pw_b", m)
                               ).then_inc(sem("conv_done"), 1)
            act.wait_ge(sem("four_mir"), 4)
            with act.Fori(0, PAIRS // 2) as i:
                def v_out(s, r):
                    lo, cnt = 8 * r, 8 if r == 0 else 2
                    src = bank2(2 * ((V_STEP + r) % 2)) if s else bank2(4 + 2 * r)
                    act.wait_ge(sem("v_turned"), i * 4 + (2 * s + r + 2))
                    act.activation(vt[s][:, lo:lo + cnt, :], src[:, 0:cnt * P].rearrange("p (t c) -> p t c", c=P),
                                   ACT.Copy).then_inc(sem("vt_set"), 1)

                for n in range(33):
                    if n < 32:
                        w = WIN_N[n % 8]
                        act.wait_ge(sem("na_max"), i * 32 + (n + 1))
                        act.activation(prob[n % 2][:, 0:w], sbias[n % 2][:, 0:w], ACT.Exp,
                                       bias=st_neg[:, n % 2:n % 2 + 1], accum_out=st_d[:, n % 2:n % 2 + 1]
                                       ).then_inc(sem("na_exp"), 1)
                        act.activation(prob[n % 2][:, w:w + CTX], bank2(2 * (n % 2))[:, w:w + CTX], ACT.Exp,
                                       bias=st_neg[:, n % 2:n % 2 + 1], accum_out=st_d2[:, n % 2:n % 2 + 1]
                                       ).then_inc(sem("na_exp"), 1)
                    if n == 1:
                        for r in range(2):
                            v_out(0, r)
                    if n >= 1:
                        w = WIN_N[(n - 1) % 8] + CTX
                        act.wait_ge(sem("na_turned"), i * 32 + n)
                        act.activation(probt[(n - 1) % 2][:, 0:w], bank2(4)[:, 0:w], ACT.Copy).then_inc(sem("probt_set"), 1)
                    if n == V_STEP + 1:
                        for r in range(2):
                            v_out(1, r)
            for k in range(4):
                act.wait_ge(sem("four_mir"), 4)
                src = four_y[:, k, :] if k < 2 else conv_out[:, k - 2, :]
                if k == 0:
                    act.wait_ge(sem("na_o"), 16 * PAIRS + 1)
                    act.wait_ge(sem("four_e"), 4)
                act.activation(mix_h[:, k, :], src, ACT.Copy).then_inc(sem("mix_high"), 1)
            for f in range(4):
                act.activation(mix_h[:, 4 + f, :], ao[:, f, :], ACT.Copy).then_inc(sem("mix_high"), 1)
            act.wait_ge(sem("mix_low"), KT)
            def x_tile(u, s):
                act.wait_ge(sem("slab_used"), u + 1)
                act.activation(xt[:, u, :], bank2(4), ACT.Copy).then_inc(sem("xt_set"), 1)

            def x_square(u, s):
                act.wait_ge(up_evac, u + (U_WO1 + 3))
                square(act, "mlp", u, s, nsq, sq_sum, xt[:, u, :])

            for s in range(2):
                x_tile(s, s)
            x_square(0, 0)
            with act.Fori(1, KT // 2) as i:
                for s in range(2):
                    x_tile(i * 2 + s, s)
                    x_square(i * 2 + (s - 1), 1 - s)
            x_square(KT - 1, 1)
            norm_root(act, "mlp")
            modulate_scalar(act, "mlp", gs2, mod1[:, 24:32])

            def ff1_square(c, s, hid, wait_free):
                act.wait_ge(up_done, c * 2 + U_FF1 + s + 3)
                if wait_free:
                    act.wait_ge(sem("ff1_low"), c * 2 + s - 1)
                act.activation(sq[:, s, :], bank2(2 * s), ACT.Relu).then_inc(up_evac, 1)
                act.wait_ge(up_evac, c * 2 + U_FF1 + s + 3)
                act.activation(sq[:, s, :], sq[:, s, :], ACT.Square).then_inc(sem("ff1_sq"), 1)
                act.wait_ge(sem("ff1_sq"), c * 2 + s + 1)
                if wait_free:
                    act.wait_ge(dn_done, c * 16 - 15 + 16 * C_FF1)
                act.activation(hid_h[:, hid, s, :], sq[:, s, :], ACT.Copy).then_inc(sem("ff1_high"), 1)

            for s in range(2):
                ff1_square(0, s, 0, False)
            with act.Fori(0, (CH1 - 2) // 2) as j:
                for e in range(2):
                    for s in range(2):
                        ff1_square(j * 2 + 1 + e, s, 1 - e, True)
            for s in range(2):
                ff1_square(CH1 - 1, s, 1, True)
            for k in range(KT):
                act.wait_ge(dn_evac, 16 * (CH1 - 1) + 2 * k + 4)
                if k >= 3:
                    act.wait_ge(nsem["acc"], 7 * SUMS["final"] + k)
                    act.wait_ge(sem("acc_m"), k - 2)
                act.activation(nsq_fm[:, 2 * (k % 2), :] if k else sq_sum_f[:, :], xt[:, k, :], ACT.Square)
                act.activation(nsq_fm[:, 2 * (k % 2) + 1, :] if k else sq_sum_m[:, :], xt[:, k, :], ACT.Square,
                               scale=vec("final_norm_g", k)).then_inc(nsem["sq"], 1)
            norm_root(act, "final")
            act.wait_ge(sem("ms_m"), 2)
            act.activation(root_m, ms_m, ACT.Sqrt, scale=1.0 / D, bias=eps_rms).then_inc(nsem["root"], 1)
            modulate_scalar(act, "mix2", gs_fm, mod2[:, 0:8])

            def out2(p, m, scale, slot):
                act.wait_ge(up_done, p + (U_WIN2 + 3))
                act.activation(pt2[:, m, :], bank2(2 * slot), ACT.Copy, scale=scale).then_inc(up_evac, 1)

            def partner(r, p, m):
                act.wait_ge(up_evac, p + (U_WIN2 + 3))
                act.wait_ge(sem("qk2_set"), r + 1)
                for h in range(2):
                    for two in range(2):
                        dst, src = h * DH + two * (ROT // 2), h * DH + (1 - two) * (ROT // 2)
                        act.dma_start(rt2[dst:dst + ROT // 2, :], pt2[src:src + ROT // 2, m, :] if isinstance(m, int) else
                                      pt2[src:src + ROT // 2, bass.ds(m, 1), :]).then_inc(sem("rotated"), 16)

            with act.Fori(0, 3) as i:
                for s in range(2):
                    out2(i * 2 + s, i * 2 + (V2 + s), 1.0, s)
            act.wait_ge(sem("angle"), 1)
            act.activation(sin[:, :], ang[:, :], ACT.Sin).then_inc(sem("rot_tab"), 1)
            act.wait_ge(sem("angle"), 2)
            act.activation(cos[:, :], turn[:, :], ACT.Sin).then_inc(sem("rot_tab"), 1)
            with act.Fori(3, 6) as i:
                for s in range(2):
                    out2(i * 2 + s, i * 2 + (K2 - 6 + s), 1.0, s)
                    partner(i * 2 + (s - 6), i * 2 + s, i * 2 + (K2 - 6 + s))
            act.wait_ge(sem("x_moved"), 16)
            for s in range(2):
                out2(12 + s, s, 1.0, s)
            with act.Fori(1, 3) as i:
                for s in range(2):
                    out2(i * 2 + (12 + s), i * 2 + s, SCALE, s)
                    partner(i * 2 + (s + 4), i * 2 + (12 + s), i * 2 + s)
            out2(18, Q2 + 4, SCALE, 0)
            partner(10, 18, Q2 + 4)
            out2(19, Q2 + 5, SCALE, 1)
            for n in range(GROUPS * TT // 4):
                act.wait_ge(sem("v2_turned"), n + 1)
                act.activation(v2[:, 4 * n:4 * n + 4, :], bank2(2 * (n % 2)).rearrange("p (t c) -> p t c", c=256), ACT.Copy
                               ).then_inc(sem("v2_set"), 1)
                if n == 1:
                    partner(11, 19, Q2 + 5)
                if n in POOL_AT:
                    c = POOL_AT.index(n)
                    act.wait_ge(sem("pool_y"), c + 1)
                    act.wait_ge(sem("pool_b"), 1)
                    act.activation(pout[:, c, :], bank2(4 + 2 * c), ACT.Identity, scale=vec("pool_scale_2", c),
                                   bias=pbias[:, c:c + 1]).then_inc(sem("pout"), 1)
            for c in range(2):
                act.wait_ge(sem("pout"), c + 1)
                act.activation(mix2_h[:, c, :], pout[:, c, :], ACT.Copy).then_inc(sem("mix2_high"), 1)
            for n in range(GROUPS * TT + 1):
                if n < GROUPS * TT:
                    w = keys2(n)
                    act.wait_ge(sem("d_max"), n + 1)
                    for h in range(GH):
                        act.activation(pr2[n % 2][:, h, 0:w], s2[n % 2][:, h, 0:w], ACT.Exp, bias=st2_neg[n % 2][:, h:h + 1],
                                       accum_out=st2_den[n % OG][:, h:h + 1]).then_inc(sem("d_exp"), 1)
                if n >= 1:
                    w = keys2(n - 1) // P * GH
                    act.wait_ge(sem("d_turned"), n)
                    act.activation(pt2t[(n - 1) % 2][:, 0:w, :], bank2(4)[:, 0:w * P].rearrange("p (k q) -> p k q", q=P),
                                   ACT.Copy).then_inc(sem("pt2_set"), 1)
            act.wait_ge(sem("c_weight"), 1)
            act.activation(cw[:, :, :, :], cw[:, :, :, :], ACT.Exp).then_inc(sem("c_exp"), 1)
            for c in range(2):
                act.wait_ge(sem("c_turned"), c + 1)
                act.activation(mix2_h[:, 2 + c, :], bank2(4 + 2 * c), ACT.Copy).then_inc(sem("mix2_high"), 1)
            def y_tile(u, s):
                act.wait_ge(up_done, u + (U_WO2 + 3))
                square(act, "post2", u, s, nsq_y, sq_sum_y, bank2(2 * s))
                act.activation(y2[:, u, :], bank2(2 * s), ACT.Copy).then_inc(up_evac, 1)

            for s in range(2):
                y_tile(s, s)
            with act.Fori(1, KT // 2) as i:
                for s in range(2):
                    y_tile(i * 2 + s, s)
            norm_root(act, "post2")
            for i in range(2 * KT):
                act.wait_ge(sem("x_ready"), i + 1)
                half_square(act, "ffn2", i, xt[:, i % KT, :])
                if i == KT + 2:
                    half_root(act, "ffn2", 0)
            n8 = KT * MODULATED["ffn2"]
            for i in range(2 * KT):
                h, k = divmod(i, KT)
                v = by_half(nhn[:, k % 2, :], h)
                act.wait_ge(nsem["hn"], n8 + i + 1)
                act.activation(v, v, ACT.Identity, scale=gsf[:, k:k + 1], bias=mod2[:, 24 + k:25 + k]).then_inc(nsem["mod"], 1)
                act.wait_ge(nsem["mod"], n8 + i + 1)
                act.activation(by_half(hn_h[:, k, :], h), v, ACT.Copy).then_inc(nsem["high"], 1)
                if i == 3:
                    half_root(act, "ffn2", 1)

            def ff2_tile(c, i, hid, wait_free):
                u = c * 4 + U_FF2 + 2 * i
                f = c * 2 + i
                act.wait_ge(up_done, u + 3)
                act.activation(gbuf[:, i, :], bank2(0), ACT.Identity, scale=vec("conv_w_2", f + 44),
                               bias=vec("conv_b_2", f)).then_inc(sem("ff2_gate"), 1)
                act.wait_ge(up_evac, u + 3)
                act.activation(gelu[:, i, :], gbuf[:, i, :], ACT.Gelu_apprx_tanh).then_inc(sem("ff2_gelu"), 1)
                act.wait_ge(up_evac, u + 4)
                if wait_free:
                    act.wait_ge(dn_done, c * 16 - 15 + 16 * C_FF2)
                act.activation(hid_h[:, hid, i, :], gv[:, i, :], ACT.Copy).then_inc(sem("ff2_high"), 1)

            act.wait_ge(sem("x_moved"), 48)
            for i in range(2):
                ff2_tile(0, i, 0, False)
            with act.Fori(0, (CH2 - 1) // 2) as j:
                for e in range(2):
                    for i in range(2):
                        ff2_tile(j * 2 + 1 + e, i, 1 - e, True)
            for i in range(2 * KT):
                act.wait_ge(dn_evac, OUT_UNITS + i + 3)
                half_square(act, "out", i, y2[:, i % KT, :])
                if i == KT + 2:
                    half_root(act, "out", 0)
            half_root(act, "out", 1)
            for t in range(TT):
                act.wait_ge(sem("o_turned"), t + 1)
                if t >= 2:
                    act.wait_ge(sem(f"stored{t % 2}"), 16 * (t // 2))
                act.activation(otok[:, t % 2, :], bank2(4 * (t % 2)), ACT.Copy).then_inc(sem("o_ready"), 1)

        @block.vector
        def _(dve):
            steps = 0

            def link(ins):
                nonlocal steps
                steps += 1
                ins.then_inc(sem("step"), 1)
                dve.wait_ge(sem("step"), steps)

            dve.wait_ge(sem("vec_turned"), 1)
            dve.tensor_copy(vcol[:, :], PS[:, 7, 0:VEC_TILES * P]).then_inc(sem("vec_set"), 1)
            dve.wait_ge(sem("silu"), 1)
            for k in range(KT):
                j = k // 2
                dve.wait_ge(sem(f"ada_in{j % 2}"), 16 * (j // 2 + 1))
                for v in range(2):
                    acc = ada_acc0[:, v, :]
                    c = silu_c[:, v * KT + k:v * KT + k + 1]
                    if k == 0:
                        ins = dve.tensor_scalar(acc, ada_shift[j % 2][:, k % 2, :], c, None, ALU.mult)
                    else:
                        dve.wait_ge(*((sem("ada_acc"), k) if v == 0 else (sem("ada_used"), k + 2)))
                        ins = dve.scalar_tensor_tensor(out=acc, in0=ada_shift[j % 2][:, k % 2, :], scalar=c, in1=acc,
                                                       op0=ALU.mult, op1=ALU.add)
                    ins.then_inc(sem("ada_acc") if v == 0 else sem("ada_used"), 1)
                if k % 2 and j < 3:
                    lo, hi = 4 * j, min(4 * j + 4, TT + CT)
                    dve.wait_ge(sem("root10"), j + 1)
                    link(dve.reciprocal(rstd10[:, lo:hi], root10[:, lo:hi]))
                    for t in range(lo, hi):
                        dve.tensor_scalar(xdiag[:, t, :], ident, rstd10[:, t:t + 1], None, ALU.mult).then_inc(sem("x_diag"), 1)
            dve.wait_ge(sem("ada_sum0"), 2)
            dve.tensor_tensor(mod1[:, 0:16], PS[:, 6, 0:16], vec("ada_b", 0, 16), ALU.add).then_inc(sem("mod1"), 1)
            dve.tensor_tensor(modc, PS[:, 6, 16:32], vec("ada_b", 0, 16), ALU.add).then_inc(sem("mod1"), 1)
            dve.wait_ge(sem("mod1"), 2)
            for g, m in ((gs1, mod1), (gsc, modc)):
                dve.scalar_tensor_tensor(out=g, in0=m[:, 8:16], scalar=1.0, in1=vec("norm1_g", 0, 8), op0=ALU.add,
                                         op1=ALU.mult).then_inc(sem("mod1"), 1)
            dve.wait_ge(sem("mod1"), 4)
            dve.wait_ge(sem("xs_set"), TT + CT)
            for k in range(KT + 1):
                if k < KT:
                    for lo, hi, g, m in ((0, SEQ, gs1, mod1), (SEQ, SEQ + CTX, gsc, modc)):
                        dve.tensor_scalar(xs[:, k, lo:hi], xs[:, k, lo:hi], g[:, k:k + 1], m[:, k:k + 1], ALU.mult,
                                          ALU.add).then_inc(sem("hn1"), 1)
                if k >= 1:
                    dve.wait_ge(sem("hn1_high"), k)
                    dve.tensor_tensor(hn1_l[:, k - 1, :], xs[:, k - 1, :], hn1_h[:, k - 1, :].bitcast(F32),
                                      ALU.subtract).then_inc(sem("hn1_low"), 1)
            with dve.Fori(0, 4) as i:
                for s in range(2):
                    dve.wait_ge(sem(f"ada1_in{s}"), i * 16 + 16)
                    dve.wait_ge(sem("ada1_sum"), i * 2 + (s + 1))
                    for k in range(KT):
                        c = silu_c[:, k:k + 1]
                        if k == 0:
                            ins = dve.tensor_scalar(ada_acc1[:, s, :], ada_in1[s][:, 0, :], c, None, ALU.mult)
                        else:
                            dve.wait_ge(sem("ada1_used"), i * 16 + (s * KT + k + 2))
                            ins = dve.scalar_tensor_tensor(out=ada_acc1[:, s, :], in0=ada_in1[s][:, k, :], scalar=c,
                                                           in1=ada_acc1[:, s, :], op0=ALU.mult, op1=ALU.add)
                        ins.then_inc(sem("ada1_used"), 1)
            dve.memset(vpad_edges(0), 0.0).then_inc(sem("padded"), 1)
            dve.memset(vpad_edges(1), 0.0).then_inc(sem("padded"), 1)
            dve.wait_ge(sem("padded"), 2)
            dve.wait_ge(sem("gate"), 1)
            for c in range(2):
                dve.tensor_tensor(vpad[:, c, PADT:PADT + SEQ], pt1[:, 2 + c, :], pt1[:, 4 + c, :], ALU.mult
                                  ).then_inc(sem("padded"), 1)
            dve.wait_ge(sem("padded"), 4)
            for c in range(2):
                dve.tensor_scalar(conv_acc[:, c, :], vpad[:, c, 0:SEQ], vec("conv_dw_w", c), vec("conv_dw_b", c),
                                  ALU.mult, ALU.add).then_inc(sem("taps"), 1)

            def tap(n):
                for c in range(2):
                    dve.wait_ge(sem("taps"), n * 2 + (c - 1))
                    dve.scalar_tensor_tensor(out=conv_acc[:, c, :], in0=vpad[:, c, bass.ds(n, SEQ)],
                                             scalar=vec("conv_dw_w", n * 2 + c), in1=conv_acc[:, c, :],
                                             op0=ALU.mult, op1=ALU.add).then_inc(sem("taps"), 1)

            with dve.Fori(1, 11) as n:
                tap(n)
            dve.wait_ge(sem("ada1_sum"), 8 + 2)
            dve.tensor_tensor(mod1[:, 16:48], PS[:, 7, 0:32], vec("ada_b", 16, 32), ALU.add).then_inc(sem("ada1_mod"), 1)
            with dve.Fori(11, TAPS) as n:
                tap(n)
            dve.wait_ge(sem("ada1_mod"), 1)
            dve.scalar_tensor_tensor(out=gs2, in0=mod1[:, 32:40], scalar=1.0, in1=vec("norm2_g", 0, 8), op0=ALU.add,
                                     op1=ALU.mult).then_inc(sem("gmix"), 1)
            dve.wait_ge(sem("ln_sums"), 1)
            for c in range(2):
                dve.scalar_tensor_tensor(out=conv_acc[:, c, :], in0=bank2(6), scalar=-1.0 / 256, in1=conv_acc[:, c, :],
                                         op0=ALU.mult, op1=ALU.add).then_inc(sem("ln_d"), 1)
            dve.wait_ge(sem("ln_root"), 1)
            dve.reciprocal(ln_r[:, :], ln_r[:, :]).then_inc(sem("ln_rstd"), 1)
            dve.wait_ge(sem("ln_rstd"), 1)
            for c in range(2):
                dve.tensor_tensor(conv_acc[:, c, :], conv_acc[:, c, :], ln_r[:, :], ALU.mult).then_inc(sem("ln_y"), 1)
            for n in range(2):
                dve.wait_ge(sem("four_e"), 2 * n + 2)
                dve.wait_ge(sem("four_done"), 2 * n + 2)
                odd = PS[:, 7 - 2 * n, :]
                dve.tensor_tensor(four_y[:, n, 0:NYQ], four_e[n][:, :], odd, ALU.subtract).then_inc(sem("four_mir"), 1)
                dve.tensor_tensor(four_y[:, n, SEQ - 1:NYQ:-1], four_e[n][:, 1:NYQ], odd[:, 1:NYQ], ALU.add
                                  ).then_inc(sem("four_mir"), 1)
            with dve.Fori(0, PAIRS // 2) as i:
                def biased(n):
                    s, (h, t) = n // 16, divmod(n % 16, 8)
                    w = WIN_N[t]
                    e = n % 2
                    bias = tbm[s][:, h, :] if w == 640 else \
                        tb[s][:, h, (WIN_U[t] - 2 * t + 6) * GRID_W:(WIN_U[t] - 2 * t + 6) * GRID_W + w]
                    if n % 16 == 0:
                        dve.wait_ge(sem("bias_set"), i * 10 + (5 * s + 5))
                    dve.wait_ge(sem("na_scored"), i * 32 + (n + 1))
                    if n >= 2:
                        dve.wait_ge(sem("na_exp"), i * 64 + (2 * n - 2))
                    carry(dve)
                    scores = bank2(2 * e)
                    dve.tensor_tensor_reduce(sbias[e][:, 0:w], scores[:, 0:w], bias, 1.0, BIG, ALU.add, ALU.max,
                                             st_m[:, e:e + 1]).then_inc(sem("na_biased"), 1)
                    dve.tensor_reduce(st_m2[:, e:e + 1], scores[:, w:w + CTX], AX.X, ALU.max).then_inc(sem("na_max2"), 1)
                    dve.wait_ge(sem("na_biased"), i * 32 + (n + 18))
                    dve.wait_ge(sem("na_max2"), i * 32 + (n + 1))
                    dve.tensor_scalar(st_neg[:, e:e + 1], st_m[:, e:e + 1], st_m2[:, e:e + 1], -1.0, ALU.max,
                                      ALU.mult).then_inc(sem("na_max"), 1)

                def divided(n):
                    e = n % 2
                    dve.wait_ge(sem("na_exp"), i * 64 + (2 * n + 2))
                    dve.tensor_tensor(st_r[:, e:e + 1], st_d[:, e:e + 1], st_d2[:, e:e + 1], ALU.add
                                      ).then_inc(sem("na_den"), 1)
                    dve.wait_ge(sem("na_den"), i * 64 + (2 * n + 1))
                    dve.reciprocal(st_rr[:, e:e + 1], st_r[:, e:e + 1]).then_inc(sem("na_den"), 1)
                    dve.wait_ge(sem("na_den"), i * 64 + (2 * n + 2))
                    dve.tensor_scalar(rdiag[e][:, :], ident, st_rr[:, e:e + 1], None, ALU.mult).then_inc(sem("na_diag"), 1)

                def result(n):
                    s, (h, t) = n // 16, divmod(n % 16, 8)
                    rows = slice(h * DH, (h + 1) * DH)
                    dve.wait_ge(sem("na_pv"), i * 32 + (n + 1))
                    dve.tensor_copy(ao[rows, bass.ds(i * 2 + s, 1), t * P:(t + 1) * P], PS[rows, 6 + n % 2, 0:P].unsqueeze(1)
                                    ).then_inc(sem("na_o"), 1)

                for n in range(34):
                    if n < 32:
                        biased(n)
                        divided(n)
                    if n >= 2:
                        result(n - 2)
            for k in range(KT):
                dve.wait_ge(sem("mix_high"), k + 1)
                src = four_y[:, k, :] if k < 2 else conv_out[:, k - 2, :] if k < 4 else ao[:, k - 4, :]
                dve.tensor_tensor(mix_l[:, k, :], src, mix_h[:, k, :].bitcast(F32), ALU.subtract).then_inc(sem("mix_low"), 1)
            def x_add(u, s):
                dve.wait_ge(up_done, u + (U_WO1 + 3))
                dve.wait_ge(sem("xt_set"), u + 1)
                dve.scalar_tensor_tensor(out=xt[:, u, :], in0=bank2(2 * s), scalar=mod1[:, bass.ds(u + 16, 1)],
                                         in1=xt[:, u, :], op0=ALU.mult, op1=ALU.add).then_inc(up_evac, 1)

            x_add(0, 0)
            x_add(1, 1)
            with dve.Fori(1, KT // 2) as i:
                for s in range(2):
                    x_add(i * 2 + s, s)
                    add_square(dve, "mlp", i * 2 + (s - 1), 1 - s, nsq, sq_sum)
            add_square(dve, "mlp", KT - 1, 1, nsq, sq_sum)
            norm_vector(dve, "mlp")
            modulate_vector(dve, "mlp", xt, 4)

            def ada2_sum(b):
                dve.wait_ge(sem("ada2_in"), b * 16 + 16)
                for k in range(KT):
                    c = silu_c[:, 16 + k:17 + k]
                    if k == 0:
                        ins = dve.tensor_scalar(ada_acc2[:, :], ada_in2[:, 0, :], c, None, ALU.mult)
                    else:
                        dve.wait_ge(sem("ada2_used"), b * KT + (k + 2))
                        ins = dve.scalar_tensor_tensor(out=ada_acc2[:, :], in0=ada_in2[:, k, :], scalar=c,
                                                       in1=ada_acc2[:, :], op0=ALU.mult, op1=ALU.add)
                    ins.then_inc(sem("ada2_used"), 1)

            def ada2_mod(b):
                dve.wait_ge(sem("ada2_sum"), b + 1)
                n = ADA2 // P
                dve.tensor_tensor(mod2[:, bass.ds(b * n, n)], PS[:, 6, 0:n], vec("b_ada_2", b * n, n), ALU.add
                                  ).then_inc(sem("mod2"), 1)

            def ff1_lowhalf(c, s, hid):
                dve.wait_ge(sem("ff1_high"), c * 2 + s + 1)
                dve.tensor_tensor(hid_l[:, hid, s, :], sq[:, s, :], hid_h[:, hid, s, :].bitcast(F32), ALU.subtract
                                  ).then_inc(sem("ff1_low"), 1)

            def ff1_add(c, lo, hi):
                for n in range(lo, hi):
                    m, j = divmod(n, 2)
                    part = xt[:, m, j * HALF:(j + 1) * HALF]
                    dve.wait_ge(dn_done, c * 16 + (16 * C_FF1 + n + 2))
                    dve.scalar_tensor_tensor(out=part, in0=PS[:, 4 + n % 2, :], scalar=mod1[:, 40 + m:41 + m], in1=part,
                                             op0=ALU.mult, op1=ALU.add).then_inc(dn_evac, 1)

            def ff1_step(c, prev, hid):
                ff1_lowhalf(c, 0, hid)
                ff1_add(prev, 0, 4)
                ff1_lowhalf(c, 1, hid)
                ff1_add(prev, 4, 8)
                ada2_mod(prev)
                ff1_add(prev, 8, 16)
                ada2_sum(c)

            ada2_sum(0)
            for s in range(2):
                ff1_lowhalf(0, s, 0)
            with dve.Fori(0, (CH1 - 2) // 2) as j:
                for e in range(2):
                    ff1_step(j * 2 + 1 + e, j * 2 + e, 1 - e)
            ada2_mod(CH1 - 2)
            ada2_sum(CH1 - 1)
            ff1_lowhalf(CH1 - 1, 0, 1)
            ff1_add(CH1 - 2, 0, 4)
            ff1_lowhalf(CH1 - 1, 1, 1)
            ff1_add(CH1 - 2, 4, 16)
            dve.wait_ge(sem("mod2"), CH1)
            def gain(g, w, c, op):
                dve.scalar_tensor_tensor(out=g, in0=mod2[:, c:c + 8], scalar=1.0, in1=vec(w, 0, 8), op0=op, op1=ALU.mult
                                         ).then_inc(sem("gmix"), 1)

            gain(gsm, "g_pre_mix_2", 8, ALU.add)
            gain(ggm, "g_post_mix_2", 16, ALU.mult)
            gain(gsf, "g_pre_ffn_2", 32, ALU.add)
            dve.wait_ge(sem("gmix"), 4)
            dve.tensor_tensor(gs_fm, gsm, vec("final_norm_g", 0, 8), ALU.mult).then_inc(sem("gmix"), 1)
            for m in range(KT):
                ff1_add(CH1 - 1, 2 * m, 2 * m + 2)
                if m >= 2:
                    add_square(dve, "final", m - 1, (m - 1) % 2 * 2, nsq_fm, sq_sum_f)
            add_square(dve, "final", KT - 1, 2, nsq_fm, sq_sum_f)
            norm_rstd(dve, "final", rstd8, root8)
            dve.tensor_tensor(ms_m, PS[:, 7, TT:2 * TT], rstd8, ALU.mult).then_inc(sem("ms_m"), 1)
            dve.wait_ge(sem("ms_m"), 1)
            dve.tensor_tensor(ms_m, ms_m, rstd8, ALU.mult).then_inc(sem("ms_m"), 1)
            norm_rstd(dve, "mix2", rstd_m, root_m)
            dve.tensor_tensor(rstd_fm, rstd_m, rstd8, ALU.mult).then_inc(sem("ms_m"), 1)
            dve.wait_ge(sem("ms_m"), 3)
            norm_diag(dve, ndiag_m, rstd_fm)
            norm_diag(dve, ndiag, rstd8)
            dve.wait_ge(nsem["bc"], SPREADS["mix2"] + 1)
            modulate_vector(dve, "mix2", xt, 6)
            dve.wait_ge(nsem["bc"], SPREADS["final"] + 1)
            for k in range(KT):
                dve.scalar_tensor_tensor(out=xt[:, k, :], in0=xt[:, k, :], scalar=vec("final_norm_g", k), in1=bank2(4),
                                         op0=ALU.mult, op1=ALU.mult).then_inc(sem("x1_ready"), 1)
            ada2_mod(CH1 - 1)
            dve.wait_ge(sem("mod2"), CH1 + 1)
            gain(ggf, "g_post_ffn_2", 40, ALU.mult)
            dve.wait_ge(sem("pos_in"), 16)
            for part, shift in (("sin", 0.0), ("cos", 0.25)):
                out_arg = ang if part == "sin" else turn
                if part == "cos":
                    dve.wait_ge(sem("rot_tab"), 1)
                link(dve.tensor_copy(ang[:, :], pos[:, :]))
                link(dve.tensor_scalar(ang[:, :], ang[:, :], const("inv_signed" if part == "sin" else "inv_freq"), None, ALU.mult))
                link(dve.tensor_scalar(turn[:, :], ang[:, :], 1.0 / (2 * math.pi), shift, ALU.mult, ALU.add))
                link(dve.tensor_copy(turn_i[:, :], turn[:, :]))
                link(dve.tensor_copy(turn[:, :], turn_i[:, :]))
                for step in two_pi_parts():
                    link(dve.scalar_tensor_tensor(out=ang[:, :], in0=turn[:, :], scalar=-step, in1=ang[:, :], op0=ALU.mult,
                                                  op1=ALU.add))
                if part == "cos":
                    link(dve.tensor_scalar(ang[:, :], ang[:, :], math.pi / 2, None, ALU.add))
                lim = float(np.nextafter(np.float32(math.pi), np.float32(0)))
                dve.tensor_scalar(out_arg[:, :], ang[:, :], lim, -lim, ALU.min, ALU.max).then_inc(sem("angle"), 1)

            def rotary(r, p, m):
                dve.wait_ge(up_evac, U_WIN2 + p + 3)
                dve.wait_ge(sem("qk2_set"), r + 1)
                link(dve.tensor_tensor(rt[:, :], pt2[:, m, :], cos[:, :], ALU.mult))
                dve.wait_ge(sem("rotated"), 64 * (r + 1))
                link(dve.tensor_tensor(rt2[:, :], rt2[:, :], sin[:, :], ALU.mult))
                dve.tensor_tensor(pt2[:, m, :], rt[:, :], rt2[:, :], ALU.add).then_inc(sem("qk2_set"), 1)

            dve.wait_ge(sem("angle"), 2)
            dve.memset(rt2[:, :], 0.0).then_inc(sem("qk2_set"), 1)
            dve.wait_ge(sem("rot_tab"), 2)
            for r in range(6):
                rotary(r, 6 + r, K2 + r)
            dve.wait_ge(up_evac, U_WIN2 + 13 + 3)
            dve.tensor_tensor(pbias, vec("b_pool_2", 0, 2), vec("pool_scale_2", 0, 2), ALU.mult).then_inc(sem("pool_b"), 1)
            for c in range(2):
                u = pt2[:, c, :]
                bufs = [ps2, ps4]
                src, lo, lag = u, 0, 1
                for n in range(2 if c == 0 else 4):
                    dst = bufs[n % 2]
                    if c == 0 and n == 1 or c == 1 and n == 3:
                        lo = 64
                        old = bufs[(n - 1) % 2]
                        link(dve.tensor_copy(dst[0:64, :], old[0:64, :]))
                    link(dve.tensor_copy(dst[lo:, 0:lag], src[lo:, 0:lag]))
                    link(dve.tensor_tensor(dst[lo:, lag:], src[lo:, lag:], src[lo:, 0:SEQ - lag], ALU.add))
                    src, lag = dst, 2 * lag
                head = const("pool_head")[:, 16 * c:16 * c + 16]
                link(dve.scalar_tensor_tensor(out=pmix[:, c, :], in0=src[:, :], scalar=const("pool_inv")[:, c:c + 1], in1=u,
                                               op0=ALU.mult, op1=ALU.subtract))
                link(dve.tensor_tensor(pmix[:, c, 0:16], src[:, 0:16], head, ALU.mult))
                dve.tensor_tensor(pmix[:, c, 0:16], pmix[:, c, 0:16], u[:, 0:16], ALU.subtract).then_inc(sem("pmix"), 1)
            for r in range(6, 12):
                rotary(r, 8 + r, Q2 + r - 6)
            for n in range(GROUPS * TT + 3):
                e = n % 2
                if n in (1, 2):
                    dve.wait_ge(sem("mix2_high"), n)
                    dve.tensor_tensor(mix2_l[:, n - 1, :], pout[:, n - 1, :], mix2_h[:, n - 1, :].bitcast(F32), ALU.subtract
                                      ).then_inc(sem("mix2_split"), 1)
                if n < GROUPS * TT:
                    w = keys2(n)
                    mask = const("causal16") if D_ORDER[n][0] == 2 else const("causal")[:, 256 - w:]
                    dve.wait_ge(sem("d_scored"), n + 1)
                    if n >= 2:
                        dve.wait_ge(sem("d_exp"), 4 * n - 4)
                    if n >= OG:
                        dve.wait_ge(sem(f"o2_out{n % OG}"), 16 * (n // OG))
                    sc = bank2(2 * e).rearrange("p (h k) -> p h k", h=GH)[:, :, 0:w]
                    dve.tensor_tensor(s2[e][:, :, 0:w], sc, mask.unsqueeze(1).to_broadcast([P, GH, w]), ALU.add
                                      ).then_inc(sem("d_masked"), 1)
                    dve.wait_ge(sem("d_masked"), n + 1)
                    link(dve.tensor_reduce(og[n % OG][:, GH * DH:GH * DH + GH], s2[e][:, :, 0:w], AX.X, ALU.max))
                    dve.tensor_scalar(st2_neg[e], og[n % OG][:, GH * DH:GH * DH + GH], -1.0, None, ALU.mult).then_inc(sem("d_max"), 1)
                if n >= 3:
                    j = n - 3
                    dve.wait_ge(sem("d_pv"), j + 1)
                    dve.tensor_copy(og[j % OG][:, 0:GH * DH], PS[:, 6 + j % 2, 0:GH * DH]).then_inc(sem("o2_ready"), 1)
            dve.wait_ge(sem("oall_in"), 16 * GROUPS)
            mx = [oall[:, :, g, GH * DH:GH * DH + GH] for g in range(GROUPS)]
            dn = [oall[:, :, g, GH * DH + GH:] for g in range(GROUPS)]
            link(dve.tensor_tensor(cmax[:, :, :], mx[0], mx[1], ALU.max))
            link(dve.tensor_tensor(cmax[:, :, :], cmax[:, :, :], mx[2], ALU.max))
            for g in range(2):
                link(dve.tensor_tensor(cw[:, :, g, :], mx[g], cmax[:, :, :], ALU.subtract))
            dve.tensor_tensor(cw[:, :, 2, :], mx[2], cmax[:, :, :], ALU.subtract).then_inc(sem("c_weight"), 1)
            dve.wait_ge(sem("c_exp"), 1)
            link(dve.tensor_tensor(cden[:, :, :], cw[:, :, 0, :], dn[0], ALU.mult))
            for g in range(1, GROUPS):
                link(dve.tensor_tensor(cmax[:, :, :], cw[:, :, g, :], dn[g], ALU.mult))
                link(dve.tensor_tensor(cden[:, :, :], cden[:, :, :], cmax[:, :, :], ALU.add))
            link(dve.reciprocal(cden[:, :, :], cden[:, :, :]))
            for g in range(GROUPS):
                ins = dve.tensor_tensor(cwn[:, :, g, :].rearrange("p t (a b) -> p t b a", b=2),
                                        cw[:, :, g, :].rearrange("p t (b a) -> p t b a", a=2),
                                        cden[:, :, :].rearrange("p t (b a) -> p t b a", a=2), ALU.mult)
                if g < GROUPS - 1:
                    link(ins)
                else:
                    ins.then_inc(sem("c_weight"), 1)
            dve.wait_ge(sem("c_weight"), 2)
            ts = slice(0, C_SPLIT)
            for g in range(GROUPS):
                src, wt = c_group(g, ts)
                link(dve.tensor_tensor(cterm[:, ts, :, :] if g else csum[:, ts, :, :], src, wt, ALU.mult))
                if g:
                    ins = dve.tensor_tensor(csum[:, ts, :, :], csum[:, ts, :, :], cterm[:, ts, :, :], ALU.add)
                    if g < GROUPS - 1:
                        link(ins)
                    else:
                        ins.then_inc(sem("c_weight"), 1)
            for c in range(2):
                dve.wait_ge(sem("mix2_high"), 3 + c)
                dve.tensor_tensor(mix2_l[:, 2 + c, :], bank2(4 + 2 * c), mix2_h[:, 2 + c, :].bitcast(F32), ALU.subtract
                                  ).then_inc(sem("mix2_split"), 1)
            for k in range(1, KT):
                add_square(dve, "post2", k, k % 2, nsq_y, sq_sum_y)
            norm_rstd(dve, "post2", rstd8, root8)
            for h in range(2):
                diag_half(dve, h)
            dve.wait_ge(sem("x_moved"), 32)
            for i in range(2 * KT):
                h, k = divmod(i, KT)
                x, y = by_half(xt[:, k, :], h), by_half(y2[:, k, :], h)
                if k == 0:
                    dve.wait_ge(nsem["bc"], HALF_SPREAD["post2"] + h + 1)
                dve.scalar_tensor_tensor(out=y, in0=y, scalar=ggm[:, k:k + 1], in1=PS[:, 2 + h, :], op0=ALU.mult,
                                         op1=ALU.mult).then_inc(sem("y_gated"), 1)
                dve.wait_ge(sem("y_gated"), i + 1)
                dve.tensor_tensor(x, x, y, ALU.add).then_inc(sem("x_ready"), 1)
                if i == KT + 4:
                    half_diag(dve, "ffn2", 0)
            n8 = KT * MODULATED["ffn2"]
            for i in range(2 * KT + 1):
                if i < 2 * KT:
                    h, k = divmod(i, KT)
                    if k == 0:
                        dve.wait_ge(nsem["bc"], HALF_SPREAD["ffn2"] + h + 1)
                    if i >= 2:
                        dve.wait_ge(nsem["low"], n8 + i - 1)
                    dve.tensor_tensor(by_half(nhn[:, k % 2, :], h), by_half(xt[:, k, :], h), PS[:, 4 + h, :], ALU.mult
                                      ).then_inc(nsem["hn"], 1)
                if i >= 1:
                    h, k = divmod(i - 1, KT)
                    dve.wait_ge(nsem["high"], n8 + i)
                    dve.tensor_tensor(by_half(hn_l[:, k, :], h), by_half(nhn[:, k % 2, :], h),
                                      by_half(hn_h[:, k, :], h).bitcast(F32), ALU.subtract).then_inc(nsem["low"], 1)
                if i == 5:
                    half_diag(dve, "ffn2", 1)

            def ff2_gate(c, i):
                u = c * 4 + U_FF2 + 2 * i
                f = c * 2 + i
                dve.wait_ge(sem("ff2_gate"), f + 1)
                dve.scalar_tensor_tensor(out=gbuf[:, i, 1:], in0=bank2(0)[:, 0:SEQ - 1], scalar=vec("conv_w_2", f + 22),
                                         in1=gbuf[:, i, 1:], op0=ALU.mult, op1=ALU.add).then_inc(sem("ff2_tap"), 1)
                dve.wait_ge(sem("ff2_tap"), f + 1)
                dve.scalar_tensor_tensor(out=gbuf[:, i, 2:], in0=bank2(0)[:, 0:SEQ - 2], scalar=vec("conv_w_2", f),
                                         in1=gbuf[:, i, 2:], op0=ALU.mult, op1=ALU.add).then_inc(up_evac, 1)

            def ff2_value(c, i):
                u = c * 4 + U_FF2 + 2 * i + 1
                dve.wait_ge(sem("ff2_gelu"), c * 2 + i + 1)
                dve.wait_ge(up_done, u + 3)
                dve.tensor_tensor(gv[:, i, :], gelu[:, i, :], bank2(2), ALU.mult).then_inc(up_evac, 1)

            def ff2_lowhalf(c, i, hid):
                dve.wait_ge(sem("ff2_high"), c * 2 + i + 1)
                dve.tensor_tensor(hid_l[:, hid, i, :], gv[:, i, :], hid_h[:, hid, i, :].bitcast(F32), ALU.subtract
                                  ).then_inc(sem("ff2_low"), 1)

            def ff2_add(c, lo, hi):
                for n in range(lo, hi):
                    m, j = divmod(n, 2)
                    part = y2[:, m, j * HALF:(j + 1) * HALF]
                    dve.wait_ge(dn_done, c * 16 + (16 * C_FF2 + n + 2))
                    dve.tensor_tensor(part, part, PS[:, 4 + n % 2, :], ALU.add).then_inc(dn_evac, 1)

            for i in range(2):
                ff2_gate(0, i)
                ff2_value(0, i)
                ff2_lowhalf(0, i, 0)
            dve.wait_ge(sem("y2_zero"), 1)
            with dve.Fori(0, (CH2 - 1) // 2) as j:
                for e in range(2):
                    c = j * 2 + 1 + e
                    ff2_gate(c, 0)
                    ff2_value(c, 0)
                    ff2_lowhalf(c, 0, 1 - e)
                    ff2_gate(c, 1)
                    ff2_value(c, 1)
                    ff2_add(j * 2 + e, 0, 4)
                    ff2_lowhalf(c, 1, 1 - e)
                    ff2_add(j * 2 + e, 4, 16)
            def out_gated(h, k):
                if k == 0:
                    dve.wait_ge(nsem["bc"], HALF_SPREAD["out"] + h + 1)
                y = by_half(y2[:, k, :], h)
                dve.scalar_tensor_tensor(out=y, in0=y, scalar=ggf[:, k:k + 1], in1=PS[:, 2 + h, :], op0=ALU.mult,
                                         op1=ALU.mult).then_inc(sem("y_gated"), 1)

            for i in range(2 * KT):
                h, k = divmod(i, KT)
                part = by_half(y2[:, k, :], h)
                dve.wait_ge(dn_done, OUT_UNITS + i + 2)
                dve.tensor_tensor(part, part, PS[:, 4 + i % 2, :], ALU.add).then_inc(dn_evac, 1)
                if i:
                    add_half_square(dve, "out", i - 1)
                if i == KT + 4:
                    half_diag(dve, "out", 0)
            add_half_square(dve, "out", 2 * KT - 1)
            for k in range(4):
                out_gated(0, k)
            half_diag(dve, "out", 1)
            for k in range(4, KT):
                out_gated(0, k)
            dve.wait_ge(sem("x_moved"), 64)
            for k in range(KT):
                out_gated(1, k)
                dve.wait_ge(sem("y_gated"), 3 * KT + k + 1)
                x = by_half(xt[:, k, :], 1)
                dve.tensor_tensor(x, x, by_half(y2[:, k, :], 1), ALU.add).then_inc(sem("x_ready1"), 1)

        @block.tensor
        def _(pe):
            pe.wait_ge(sem("tables_in"), 32)
            for t in range(VEC_TILES):
                mm = pe.transpose(PS[:, 7, t * P:(t + 1) * P], vrow[:, t, :], ident)
            mm.then_inc(sem("vec_turned"), 1)
            def x_turn(lo, hi):
                for t in range(lo, hi):
                    pe.wait_ge(sem("x_diag"), t + 1)
                    if t >= 2:
                        pe.wait_ge(sem("xs_set"), t - 1)
                    for k in range(KT):
                        mm = pe.matmul(bank2(2 * (t % 2))[:, k * P:(k + 1) * P], xtok[:, t, k * P:(k + 1) * P], xdiag[:, t, :],
                                       start=True, stop=True)
                    mm.then_inc(sem("x_turned"), 1)

            def scale_rows(j):
                pe.wait_ge(sem(f"ada_sc{j}"), 16)
                for k in range(4 * j, 4 * j + 4):
                    for f in range(2):
                        mm = pe.matmul(PS[0:2, 4 + f, :], silu_c[:, k:k + KT + 1:KT], ada_scale[:, k, f * HALF:(f + 1) * HALF],
                                       start=(k == 0), stop=(k == KT - 1))
                if j == 1:
                    mm.then_inc(sem("ada_row"), 1)

            pe.wait_ge(sem("silu"), 1)
            x_turn(0, 6)
            scale_rows(0)
            x_turn(6, 10)
            scale_rows(1)
            pe.wait_ge(sem("ones_set"), 3)
            pe.wait_ge(sem("ada_acc"), KT)
            pe.wait_ge(sem("ada_used"), 2 + KT)
            for v in range(2):
                for f in range(KT):
                    mm = pe.matmul(PS[:, 6, v * 16 + f:v * 16 + f + 1], ada_acc0[:, v, f * P:(f + 1) * P], ones[:, 0:1],
                                   start=True, stop=True)
            mm.then_inc(sem("ada_sum0"), 1)
            pe.wait_ge(sem("ada_row"), 2)
            for f in range(KT):
                mm = pe.matmul(PS[:, 6, KT + f:KT + f + 17:16], ada_rows[0:2, f * P:(f + 1) * P], ident[0:2, 0:2],
                               start=True, stop=True)
            mm.then_inc(sem("ada_sum0"), 1)
            mul_first(pe, U_G2, hn1_h, hn1_l, lambda k: (sem("hn1_low"), k + 1))
            with pe.Fori(1, K0 // 2) as i:
                for s in range(2):
                    mul_up(pe, i * 2 + s, s, hn1_h, hn1_l)
                    pe.wait_ge(sem("ada1_used"), i * 16 + (s * KT - 6))
                    for f in range(ADA1 // P):
                        mm = pe.matmul(PS[:, 7, bass.ds(i * 8 + (4 * s + f - 8), 1)], ada_acc1[:, s, f * P:(f + 1) * P],
                                       ones[:, 0:1], start=True, stop=True)
                    mm.then_inc(sem("ada1_sum"), 1)
            for s in range(2):
                mul_up(pe, K0 + s, s, hn1_h, hn1_l, extra=CTX)
            pe.wait_ge(sem("four_in"), 16)
            pe.wait_ge(sem("ada1_mod"), 1)
            for c in range(2):
                pe.matmul(PS[:, 6 + c, 0:256], const("dft_c"), wf[:, c, :], start=True, stop=True)
                pe.matmul(PS[:, 6 + c, 256:512], const("dft_s"), wf[:, c, :], start=True, stop=True
                          ).then_inc(sem("four_w"), 1)
            with pe.Fori(1, 3) as i:
                for s in range(2):
                    mul_up(pe, i * 2 + (K0 + s), s, hn1_h, hn1_l, extra=CTX)
            pe.wait_ge(sem("taps"), 2 * TAPS)
            pe.wait_ge(sem("four_ab"), 2)
            for j in range(2):
                for c in range(2):
                    mm = pe.matmul(PS[:, 6 + j, :], ones[:, :], conv_acc[:, c, j * HALF:(j + 1) * HALF],
                                   start=(c == 0), stop=(c == 1))
            mm.then_inc(sem("ln_sums"), 1)
            mul_up(pe, K0 + 6, 0, hn1_h, hn1_l, extra=CTX)
            pe.wait_ge(sem("ln_sq"), 2)
            for j in range(2):
                for c in range(2):
                    mm = pe.matmul(PS[:, 6 + j, :], ones[:, :], conv_sq[:, c, j * HALF:(j + 1) * HALF],
                                   start=(c == 0), stop=(c == 1))
            mm.then_inc(sem("ln_sums"), 1)
            mul_up(pe, K0 + 7, 1, hn1_h, hn1_l, extra=CTX)
            pe.wait_ge(up_evac, W_IN_TILES + 2)
            for t in range(TT):
                if t >= 2:
                    pe.wait_ge(sem("zf_set"), t - 1)
                for c in range(2):
                    mm = pe.matmul(PS[:, 4 + t % 2, :], pt1[:, c, t * P:(t + 1) * P], four_ab[:, c, :],
                                   start=(c == 0), stop=(c == 1))
                mm.then_inc(sem("four_z"), 1)
            pe.wait_ge(sem("four_in"), 32)
            pe.wait_ge(sem("zf_set"), TT)
            pe.wait_ge(sem("ln_root"), 1)
            for nt in range(2):
                even, odd = PS[:, 6 - 2 * nt, :], PS[:, 7 - 2 * nt, :]
                for tt in range(TT):
                    pe.matmul(even, zf[:, tt, nt * P:(nt + 1) * P], dseq[:, tt, 0:NYQ], start=(tt == 0), stop=(tt == TT - 1))
                for tt in range(TT):
                    mm = pe.matmul(PS[:, nt, 0:1], zf[:, tt, nt * P:(nt + 1) * P], dseq[:, tt, NYQ:NYQ + 1],
                                   start=(tt == 0), stop=(tt == TT - 1))
                mm.then_inc(sem("four_done"), 1)
                for tt in range(TT):
                    mm = pe.matmul(odd, zf[:, tt, 256 + nt * P:256 + (nt + 1) * P], dseq[:, tt, NYQ + 1:],
                                   start=(tt == 0), stop=(tt == TT - 1))
                mm.then_inc(sem("four_done"), 1)
            pe.wait_ge(sem("point_in"), 16)
            pe.wait_ge(sem("conv_s"), 2)
            pe.wait_ge(sem("four_e"), 4)
            for m in range(2):
                for j in range(2):
                    for c in range(2):
                        mm = pe.matmul(PS[:, 2 * m + j, :], pw[:, c, m * P:(m + 1) * P], conv_acc[:, c, j * HALF:(j + 1) * HALF],
                                       start=(c == 0), stop=(c == 1))
                mm.then_inc(sem("conv_pw"), 1)

            pe.wait_ge(sem("conv_done"), 2)
            pe.wait_ge(sem("four_mir"), 4)
            with pe.Fori(0, PAIRS // 2) as i:
                def scores(n):
                    s, (h, t) = n // 16, divmod(n % 16, 8)
                    w, k0 = WIN_N[t], WIN_U[t] * GRID_W
                    rows = slice(h * DH, (h + 1) * DH)
                    dst = bank2(2 * (n % 2))
                    q = qs[s][rows, t * P:(t + 1) * P]
                    if n in (V_STEP + 2, V_STEP + 3):
                        pe.wait_ge(sem("vt_set"), i * 4 + (n - V_STEP + 1))
                    elif n >= 2:
                        pe.wait_ge(sem("na_exp"), i * 64 + (2 * n - 2))
                    spans = [(0, min(w, HALF), k0), (HALF, w, k0 + HALF), (w, w + CTX, SEQ)]
                    for lo, hi, k in spans:
                        if hi > lo:
                            mm = pe.matmul(dst[:, lo:hi], q, ks[s][rows, k:k + hi - lo], start=True, stop=True)
                    mm.then_inc(sem("na_scored"), 1)

                def turned(n):
                    pe.wait_ge(sem("na_diag"), i * 32 + (n + 1))
                    if n:
                        pe.wait_ge(sem("probt_set"), i * 32 + (n + 1))
                    else:
                        pe.wait_ge(sem("vt_set"), i * 4 + 1)
                    for c in range((WIN_N[n % 8] + CTX) // P):
                        mm = pe.matmul(bank2(4)[:, c * P:(c + 1) * P], prob[n % 2][:, c * P:(c + 1) * P], rdiag[n % 2][:, :],
                                       start=True, stop=True)
                    mm.then_inc(sem("na_turned"), 1)

                def values(n):
                    s, (h, t) = n // 16, divmod(n % 16, 8)
                    if n % 16 == 0:
                        pe.wait_ge(sem("vt_set"), i * 4 + (2 * s + 2))
                    pe.wait_ge(sem("probt_set"), i * 32 + (n + 2))
                    if n >= 2:
                        pe.wait_ge(sem("na_o"), i * 32 + n)
                    tiles = [WIN_U[t] // 2 + c for c in range(WIN_N[t] // P)] + [TT, TT + 1]
                    for c, kt in enumerate(tiles):
                        mm = pe.matmul(PS[h * DH:(h + 1) * DH, 6 + n % 2, 0:P], vt[s][:, kt, h * DH:(h + 1) * DH],
                                       probt[n % 2][:, c * P:(c + 1) * P], start=(c == 0), stop=(c == len(tiles) - 1))
                    mm.then_inc(sem("na_pv"), 1)

                def v_turn(s, r):
                    lo, cnt = 8 * r, 8 if r == 0 else 2
                    dst = bank2(2 * ((V_STEP + r) % 2)) if s else bank2(4 + 2 * r)
                    for t in range(cnt):
                        mm = pe.transpose(dst[:, t * P:(t + 1) * P], vs[:, (lo + t) * P:(lo + t + 1) * P], ident)
                    mm.then_inc(sem("v_turned"), 1)

                pe.wait_ge(sem("na_o"), i * 32 + 1)
                pe.wait_ge(sem("probt_set"), i * 32 + 1)
                pe.wait_ge(sem("staged"), i * 10 + 3)
                scores(0)
                scores(1)
                pe.wait_ge(sem("staged"), i * 10 + 5)
                for r in range(2):
                    v_turn(0, r)
                for n in range(32):
                    turned(n)
                    if n in (V_STEP, V_STEP + 1):
                        pe.wait_ge(sem("staged"), i * 10 + 10)
                        v_turn(1, n - V_STEP)
                    if n == V_STEP + 1:
                        scores(n + 1)
                        values(n - 1)
                        scores(n + 2)
                    else:
                        if n < 30 and n != V_STEP:
                            scores(n + 2)
                        if n:
                            values(n - 1)
                values(31)
            def wo1(u, s, slab, ready=None):
                mul_up(pe, u + U_WO1, s, mix_h, mix_l, ready=ready)
                pe.wait_ge(sem(f"slab_in{s}"), slab)
                if not isinstance(u, int) or u:
                    pe.wait_ge(sem("xt_set"), u)
                for t in range(TT):
                    mm = pe.transpose(bank2(4)[:, t * P:(t + 1) * P], xslab[:, s, t, :], ident)
                mm.then_inc(sem("slab_used"), 1)

            wo1(0, 0, 16, lambda k: (sem("mix_low"), k + 1))
            wo1(1, 1, 16)
            with pe.Fori(1, KT // 2) as i:
                for s in range(2):
                    wo1(i * 2 + s, s, i * 16 + 16)
            add_sums(pe, "mlp", sq_sum)
            norm_spread(pe, "mlp", ndiag, 4)

            def split_tile(n):
                return lambda k: (nsem["low"], KT * MODULATED[n] + k + 1)

            def ff1_up(c):
                for s in range(2):
                    mul_up(pe, c * 2 + (U_FF1 + s), s, hn_h, hn_l)

            def ff1_dn(c, hid, **place):
                pe.wait_ge(sem("ff1_low"), c * 2 + 2)
                mul_dn(pe, c * 2 + 2 * C_FF1, hid, c * 16 + 16 * C_FF1, **place)

            def ada2_reduce(b):
                pe.wait_ge(sem("ada2_used"), b * KT + (2 + KT))
                pe.wait_ge(sem("mod2"), b + 1)
                for f in range(ADA2 // P):
                    mm = pe.matmul(PS[:, 6, f:f + 1], ada_acc2[:, f * P:(f + 1) * P], ones[:, 0:1], start=True, stop=True)
                mm.then_inc(sem("ada2_sum"), 1)

            mul_first(pe, U_FF1, hn_h, hn_l, split_tile("mlp"))
            with pe.Fori(0, (CH1 - 2) // 2) as j:
                for e in range(2):
                    ff1_up(j * 2 + 1 + e)
                    ada2_reduce(j * 2 + e)
                    ff1_dn(j * 2 + e, e)
            for s in range(2):
                mul_up(pe, U_FF1 + 2 * (CH1 - 1) + s, s, hn_h, hn_l)
                if s == 0:
                    ada2_reduce(CH1 - 2)
            ff1_dn(CH1 - 2, 0)
            ff1_dn(CH1 - 1, 1, wh=up_h, wl=up_l)
            for j, acc in enumerate((sq_sum_f, sq_sum_m)):
                if j == 0:
                    pe.wait_ge(nsem["acc"], 7 * SUMS["final"] + 9)
                else:
                    pe.wait_ge(sem("acc_m"), KT - 1)
                for t in range(TT):
                    mm = pe.matmul(PS[:, 7, j * TT + t:j * TT + t + 1], acc[:, t * P:(t + 1) * P], ones[:, 0:1],
                                   start=True, stop=True)
            mm.then_inc(nsem["sums"], 1)
            norm_spread(pe, "mix2", ndiag_m, 6)
            norm_spread(pe, "final", ndiag, 4)
            def win2(p, s):
                mul_up(pe, p + U_WIN2, s, hn_h, hn_l)

            mul_first(pe, U_WIN2, hn_h, hn_l, split_tile("mix2"))
            ada2_reduce(CH1 - 1)
            with pe.Fori(1, W_IN2_TILES // 2) as i:
                for s in range(2):
                    win2(i * 2 + s, s)
            pe.wait_ge(up_evac, U_WIN2 + W_IN2_TILES + 1)
            for n in range(GROUPS * TT // 4):
                if n == 1:
                    pe.wait_ge(up_evac, U_WIN2 + W_IN2_TILES + 2)
                if n >= 2:
                    pe.wait_ge(sem("v2_set"), n - 1)
                for gb in range(4 * n, 4 * n + 4):
                    g, b = divmod(gb, TT)
                    for hp in range(2):
                        lo = gb % 4 * 256 + hp * P
                        mm = pe.transpose(bank2(2 * (n % 2))[:, lo:lo + P], perm(pt2[:, V2 + 2 * g + hp, :], g, b), ident)
                mm.then_inc(sem("v2_turned"), 1)
                if n in POOL_AT:
                    c = POOL_AT.index(n)
                    pe.wait_ge(sem("point_in"), 32)
                    pe.wait_ge(sem("x1_ready"), KT)
                    pe.wait_ge(sem("mod2"), CH1 + 1)
                    pe.wait_ge(sem("pmix"), c + 1)
                    for j in range(2):
                        mm = pe.matmul(PS[:, 4 + 2 * c + j, :], wp[:, c, :], pmix[:, c, j * HALF:(j + 1) * HALF], start=True, stop=True)
                    mm.then_inc(sem("pool_y"), 1)

            pe.wait_ge(sem("v2_set"), GROUPS * TT // 4)

            def d_blocks(n):
                g, b = D_ORDER[n]
                return [b - (1 if g == 0 else 4), b] if keys2(n) == 256 else [b]

            def d_scores(n):
                g, b = D_ORDER[n]
                if n == D_FIRST[g]:
                    pe.wait_ge(sem("qk2_set"), 9 + 2 * g)
                if n >= 2:
                    pe.wait_ge(sem("d_masked"), n - 1)
                for j, h in enumerate(HEAD_AT):
                    rows = slice(DH * (h % 2), DH * (h % 2) + DH)
                    q = perm(pt2[rows, Q2 + 2 * g + h // 2, :], g, b)
                    k = pt2[rows, K2 + 2 * g + h // 2, :]
                    for c, kb in enumerate(d_blocks(n)):
                        lo = j * 256 + c * P
                        mm = pe.matmul(bank2(2 * (n % 2))[:, lo:lo + P], q, perm(k, g, kb),
                                       start=True, stop=True)
                mm.then_inc(sem("d_scored"), 1)

            def d_turned(n):
                nk = keys2(n) // P
                pe.wait_ge(sem("d_exp"), GH * (n + 1))
                if n:
                    pe.wait_ge(sem("pt2_set"), n)
                else:
                    pe.wait_ge(sem("pout"), 2)
                for j in range(GH):
                    for c in range(nk):
                        lo = (j * nk + c) * P
                        mm = pe.matmul(bank2(4)[:, lo:lo + P], pr2[n % 2][:, j, c * P:(c + 1) * P], ident, start=True, stop=True)
                mm.then_inc(sem("d_turned"), 1)

            def d_values(n):
                g, b = D_ORDER[n]
                blocks = d_blocks(n)
                pe.wait_ge(sem("pt2_set"), n + 1)
                if n >= 2:
                    pe.wait_ge(sem("o2_ready"), n - 1)
                for j, h in enumerate(HEAD_AT):
                    for c, kb in enumerate(blocks):
                        mm = pe.matmul(PS[:, 6 + n % 2, h * DH:(h + 1) * DH], pt2t[n % 2][:, j * len(blocks) + c, :],
                                       v2[:, g * TT + kb, h * DH:(h + 1) * DH], start=(c == 0), stop=(c == len(blocks) - 1))
                mm.then_inc(sem("d_pv"), 1)

            d_scores(0)
            d_scores(1)
            for n in range(GROUPS * TT):
                if n + 2 < GROUPS * TT:
                    d_scores(n + 2)
                d_turned(n)
                if n:
                    d_values(n - 1)
            d_values(GROUPS * TT - 1)
            pe.wait_ge(sem("mix2_split"), 2)
            for s in range(2):
                mul_up(pe, U_WO2 + s, s, mix2_h, mix2_l, kt=4, ks=range(0, 2))
            pe.wait_ge(sem("o2_ready"), GROUPS * TT)
            pe.wait_ge(sem("c_weight"), 3)
            pe.wait_ge(sem("c_sum"), 5)
            for c in range(2):
                for t in range(TT):
                    mm = pe.transpose(bank2(4 + 2 * c)[:, t * P:(t + 1) * P], csum[:, t, 2 * c:2 * c + 2, :].rearrange("p h d -> p (h d)"), ident)
                mm.then_inc(sem("c_turned"), 1)
            for k in range(2, 4):
                pe.wait_ge(sem("mix2_split"), k + 1)
                for s in range(2):
                    mul_up(pe, U_WO2 + s, s, mix2_h, mix2_l, kt=4, ks=range(k, k + 1))
            with pe.Fori(1, KT // 2) as i:
                for s in range(2):
                    mul_up(pe, i * 2 + (U_WO2 + s), s, mix2_h, mix2_l, kt=4)
            add_sums(pe, "post2", sq_sum_y)
            for h in range(2):
                half_spread(pe, "post2", h, 2)
            half_sums(pe, "ffn2", 0)
            half_spread(pe, "ffn2", 0, 4)
            half_sums(pe, "ffn2", 1)

            def ff2_up(c, pieces=range(4)):
                for i in pieces:
                    mul_up(pe, c * 4 + (U_FF2 + i), i % 2, hn_h, hn_l)

            def ff2_dn(c, hid, **place):
                pe.wait_ge(sem("ff2_low"), c * 2 + 2)
                mul_dn(pe, c * 2 + 2 * C_FF2, hid, c * 16 + 16 * C_FF2, **place)

            n8 = KT * MODULATED["ffn2"]
            pe.wait_ge(up_full, U_FF2 + 4)
            pe.wait_ge(up_evac, U_FF2 + 2)
            for k in range(KT):
                pe.wait_ge(nsem["low"], n8 + k + 1)
                for s in range(2):
                    first_half(pe, U_FF2, hn_h, hn_l, 0, k, s)
                if k == 3:
                    half_spread(pe, "ffn2", 1, 4)
            for k in range(KT):
                pe.wait_ge(nsem["low"], n8 + KT + k + 1)
                first_half(pe, U_FF2, hn_h, hn_l, 1, k, 0)
            for k in range(KT):
                first_half(pe, U_FF2, hn_h, hn_l, 1, k, 1)
            ff2_up(0, range(2, 4))
            with pe.Fori(0, (CH2 - 1) // 2) as j:
                ff2_up(j * 2 + 1)
                ff2_dn(j * 2, 0)
                ff2_up(j * 2 + 2)
                ff2_dn(j * 2 + 1, 1)
            c = CH2 - 1
            pe.wait_ge(sem("ff2_low"), c * 2 + 2)
            pe.wait_ge(dn_full, c * 2 + 2 * C_FF2 + 4)
            for i in range(2 * KT):
                dn_unit(pe, i, i % KT, i // KT, 0, OUT_UNITS, up_h, up_l)
                if i == KT + 2:
                    half_sums(pe, "out", 0)
                if i == KT + 6:
                    half_spread(pe, "out", 0, 2)
            half_sums(pe, "out", 1)
            half_spread(pe, "out", 1, 2)
            for t in range(TT):
                if t == 0:
                    pe.wait_ge(sem("x_ready"), 3 * KT)
                if t == TT // 2:
                    pe.wait_ge(sem("x_ready1"), KT)
                if t >= 2:
                    pe.wait_ge(sem("o_ready"), t - 1)
                for k in range(KT):
                    mm = pe.transpose(bank2(4 * (t % 2))[:, k * P:(k + 1) * P], xt[:, k, t * P:(t + 1) * P], ident)
                mm.then_inc(sem("o_turned"), 1)


_INS = ["x", "ctx", "ada_w", "w_in", "w_fourier", "conv_pw_w", "w_out", "mlp_w1", "mlp_w2", "w_ada_2", "w_in_2",
        "w_out_2", "w_up_2", "w_down_2"]


def kernel(**inputs):
    import concourse.bacc as bacc
    from concourse.bass_utils import run_bass_kernel_spmd

    arr = {n: np.asarray(v) for n, v in inputs.items()}
    data = {n: np.ascontiguousarray(arr[n].reshape(arr[n].shape[-2:])) for n in _INS}
    data["positions_2"] = np.ascontiguousarray(arr["positions_2"].reshape(1, SEQ))
    vecs = np.zeros((VEC_TILES * P, P), np.float32)
    for name, rows in VECS:
        vecs[VROW[name]:VROW[name] + rows] = arr[name].reshape(rows, P)
    data["vecs"] = vecs
    rpb = np.zeros(2 * RPB_PAD + arr["na_rpb"].size, np.float32)
    rpb[RPB_PAD:-RPB_PAD] = arr["na_rpb"].ravel()
    data["rpb"] = rpb
    wp = np.zeros((2, P, P), np.float32)
    for g in range(4):
        lo = g % 2 * DH
        wp[g // 2, lo:lo + DH, lo:lo + DH] = arr["w_pool_2"].reshape(4, DH, DH)[g]
    data["w_pool"] = wp
    data["consts"] = constants()
    data["dft_seq"] = dft_seq()

    nc = bacc.Bacc("TRN2", target_bir_lowering=False, num_devices=1)
    aps = {n: nc.dram_tensor(n, v.shape, mybir.dt.from_np(v.dtype), kind="ExternalInput").ap() for n, v in data.items()}
    out = nc.dram_tensor("out", [SEQ, D], F32, kind="ExternalOutput").ap()
    bass_two_blocks(nc, aps, out)
    r = run_bass_kernel_spmd(nc, [data], core_ids=[0])
    return r.results[0]["out"].reshape(1, SEQ, D)
```
